# Optimizing a Trainium2 kernel written in Bass

```python
import jax, jax.numpy as jnp
from jax import lax
import numpy as np

D_MODEL = 1024
BATCH = 1
SEQ = 2048
DEPTH = 1

CHUNK = 64
D_MIX = 2 * D_MODEL
HEAD_DIM = 64
ATT_HEADS = D_MIX // 4 // HEAD_DIM
D_ATT = ATT_HEADS * HEAD_DIM
D_SSD = D_MIX - D_ATT
SSD_HEADS = D_SSD // HEAD_DIM
SSD_GROUPS = 4
SSD_STATE = 128
CONV_WIDTH = 4
CONV_DIM = D_SSD + 2 * SSD_GROUPS * SSD_STATE
IN_PROJ_DIM = D_SSD + CONV_DIM + SSD_HEADS + 3 * D_ATT
N_PREV_CHUNKS = 8
BAND = (N_PREV_CHUNKS + 1) * CHUNK
REL_CLIP = 256
MOE_GROUPS = 4
EXPERTS_PER_GROUP = 8
N_EXPERTS = MOE_GROUPS * EXPERTS_PER_GROUP
TOP_K = 2
D_EXPERT = 512
MOE_BLOCK = 128
EPS = 1e-6

kernel_name = "hymba_ssd_chunkattn_hmoe_adaln"

def rmsnorm(x, g):
    xf = x.astype(jnp.float32)
    xf = xf * lax.rsqrt(jnp.mean(xf * xf, axis=-1, keepdims=True) + EPS)
    return xf.astype(x.dtype) * g

def causal_depthwise_conv(u, w, b):
    out = lax.conv_general_dilated(u, w[:, None, :].astype(u.dtype), window_strides=(1,),
                                   padding=[(CONV_WIDTH - 1, 0)],
                                   dimension_numbers=("NWC", "WIO", "NWC"),
                                   feature_group_count=u.shape[-1])
    return out + b

def ssd_scan(X, A, Bm, Cm):
    b, s, h, p = X.shape
    g, n = Bm.shape[2], Bm.shape[3]
    e = h // g
    nc = s // CHUNK
    X = X.reshape(b, nc, CHUNK, g, e, p)
    A = A.reshape(b, nc, CHUNK, g, e).transpose(0, 1, 3, 4, 2)
    Bm = Bm.reshape(b, nc, CHUNK, g, n)
    Cm = Cm.reshape(b, nc, CHUNK, g, n)
    A_cum = jnp.cumsum(A, axis=-1)
    causal = jnp.tril(jnp.ones((CHUNK, CHUNK), dtype=bool))
    seg = A_cum[..., :, None] - A_cum[..., None, :]
    Lmat = jnp.exp(jnp.where(causal, seg, -jnp.inf))
    CB = jnp.einsum("bclgn,bcsgn->bcgls", Cm, Bm)
    y_diag = jnp.einsum("bcgels,bcsgep->bclgep", CB[:, :, :, None] * Lmat, X)
    decay_states = jnp.exp(A_cum[..., -1:] - A_cum)
    states = jnp.einsum("bclgn,bcgel,bclgep->bcgepn", Bm, decay_states, X)
    chunk_decay = jnp.exp(A_cum[..., -1])

    def step(carry, inp):
        st, dec = inp
        return carry * dec[..., None, None] + st, carry

    init = jnp.zeros((b, g, e, p, n), states.dtype)
    _, prev = lax.scan(step, init, (states.transpose(1, 0, 2, 3, 4, 5),
                                    chunk_decay.transpose(1, 0, 2, 3)))
    prev = prev.transpose(1, 0, 2, 3, 4, 5)
    y_off = jnp.einsum("bclgn,bcgepn,bcgel->bclgep", Cm, prev, jnp.exp(A_cum))
    return (y_diag + y_off).reshape(b, s, h, p)

def ssd_group(z, xbc, dt_raw, conv_w, conv_b, dt_bias, a_log, d_skip, norm_g):
    bsz, s, _ = z.shape
    xbc = jax.nn.silu(causal_depthwise_conv(xbc, conv_w, conv_b))
    xs, Bm, Cm = jnp.split(xbc, [D_SSD, D_SSD + SSD_GROUPS * SSD_STATE], axis=-1)
    xs = xs.reshape(bsz, s, SSD_HEADS, HEAD_DIM).astype(jnp.float32)
    Bm = Bm.reshape(bsz, s, SSD_GROUPS, SSD_STATE).astype(jnp.float32)
    Cm = Cm.reshape(bsz, s, SSD_GROUPS, SSD_STATE).astype(jnp.float32)
    dt = jax.nn.softplus(dt_raw.astype(jnp.float32) + dt_bias.astype(jnp.float32))
    A = -jnp.exp(a_log.astype(jnp.float32))
    y = ssd_scan(xs * dt[..., None], dt * A, Bm, Cm)
    y = y + xs * d_skip.astype(jnp.float32)[:, None]
    y = y.reshape(bsz, s, D_SSD).astype(z.dtype)
    return rmsnorm(y * jax.nn.silu(z), norm_g)

def chunk_band_attention(q, k, v, rel_bias):
    bsz, s, h, dh = q.shape
    nc = s // CHUNK
    pad = N_PREV_CHUNKS * CHUNK
    band_idx = np.arange(nc)[:, None] * CHUNK + np.arange(BAND)[None, :]
    kp = jnp.pad(k, ((0, 0), (pad, 0), (0, 0), (0, 0)))
    vp = jnp.pad(v, ((0, 0), (pad, 0), (0, 0), (0, 0)))
    kb = kp[:, band_idx]
    vb = vp[:, band_idx]
    qc = q.reshape(bsz, nc, CHUNK, h, dh)
    scores = jnp.einsum("bnqhd,bnkhd->bnhqk", qc, kb).astype(jnp.float32) * (dh ** -0.5)
    rel = np.clip(pad + np.arange(CHUNK)[:, None] - np.arange(BAND)[None, :],
                  -REL_CLIP, REL_CLIP) + REL_CLIP
    bias = rel_bias[:, rel].astype(jnp.float32)
    valid = (band_idx - pad) >= 0
    scores = jnp.where(valid[None, :, None, None, :], scores + bias[None, None], -jnp.inf)
    probs = jax.nn.softmax(scores, axis=-1).astype(v.dtype)
    out = jnp.einsum("bnhqk,bnkhd->bnqhd", probs, vb)
    return out.reshape(bsz, s, h * dh)

def hierarchical_moe(h, w_rg, b_rg, w_re, b_re, w1, w3, w2):
    T, d = h.shape
    g_prob = jax.nn.softmax((h @ w_rg + b_rg).astype(jnp.float32), axis=-1)
    g_p, g_idx = lax.top_k(g_prob, 1)
    e_logits = (h @ w_re + b_re).astype(jnp.float32).reshape(T, MOE_GROUPS, EXPERTS_PER_GROUP)
    e_logits = jnp.take_along_axis(e_logits, g_idx[:, :, None], axis=1)[:, 0]
    e_p, e_idx = lax.top_k(jax.nn.softmax(e_logits, axis=-1), TOP_K)
    e_p = e_p / jnp.sum(e_p, axis=-1, keepdims=True)
    gate = g_p * e_p
    expert_id = g_idx * EXPERTS_PER_GROUP + e_idx

    n_assign = T * TOP_K
    flat_e = expert_id.reshape(-1)
    flat_t = jnp.repeat(jnp.arange(T, dtype=jnp.int32), TOP_K)
    flat_g = gate.reshape(-1)
    order = jnp.argsort(flat_e)
    se = flat_e[order]
    counts = jnp.bincount(flat_e, length=N_EXPERTS)
    offsets = jnp.cumsum(counts) - counts
    padded = ((counts + MOE_BLOCK - 1) // MOE_BLOCK) * MOE_BLOCK
    pad_ends = jnp.cumsum(padded)
    pad_offsets = pad_ends - padded
    dest = pad_offsets[se] + (jnp.arange(n_assign) - offsets[se])
    n_blocks = n_assign // MOE_BLOCK + N_EXPERTS
    cap = n_blocks * MOE_BLOCK
    slot_tok = jnp.full((cap,), T, jnp.int32).at[dest].set(flat_t[order])
    slot_gate = jnp.zeros((cap,), h.dtype).at[dest].set(flat_g[order].astype(h.dtype))
    block_e = jnp.minimum(jnp.searchsorted(pad_ends, jnp.arange(n_blocks) * MOE_BLOCK, side="right"),
                          N_EXPERTS - 1).astype(jnp.int32)
    h_pad = jnp.concatenate([h, jnp.zeros((1, d), h.dtype)], axis=0)
    xb = h_pad[slot_tok].reshape(n_blocks, MOE_BLOCK, d)

    def expert_block(args):
        xblk, e = args
        return (jax.nn.silu(xblk @ w1[e]) * (xblk @ w3[e])) @ w2[e]

    yb = lax.map(expert_block, (xb, block_e)).reshape(cap, d) * slot_gate[:, None]
    return jnp.zeros((T + 1, d), h.dtype).at[slot_tok].add(yb)[:T]

def setup_inputs(seed: int = 0) -> dict:
    key = jax.random.key(seed)
    ks = jax.random.split(key, 26)
    f32 = jnp.float32

    def nrm(k, shape, scale):
        return jax.random.normal(k, shape, f32) * scale

    dt = jnp.exp(jax.random.uniform(ks[8], (DEPTH, SSD_HEADS), f32,
                                    minval=float(np.log(1e-3)), maxval=float(np.log(1e-1))))
    return {
        "x": nrm(ks[0], (BATCH, SEQ, D_MODEL), 1.0),
        "c": nrm(ks[1], (BATCH, D_MODEL), 1.0),
        "w_ada": nrm(ks[2], (DEPTH, D_MODEL, 6 * D_MODEL), D_MODEL ** -0.5),
        "b_ada": nrm(ks[3], (DEPTH, 6 * D_MODEL), 0.02),
        "norm_mix_g": 1.0 + nrm(ks[4], (DEPTH, D_MODEL), 0.02),
        "w_in": nrm(ks[5], (DEPTH, D_MODEL, IN_PROJ_DIM), D_MODEL ** -0.5),
        "conv_w": nrm(ks[6], (DEPTH, CONV_WIDTH, CONV_DIM), CONV_WIDTH ** -0.5),
        "conv_b": nrm(ks[7], (DEPTH, CONV_DIM), 0.02),
        "dt_bias": dt + jnp.log(-jnp.expm1(-dt)),
        "a_log": jnp.log(jax.random.uniform(ks[9], (DEPTH, SSD_HEADS), f32, minval=1.0, maxval=16.0)),
        "d_skip": 1.0 + nrm(ks[10], (DEPTH, SSD_HEADS), 0.02),
        "ssd_norm_g": 1.0 + nrm(ks[11], (DEPTH, D_SSD), 0.02),
        "rel_bias": nrm(ks[12], (DEPTH, ATT_HEADS, 2 * REL_CLIP + 1), 0.1),
        "attn_norm_g": 1.0 + nrm(ks[13], (DEPTH, D_ATT), 0.02),
        "w_out": nrm(ks[14], (DEPTH, D_MIX, D_MODEL), D_MIX ** -0.5),
        "norm_ffn_g": 1.0 + nrm(ks[15], (DEPTH, D_MODEL), 0.02),
        "w_router_group": nrm(ks[16], (DEPTH, D_MODEL, MOE_GROUPS), D_MODEL ** -0.5),
        "b_router_group": nrm(ks[17], (DEPTH, MOE_GROUPS), 0.01),
        "w_router_expert": nrm(ks[18], (DEPTH, D_MODEL, N_EXPERTS), D_MODEL ** -0.5),
        "b_router_expert": nrm(ks[19], (DEPTH, N_EXPERTS), 0.01),
        "w1": nrm(ks[20], (DEPTH, N_EXPERTS, D_MODEL, D_EXPERT), D_MODEL ** -0.5),
        "w3": nrm(ks[21], (DEPTH, N_EXPERTS, D_MODEL, D_EXPERT), D_MODEL ** -0.5),
        "w2": nrm(ks[22], (DEPTH, N_EXPERTS, D_EXPERT, D_MODEL), D_EXPERT ** -0.5),
        "final_norm_g": 1.0 + nrm(ks[23], (D_MODEL,), 0.02),
    }

def reference(x, c, w_ada, b_ada, norm_mix_g, w_in, conv_w, conv_b, dt_bias, a_log, d_skip,
              ssd_norm_g, rel_bias, attn_norm_g, w_out, norm_ffn_g, w_router_group,
              b_router_group, w_router_expert, b_router_expert, w1, w3, w2, final_norm_g):
    bsz, s, d = x.shape
    split_pts = np.cumsum([D_SSD, CONV_DIM, SSD_HEADS, D_ATT, D_ATT]).tolist()
    for l in range(DEPTH):
        mod = (jax.nn.silu(c) @ w_ada[l] + b_ada[l])[:, None, :]
        sh_m, sc_m, gt_m, sh_f, sc_f, gt_f = jnp.split(mod, 6, axis=-1)

        h = rmsnorm(x, norm_mix_g[l]) * (1.0 + sc_m) + sh_m
        proj = h @ w_in[l]
        z, xbc, dt_raw, q, k, v = jnp.split(proj, split_pts, axis=-1)
        y_ssd = ssd_group(z, xbc, dt_raw, conv_w[l], conv_b[l], dt_bias[l], a_log[l],
                          d_skip[l], ssd_norm_g[l])
        hs = (bsz, s, ATT_HEADS, HEAD_DIM)
        y_att = chunk_band_attention(q.reshape(hs), k.reshape(hs), v.reshape(hs), rel_bias[l])
        y_att = rmsnorm(y_att, attn_norm_g[l])
        y = jnp.concatenate([y_ssd, y_att], axis=-1) @ w_out[l]
        x = x + gt_m * y

        h = rmsnorm(x, norm_ffn_g[l]) * (1.0 + sc_f) + sh_f
        y = hierarchical_moe(h.reshape(bsz * s, d), w_router_group[l], b_router_group[l],
                             w_router_expert[l], b_router_expert[l], w1[l], w3[l], w2[l])
        x = x + gt_f * y.reshape(bsz, s, d)
    return rmsnorm(x, final_norm_g)


_drawn_inputs = setup_inputs


def setup_inputs(seed=0):
    import zlib

    import numpy as np

    out = dict(_drawn_inputs(seed))
    spreads = {}
    factors = {'d_skip': 27.225,
     'rel_bias': 3.26,
     'attn_norm_g': 4.694,
     'b_router_group': 14.605,
     'b_router_expert': 14.301,
     'final_norm_g': 8.152,
     'norm_mix_g': 3.057,
     'conv_b': 5.271,
     'ssd_norm_g': 6.533,
     'norm_ffn_g': 3.102}
    for name, (base, spread) in spreads.items():
        noise = np.random.default_rng([zlib.crc32(name.encode()), seed]).standard_normal(out[name].shape)
        drawn = base * np.exp(spread * noise) if base else spread * noise
        out[name] = __import__('jax').numpy.asarray(drawn.astype(out[name].dtype))
    for name, factor in factors.items():
        out[name] = (out[name] * factor).astype(out[name].dtype)
    return out
```

```python
from contextlib import ExitStack

import numpy as np
import concourse.bass as bass
from concourse import mybir

F32 = mybir.dt.float32
I32 = mybir.dt.int32
U32 = mybir.dt.uint32
ALU = mybir.AluOpType
ACT = mybir.ActivationFunctionType
AX = mybir.AxisListType

P = 128
T = 2048
NT = T // P
D = 1024
KD = D // P
CHUNK = 64
HD = 64
D_SSD = 1536
GROUPS = 4
GH = 6
NH = GROUPS * GH
GD = GH * HD
GF = GD // P
NSTATE = 128
D_ATT = 512
PAIRS = 4
CONV = 4
COL_Z = 0
COL_X = D_SSD
COL_B = 2 * D_SSD
COL_C = COL_B + GROUPS * NSTATE
COL_DT = COL_C + GROUPS * NSTATE
COL_Q = COL_DT + NH
COL_K = COL_Q + D_ATT
COL_V = COL_K + D_ATT
IN_COLS = COL_V + D_ATT
BACK = 8 * CHUNK
BAND = BACK + P
CLIP = 256
EXT = 768
MIX = 2 * D
KM = MIX // P
KS = D_SSD // P
NG = 4
NE = 32
PER_G = NE // NG
DE = 512
KE = DE // P
BLOCKS = 2 * T // P + NE
SLOTS = BLOCKS * P
W_BUFS = 3
EPS = 1e-6
NEG = -1e30
QT = T // 512


class Chain:

    def __init__(self, eng, sem):
        self.eng, self.sem, self.base, self.n = eng, sem, 0, 0

    def __call__(self, ins):
        ins.then_inc(self.sem, 1)
        self.n += 1
        self.eng.wait_ge(self.sem, self.base + self.n)


def bc(ap, axis, shape):
    return ap.unsqueeze(axis).broadcast_to(shape)


def rows(ap2d):
    return bass.AP(ap2d.tensor, ap2d.offset, [[0, P]] + list(ap2d.ap)[1:])


def prepare(nc, a, s):
    with ExitStack() as ctx:
        sb = lambda n, sh, dt=F32: ctx.enter_context(nc.sbuf_tensor("p_" + n, sh, dt))
        sem = lambda n: ctx.enter_context(nc.semaphore("p_" + n))
        ps = [ctx.enter_context(nc.psum_tensor(f"p_ps{i}", [P, 512], F32)) for i in range(8)]
        wa = [sb(f"wa{i}", [P, KD, 512]) for i in range(2)]
        brow = [sb(f"brow{i}", [1, 512]) for i in range(2)]
        modrow = [sb(f"modrow{i}", [P, 512]) for i in range(2)]
        modcol = sb("modcol", [P, 6, KD])
        silc = sb("silc", [P, KD])
        silcb = sb("silcb", [P, KD, P])
        xt = [sb(f"xt{i}", [P, D]) for i in range(2)]
        xn = [sb(f"xn{i}", [P, D]) for i in range(2)]
        junk = [sb(f"junk{i}", [P, D]) for i in range(2)]
        std = sb("std", [P, NT])
        ssq = sb("ssq", [P, NT])
        rstd = sb("rstd", [P, NT])
        gcol = sb("gcol", [P, 2, KD])
        wdt = sb("wdt", [P, KD, NH])
        hrow = sb("hrow", [P, 2, NH])
        tmp = [sb(f"tmp{i}", [P, NT * NH]) for i in range(6)]
        accT = sb("accT", [NH, T])
        extb = sb("extb", [8, EXT])

        ada_loaded = [sem("ada_loaded0"), sem("ada_loaded1")]
        x_loaded = [sem("x_loaded0"), sem("x_loaded1")]
        small_loaded = sem("small_loaded")
        consts_made = sem("consts_made")
        pool_step = sem("pool_step")
        silc_ready = sem("silc_ready")
        silcb_ready = sem("silcb_ready")
        ada_summed = sem("ada_summed")
        ada_row = sem("ada_row")
        ada_turned = sem("ada_turned")
        ada_col = sem("ada_col")
        ssq_ready = sem("ssq_ready")
        rstd_ready = sem("rstd_ready")
        std_ready = sem("std_ready")
        xn_ready = sem("xn_ready")
        x_turned = sem("x_turned")
        h_written = sem("h_written")
        v_step = sem("v_step")
        dt_raw = sem("dt_raw")
        to_scalar = sem("to_scalar")
        from_scalar = sem("from_scalar")
        a_ready = sem("a_ready")
        cum_ready = sem("cum_ready")
        accT_ready = sem("accT_ready")
        stored = sem("stored")
        ext_loaded = sem("ext_loaded")
        ext_ready = sem("ext_ready")

        block = ctx.enter_context(nc.Block())
        wada = a["w_ada"].rearrange("(k p) n -> p k n", p=P)
        ROWS = {2: 0, 5: 1}
        gates = sb("gates", [1, 2, D])
        gate_row = sem("gate_row")

        @block.sync
        def _(sp):
            for j in range(12):
                if j >= 2:
                    sp.wait_ge(ada_summed, j - 1)
                sp.dma_start(wa[j % 2][:], wada[:, :, j * 512:(j + 1) * 512]).then_inc(ada_loaded[j % 2], 16)
                sp.dma_start(brow[j % 2][:], a["b_ada"][:, j * 512:(j + 1) * 512]).then_inc(ada_loaded[j % 2], 16)
            sp.wait_ge(accT_ready, QT)
            sp.dma_start(a["acc_dram"], accT[:]).then_inc(stored, 16)
            sp.wait_ge(ext_ready, 1)
            sp.dma_start(a["ext_dram"].rearrange("p h j -> h p j"), bc(extb[:], 1, [2 * PAIRS, P, EXT])).then_inc(stored, 16)
            sp.wait_ge(gate_row, 4)
            sp.dma_start(a["gates_dram"], gates[:].rearrange("a i n -> a (i n)")).then_inc(stored, 16)
            sp.wait_ge(stored, 48)

        @block.gpsimd
        def _(pool):
            pool.dma_start(gcol[:, 0, :], a["norm_mix_g"]).then_inc(small_loaded, 16)
            pool.dma_start(gcol[:, 1, :], a["norm_ffn_g"]).then_inc(small_loaded, 16)
            pool.dma_start(wdt[:], a["w_dt"]).then_inc(small_loaded, 16)
            pool.dma_start(hrow[:, 0, :], rows(a["dt_bias"])).then_inc(small_loaded, 16)
            pool.dma_start(hrow[:, 1, :], rows(a["a_log"])).then_inc(small_loaded, 16)
            pool.dma_start(extb[:, EXT - 385:EXT - 1], a["rel_rev"][:, 0:384]).then_inc(ext_loaded, 16)
            pool.memset(s.ident[:], 0.0).then_inc(pool_step, 1)
            pool.memset(s.tri[:], 1.0).then_inc(pool_step, 1)
            pool.memset(s.ones[:], 1.0).then_inc(consts_made, 1)
            pool.memset(s.eps[:], EPS).then_inc(consts_made, 1)
            pool.wait_ge(pool_step, 2)
            pool.affine_select(out=s.ident[:], in_=s.ident[:], compare_op=ALU.not_equal, fill=1.0, base=0,
                               pattern=[[-1, P]], channel_multiplier=1).then_inc(consts_made, 1)
            pool.affine_select(out=s.tri[:], in_=s.tri[:], compare_op=ALU.is_ge, fill=0.0, base=0,
                               pattern=[[1, P]], channel_multiplier=-1).then_inc(consts_made, 1)
            for t in range(NT):
                if t >= 2:
                    pool.wait_ge(xn_ready, t - 1)
                pool.dma_start(xt[t % 2][:], a["x"][t * P:(t + 1) * P, :]).then_inc(x_loaded[t % 2], 16)

        @block.tensor
        def _(pe):
            pe.wait_ge(consts_made, 4)
            pe.wait_ge(silcb_ready, 1)

            def turn_rows(j):
                pe.wait_ge(ada_row, j + 1)
                if j >= 2:
                    pe.wait_ge(ada_col, j - 1)
                for q in range(4):
                    mm = pe.transpose(ps[2 + j % 2][:, q * P:(q + 1) * P],
                                      modrow[j % 2][:, q * P:(q + 1) * P], s.ident[:])
                mm.then_inc(ada_turned, 1)

            for j in range(12):
                pe.wait_ge(ada_loaded[j % 2], 32 * (j // 2 + 1))
                if j >= 2:
                    pe.wait_ge(ada_row, j - 1)
                for k in range(KD):
                    pe.matmul(ps[j % 2][:], silcb[:, k, :], wa[j % 2][:, k, :], start=(k == 0), stop=False)
                pe.matmul(ps[j % 2][:], s.ones[0:1, :], brow[j % 2][:], start=False, stop=True).then_inc(ada_summed, 1)
                if j >= 1:
                    turn_rows(j - 1)
            turn_rows(11)
            for n in range(2 * NT):
                t, half = n // 2, n % 2
                pe.wait_ge(xn_ready, t + 1)
                if n >= 4:
                    pe.wait_ge(h_written, n - 3)
                for q in range(4):
                    k = half * 4 + q
                    mm = pe.transpose(ps[4 + n % 4][:, q * P:(q + 1) * P], xn[t % 2][:, k * P:(k + 1) * P], s.ident[:])
                mm.then_inc(x_turned, 1)
            pe.wait_ge(h_written, 2 * NT)
            pe.wait_ge(small_loaded, 80)
            pe.wait_ge(ada_row, 12)
            for t in range(NT):
                for k in range(KD):
                    mm = pe.matmul(ps[0][:, t * NH:(t + 1) * NH], s.hT[:, k, t * P:(t + 1) * P], wdt[:, k, :],
                                   start=(k == 0), stop=(k == KD - 1))
            mm.then_inc(dt_raw, 1)
            pe.wait_ge(a_ready, 1)
            pe.matmul(ps[1][:, 0:NT * NH], s.tri[:], tmp[5][:], start=True, stop=True)
            pe.matmul(ps[2][:, 0:NT * NH], s.ones[:], tmp[5][:], start=True, stop=True).then_inc(cum_ready, 1)
            for t in range(NT):
                mm = pe.matmul(ps[4 + t // 4][0:NH, (t % 4) * P:(t % 4 + 1) * P], tmp[5][:, t * NH:(t + 1) * NH],
                               s.tri[:], start=True, stop=True)
            mm.then_inc(cum_ready, 1)

        @block.scalar
        def _(act):
            act.dma_start(silc[:], a["c"]).then_inc(silc_ready, 16)
            act.wait_ge(silc_ready, 16)
            act.activation(silc[:], silc[:], ACT.Silu).then_inc(silc_ready, 1)
            act.wait_ge(consts_made, 4)
            for t in range(NT + 1):
                if t < NT:
                    act.wait_ge(x_loaded[t % 2], 16 * (t // 2 + 1))
                    act.activation(junk[t % 2][:], xt[t % 2][:], ACT.Square, scale=D ** -0.5,
                                   accum_out=ssq[:, t:t + 1]).then_inc(ssq_ready, 1)
                    act.wait_ge(ssq_ready, t + 1)
                    act.activation(std[:, t:t + 1], ssq[:, t:t + 1], ACT.Sqrt, bias=s.eps[:]).then_inc(std_ready, 1)
                if t >= 1:
                    u = t - 1
                    act.wait_ge(rstd_ready, t)
                    if u >= 2:
                        act.wait_ge(x_turned, 2 * (u - 1))
                    act.activation(xn[u % 2][:], xt[u % 2][:], ACT.Copy, scale=rstd[:, u:u + 1]).then_inc(xn_ready, 1)
            act.wait_ge(to_scalar, 1)
            act.activation(tmp[1][:], tmp[1][:], ACT.Exp, scale=-1.0).then_inc(from_scalar, 1)
            act.activation(hrow[:, 1, :], hrow[:, 1, :], ACT.Exp).then_inc(from_scalar, 1)
            act.wait_ge(to_scalar, 2)
            act.activation(tmp[3][:], tmp[2][:], ACT.Ln).then_inc(from_scalar, 1)
            act.wait_ge(to_scalar, 3)
            act.activation(tmp[1][:], tmp[0][:], ACT.Exp).then_inc(from_scalar, 1)
            act.wait_ge(cum_ready, 2)
            for q in range(QT):
                act.activation(accT[:, q * 512:(q + 1) * 512], ps[4 + q][0:NH, :], ACT.Copy).then_inc(accT_ready, 1)

        @block.vector
        def _(dve):
            link = Chain(dve, v_step)
            dve.wait_ge(silc_ready, 17)
            dve.tensor_copy(silcb[:], bc(silc[:], 2, [P, KD, P])).then_inc(silcb_ready, 1)
            dve.wait_ge(ext_loaded, 16)
            link(dve.memset(extb[:, EXT - 1:EXT], 0.0))
            link(dve.memset(extb[:, 0:EXT - 385], 0.0))
            dve.tensor_scalar(extb[:, 0:EXT - 385], extb[:, 0:EXT - 385], extb[:, EXT - 385:EXT - 384], None,
                              ALU.add).then_inc(ext_ready, 1)

            def column_of(j):
                dve.wait_ge(ada_turned, j + 1)
                dve.tensor_copy(modcol[:, j // 2, (j % 2) * 4:(j % 2) * 4 + 4],
                                ps[2 + j % 2][:, 0:512:P]).then_inc(ada_col, 1)

            for j in range(12):
                dve.wait_ge(ada_summed, j + 1)
                if j >= 2:
                    dve.wait_ge(ada_turned, j - 1)
                if j in (6, 7, 8, 9):
                    dve.wait_ge(gate_row, min(j - 5, 2))
                dve.tensor_copy(modrow[j % 2][:], ps[j % 2][:]).then_inc(ada_row, 1)
                if j // 2 in ROWS:
                    dve.wait_ge(ada_row, j + 1)
                    i = ROWS[j // 2]
                    dve.tensor_copy(gates[:, i, (j % 2) * 512:(j % 2 + 1) * 512], modrow[j % 2][0:1, :]
                                    ).then_inc(gate_row, 1)
                if j >= 1:
                    column_of(j - 1)
            column_of(11)
            dve.wait_ge(ada_col, 12)
            dve.wait_ge(small_loaded, 80)
            for m, (sh, sc) in enumerate(((0, 1), (3, 4))):
                link(dve.tensor_scalar(modcol[:, sc, :], modcol[:, sc, :], 1.0, None, ALU.add))
                link(dve.tensor_tensor(s.scale_col[:, m, :], modcol[:, sc, :], gcol[:, m, :], ALU.mult))
                link(dve.tensor_copy(s.shift_col[:, m, :], modcol[:, sh, :]))

            def rstd_of(t):
                dve.wait_ge(std_ready, t + 1)
                dve.reciprocal(rstd[:, t:t + 1], std[:, t:t + 1]).then_inc(rstd_ready, 1)

            rstd_of(0)
            for t in range(NT):
                if t + 1 < NT:
                    rstd_of(t + 1)
                for half in range(2):
                    n = 2 * t + half
                    dve.wait_ge(x_turned, n + 1)
                    for q in range(4):
                        k = half * 4 + q
                        mm = dve.tensor_scalar(s.hT[:, k, t * P:(t + 1) * P], ps[4 + n % 4][:, q * P:(q + 1) * P],
                                               s.scale_col[:, 0, k:k + 1], s.shift_col[:, 0, k:k + 1],
                                               ALU.mult, ALU.add)
                    mm.then_inc(h_written, 1)
            v3 = lambda t: t[:].rearrange("p (c h) -> p c h", h=NH)
            dve.wait_ge(dt_raw, 1)
            link(dve.tensor_tensor(v3(tmp[0]), ps[0][:, 0:NT * NH].rearrange("p (c h) -> p c h", h=NH),
                                   bc(hrow[:, 0, :], 1, [P, NT, NH]), ALU.add))
            link(dve.tensor_scalar(tmp[1][:], tmp[0][:], -1.0, None, ALU.mult))
            dve.tensor_tensor(tmp[1][:], tmp[1][:], tmp[0][:], ALU.max).then_inc(to_scalar, 1)
            dve.wait_ge(from_scalar, 2)
            link(dve.tensor_scalar(tmp[2][:], tmp[1][:], 1.0, None, ALU.add))
            link(dve.tensor_scalar(tmp[4][:], tmp[2][:], -1.0, None, ALU.add))
            dve.tensor_scalar(tmp[5][:], tmp[4][:], 0.0, None, ALU.is_equal).then_inc(to_scalar, 1)
            dve.wait_ge(to_scalar, 2)
            link(dve.tensor_tensor(tmp[4][:], tmp[4][:], tmp[5][:], ALU.add))
            link(dve.reciprocal(tmp[4][:], tmp[4][:]))
            link(dve.tensor_tensor(tmp[4][:], tmp[4][:], tmp[1][:], ALU.mult))
            link(dve.tensor_tensor(tmp[5][:], tmp[5][:], tmp[1][:], ALU.mult))
            dve.wait_ge(from_scalar, 3)
            link(dve.tensor_tensor(tmp[4][:], tmp[4][:], tmp[3][:], ALU.mult))
            link(dve.tensor_tensor(tmp[4][:], tmp[4][:], tmp[5][:], ALU.add))
            link(dve.tensor_scalar(tmp[0][:], tmp[0][:], 0.0, None, ALU.max))
            link(dve.tensor_tensor(s.dt[:], tmp[4][:], tmp[0][:], ALU.add))
            link(dve.tensor_tensor(v3(tmp[5]), v3(s.dt), bc(hrow[:, 1, :], 1, [P, NT, NH]), ALU.mult))
            dve.tensor_scalar(tmp[5][:], tmp[5][:], -1.0, None, ALU.mult).then_inc(a_ready, 1)
            dve.wait_ge(cum_ready, 1)
            link(dve.tensor_copy(s.acc[:], ps[1][:, 0:NT * NH]))
            link(dve.tensor_tensor(tmp[0][:], ps[2][:, 0:NT * NH], s.acc[:], ALU.subtract))
            link(dve.tensor_scalar(tmp[0][:], tmp[0][:], 0.0, None, ALU.min))
            dve.nop().then_inc(to_scalar, 1)
            dve.wait_ge(from_scalar, 4)
            link(dve.tensor_tensor(s.dtdec[:], s.dt[:], tmp[1][:], ALU.mult))


def ssd(nc, a, s):
    with ExitStack() as ctx:
        sb = lambda n, sh, dt=F32: ctx.enter_context(nc.sbuf_tensor("g_" + n, sh, dt))
        sem = lambda n: ctx.enter_context(nc.semaphore("g_" + n))
        ps = [ctx.enter_context(nc.psum_tensor(f"g_ps{i}", [P, 512], F32)) for i in range(8)]
        RING, TILES, CT, CB = 4, 8, 4, 3
        wr = [sb(f"wr{i}", [P, KD, P]) for i in range(RING)]
        raw = sb("raw", [P, CONV - 1 + T])
        act_T = [sb(f"act{i}", [P, T]) for i in range(5)]
        z_T = sb("z_T", [P, GF, T])
        par = sb("par", [P, 31])
        dt_g = sb("dt_g", [P, 3, NT, GH])
        abc = [sb(f"abc{i}", [P, GH, P]) for i in range(2)]
        ea = [sb(f"ea{i}", [P, GH, P]) for i in range(2)]
        lm = [sb(f"lm{i}", [P, GH, P]) for i in range(2)]
        cs = [sb(f"cs{i}", [P, GH, P]) for i in range(2)]
        cbm = sb("cbm", [P, P])
        xdt = [sb(f"xdt{i}", [P, GD]) for i in range(2)]
        xde = [sb(f"xde{i}", [P, GD]) for i in range(2)]
        btok = [sb(f"btok{i}", [P, NSTATE]) for i in range(2)]
        st = [sb(f"st{i}", [P, GD]) for i in range(2)]
        stmp = sb("stmp", [P, GD])
        yb = [sb(f"yb{i}", [P, GF, P]) for i in range(2)]
        sq = [sb(f"sq{i}", [P, GF, P]) for i in range(2)]
        yo = [sb(f"yo{i}", [P, GF, P]) for i in range(2)]

        w_loaded = [sem(f"w_loaded{i}") for i in range(RING)]
        w_turn = sem("w_turn")
        par_loaded = sem("par_loaded")
        acc_full = sem("acc_full")
        acc_free = sem("acc_free")
        conv_done = sem("conv_done")
        raw_zero = sem("raw_zero")
        silu_done = sem("silu_done")
        v_step = sem("v_step")
        abc_loaded = [sem("abc_loaded0"), sem("abc_loaded1")]
        seg_done = sem("seg_done")
        ea_done = sem("ea_done")
        e_done = sem("e_done")
        lm_done = sem("lm_done")
        cs_done = sem("cs_done")
        x_turned = sem("x_turned")
        xdt_done = sem("xdt_done")
        btok_done = sem("btok_done")
        cb_full = sem("cb_full")
        cbm_done = sem("cbm_done")
        st_full = sem("st_full")
        st_done = sem("st_done")
        y_full = sem("y_full")
        y_read = sem("y_read")
        gated = sem("gated")
        sq_done = sem("sq_done")
        ss_full = sem("ss_full")
        ss_read = sem("ss_read")
        y_out = sem("y_out")
        y_stored = [sem("y_stored0"), sem("y_stored1")]
        block = ctx.enter_context(nc.Block())

        w_view = a["w_in"].rearrange("(k p) n -> p k n", p=P)

        def tile_col(g, m):
            if m < GF:
                return g * GD + (COL_X + m * P)
            if m < 5:
                return g * NSTATE + (COL_B if m == CB else COL_C)
            return g * GD + (COL_Z + (m - 5) * P)

        @block.sync
        def _(sp):
            sp.sem_inc(acc_full, RING * QT)
            sp.sem_inc(y_stored[0], 16)
            sp.sem_inc(y_stored[1], 16)
            with sp.Fori(0, GROUPS) as g:
                sp.dma_start(par[:], a["group_params"][bass.ds(g, 1), :, :].rearrange("a p n -> p (a n)")
                             ).then_inc(par_loaded, 16)
                for m in range(TILES):
                    col = sp.snap(tile_col(g, m), min_val=0, max_val=IN_COLS - P)
                    sp.wait_ge(acc_full, g * (TILES * QT) + (m + 1) * QT)
                    if m == 5:
                        sp.sem_inc(w_turn, 1)
                    sp.dma_start(wr[m % RING][:], w_view[:, :, bass.ds(col, P)]
                                 ).then_inc(w_loaded[m % RING], 16)
                head0 = sp.snap(g * GH, min_val=0, max_val=NH - GH)
                feat0 = sp.snap(g * GF, min_val=0, max_val=KS - GF)
                for c in range(NT + 2):
                    if c < NT:
                        sp.wait_ge(seg_done, g * NT + (c + 1))
                        sp.wait_ge(ea_done, g * NT + (c + 1))
                        src = a["acc_dram"][bass.ds(head0, GH), c * P:(c + 1) * P]
                        sp.dma_start(abc[c % 2][:], src.partition_broadcast(P)).then_inc(abc_loaded[c % 2], 16)
                    if c >= 2:
                        u = c - 2
                        sp.wait_ge(y_out, g * NT + (u + 1))
                        dst = a["yT_dram"][bass.ds(feat0, GF), :, u * P:(u + 1) * P].rearrange("j p t -> p j t")
                        sp.dma_start(dst, yo[u % 2][:]).then_inc(y_stored[u % 2], 16)
            for i in range(2):
                sp.wait_ge(y_stored[i], 16 + 16 * GROUPS * NT // 2)

        @block.gpsimd
        def _(pool):
            with pool.Fori(0, GROUPS) as g:
                for c in range(1, NT):
                    pool.wait_ge(ea_done, g * NT + (c + 3))
                    pool.wait_ge(silu_done, g * 5 + 5)
                    if c >= 3:
                        pool.wait_ge(y_full, g * NT + (c - 1))
                    pool.tensor_tensor(cs[c % 2][:], bc(act_T[CT][:, c * P:(c + 1) * P], 1, [P, GH, P]), ea[c % 2][:],
                                       ALU.mult).then_inc(cs_done, 1)

        @block.tensor
        def _(pe):
            with pe.Fori(0, GROUPS) as g:
                for m in range(TILES):
                    pe.wait_ge(w_loaded[m % RING], g * (16 * TILES // RING) + 16 * (m // RING + 1))
                    for q in range(QT):
                        n = m * QT + q
                        pe.wait_ge(acc_free, g * (TILES * QT) + (n + 1))
                        for k in range(KD):
                            mm = pe.matmul(ps[n % 2][:], wr[m % RING][:, k, :], s.hT[:, k, q * 512:(q + 1) * 512],
                                           start=(k == 0), stop=(k == KD - 1))
                        mm.then_inc(acc_full, 1)

                pe.wait_ge(silu_done, g * 5 + 5)
                pe.wait_ge(acc_free, g * (TILES * QT) + (TILES * QT + 2))

                def turn(c):
                    cols = slice(c * P, (c + 1) * P)
                    pe.wait_ge(xdt_done, g * NT + (c + 1))
                    pe.wait_ge(btok_done, g * NT + (c + 1))
                    for j in range(GF):
                        pe.transpose(ps[2][:, j * P:(j + 1) * P], act_T[j][:, cols], s.ident[:])
                    pe.transpose(ps[0][:, 0:P], act_T[CB][:, cols], s.ident[:]).then_inc(x_turned, 1)
                    pe.wait_ge(cbm_done, g * NT + (c + 1))
                    pe.matmul(ps[3][:, 0:P], act_T[CB][:, cols], act_T[CT][:, cols], start=True, stop=True
                              ).then_inc(cb_full, 1)

                def sums(c):
                    pe.wait_ge(sq_done, g * NT + (c + 1))
                    if c == 0:
                        pe.wait_ge(ss_read, g + 1)
                    for j in range(GF):
                        mm = pe.matmul(ps[7][:, c:c + 1], sq[c % 2][:, j, :], s.ones[:, 0:1],
                                       start=(j == 0), stop=(j == GF - 1))
                    mm.then_inc(ss_full, 1)

                turn(0)
                for c in range(NT):
                    if c + 1 < NT:
                        turn(c + 1)
                    pe.wait_ge(xdt_done, g * NT + (c + 2))
                    pe.wait_ge(btok_done, g * NT + (c + 2))
                    pe.wait_ge(st_done, g * NT + (c + 1))
                    pe.matmul(ps[4][:, 0:GD], btok[c % 2][:], xde[c % 2][:], start=True, stop=True
                              ).then_inc(st_full, 1)
                    pe.wait_ge(lm_done, g * NT + (c + 1))
                    if c > 0:
                        pe.wait_ge(cs_done, g * (NT - 1) + c)
                    pe.wait_ge(y_read, g * NT + (c + 1))
                    for h in range(GH):
                        out = ps[5 + c % 2][64 * (h % 2):64 * (h % 2) + 64, (h // 2) * P:(h // 2 + 1) * P]
                        hc = slice(h * HD, (h + 1) * HD)
                        if c > 0:
                            pe.matmul(out, st[c % 2][:, hc], cs[c % 2][:, h, :], start=True, stop=False)
                        mm = pe.matmul(out, xdt[c % 2][:, hc], lm[c % 2][:, h, :], start=(c == 0), stop=True)
                    mm.then_inc(y_full, 1)
                    if c >= 1:
                        sums(c - 1)
                sums(NT - 1)

        @block.scalar
        def _(act):
            act.sem_inc(ea_done, 2)
            act.sem_inc(btok_done, 1)
            act.sem_inc(acc_free, 2)
            with act.Fori(0, GROUPS) as g:
                def silu(m):
                    act.wait_ge(conv_done, g * 5 + (m + 2))
                    act.activation(act_T[m][:], act_T[m][:], ACT.Silu, bias=par[:, 20 + m:21 + m]
                                   ).then_inc(silu_done, 1)

                for m in range(TILES):
                    for q in range(QT):
                        n = m * QT + q
                        cols = slice(q * 512, (q + 1) * 512)
                        act.wait_ge(acc_full, g * (TILES * QT) + (RING * QT + n + 1))
                        if m < 5:
                            if q == 0:
                                act.wait_ge(conv_done, g * 5 + (m + 1))
                            act.activation(raw[:, CONV - 1 + q * 512:CONV - 1 + (q + 1) * 512], ps[n % 2][:],
                                           ACT.Copy).then_inc(acc_free, 1)
                        else:
                            if m == 5 and q == 0:
                                act.wait_ge(gated, g * NT + 1)
                            act.activation(z_T[:, m - 5, cols], ps[n % 2][:], ACT.Silu).then_inc(acc_free, 1)
                        if q == 1 and 1 <= m <= 5:
                            silu(m - 1)
                for c in range(NT + 1):
                    if c < NT:
                        act.wait_ge(abc_loaded[c % 2], g * (8 * NT) + 16 * (c // 2 + 1))
                        if c >= 3:
                            act.wait_ge(cs_done, g * (NT - 1) + (c - 2))
                        act.wait_ge(st_done, g * NT + max(c, 1))
                        act.activation(ea[c % 2][:], abc[c % 2][:], ACT.Exp).then_inc(ea_done, 1)
                        act.wait_ge(x_turned, g * NT + (c + 1))
                        if c >= 2:
                            act.wait_ge(st_full, g * NT + (c - 1))
                        act.activation(btok[c % 2][:], ps[0][:, 0:P], ACT.Copy).then_inc(btok_done, 1)
                        act.wait_ge(seg_done, g * NT + (c + 3))
                        act.activation(lm[c % 2][:], lm[c % 2][:], ACT.Exp).then_inc(e_done, 1)
                    if c >= 1:
                        u = c - 1
                        act.wait_ge(gated, g * NT + (u + 2))
                        if u >= 2:
                            act.wait_ge(ss_full, g * NT + (u - 1))
                        act.activation(sq[u % 2][:], yb[u % 2][:], ACT.Square).then_inc(sq_done, 1)

        @block.vector
        def _(dve):
            dve.sem_inc(seg_done, 2)
            dve.sem_inc(conv_done, 1)
            dve.sem_inc(gated, 1)
            dve.sem_inc(xdt_done, 1)
            dve.sem_inc(cbm_done, 1)
            dve.sem_inc(st_done, 1)
            dve.sem_inc(y_read, 2)
            dve.sem_inc(ss_read, 1)
            dve.memset(raw[:, 0:CONV - 1], 0.0).then_inc(raw_zero, 1)
            dve.memset(s.norm_sum[:], 0.0).then_inc(raw_zero, 1)
            dve.wait_ge(raw_zero, 2)
            STEPS = 3 + 5 * (CONV - 1) + NT + (NT - 1) + 1
            with dve.Fori(0, GROUPS) as g:
                link = Chain(dve, v_step)
                link.base = g * STEPS
                dve.wait_ge(par_loaded, g * 16 + 16)
                for i, t in enumerate((s.dt, s.dtdec, s.acc)):
                    link(dve.tensor_copy(dt_g[:, i, :, :],
                                         t[:].rearrange("p (c h) -> p c h", h=NH)[:, :, bass.ds(g * GH, GH)]))
                for m in range(5):
                    dve.wait_ge(acc_free, g * (TILES * QT) + ((m + 1) * QT + 2))
                    for j in range(CONV):
                        w = par[:, m * CONV + j:m * CONV + j + 1]
                        if j == 0:
                            link(dve.tensor_scalar(act_T[m][:], raw[:, 0:T], w, None, ALU.mult))
                        else:
                            ins = dve.scalar_tensor_tensor(act_T[m][:], raw[:, j:j + T], w, act_T[m][:],
                                                           ALU.mult, ALU.add)
                            if j < CONV - 1:
                                link(ins)
                            else:
                                ins.then_inc(conv_done, 1)

                def state(c):
                    dve.wait_ge(st_full, g * NT + (c + 1))
                    if c >= 1:
                        dve.wait_ge(y_full, g * NT + c)
                    if c == 0:
                        dve.tensor_copy(st[1][:], ps[4][:, 0:GD]).then_inc(st_done, 1)
                    else:
                        dve.wait_ge(st_done, g * NT + (c + 1))
                        dve.wait_ge(ea_done, g * NT + (c + 3))
                        v = lambda t: t[:].rearrange("p (h d) -> p h d", d=HD)
                        link(dve.tensor_tensor(v(stmp), v(st[c % 2]), ea[c % 2][:, :, P - 1:P].broadcast_to([P, GH, HD]),
                                               ALU.mult))
                        dve.tensor_tensor(st[(c + 1) % 2][:], stmp[:], ps[4][:, 0:GD], ALU.add).then_inc(st_done, 1)

                def finish(c):
                    cols = slice(c * P, (c + 1) * P)
                    dve.wait_ge(y_full, g * NT + (c + 1))
                    if c >= 2:
                        dve.wait_ge(sq_done, g * NT + (c - 1))
                    for j in range(GF):
                        ins = dve.scalar_tensor_tensor(yb[c % 2][:, j, :], act_T[j][:, cols], par[:, 25 + j:26 + j],
                                                       ps[5 + c % 2][:, j * P:(j + 1) * P], ALU.mult, ALU.add)
                    ins.then_inc(y_read, 1)
                    dve.wait_ge(y_read, g * NT + (c + 3))
                    dve.tensor_tensor(yb[c % 2][:], yb[c % 2][:], z_T[:, :, cols], ALU.mult).then_inc(gated, 1)
                    dve.wait_ge(gated, g * NT + (c + 2))
                    dve.wait_ge(y_stored[c % 2], g * (8 * NT) + 16 * (c // 2 + 1))
                    for j in range(GF):
                        ins = dve.tensor_scalar(yo[c % 2][:, j, :], yb[c % 2][:, j, :], par[:, 28 + j:29 + j], None,
                                                ALU.mult)
                    ins.then_inc(y_out, 1)

                for c in range(NT):
                    dve.wait_ge(abc_loaded[c % 2], g * (8 * NT) + 16 * (c // 2 + 1))
                    if c >= 2:
                        dve.wait_ge(y_full, g * NT + (c - 1))
                    for h in range(GH):
                        ins = dve.tensor_scalar(lm[c % 2][:, h, :], abc[c % 2][:, h, :], dt_g[:, 2, c, h:h + 1], 0.0,
                                                ALU.subtract, ALU.min)
                    ins.then_inc(seg_done, 1)
                    dve.wait_ge(x_turned, g * NT + (c + 1))
                    x3 = ps[2][:, 0:GD].rearrange("p (h d) -> p h d", d=HD)
                    v = lambda t: t[:].rearrange("p (h d) -> p h d", d=HD)
                    link(dve.tensor_tensor(v(xdt[c % 2]), x3, bc(dt_g[:, 0, c, :], 2, [P, GH, HD]), ALU.mult))
                    dve.tensor_tensor(v(xde[c % 2]), x3, bc(dt_g[:, 1, c, :], 2, [P, GH, HD]), ALU.mult
                                      ).then_inc(xdt_done, 1)
                    dve.wait_ge(cb_full, g * NT + (c + 1))
                    if c >= 1:
                        dve.wait_ge(lm_done, g * NT + c)
                    dve.tensor_tensor(cbm[:], ps[3][:, 0:P], s.tri[:], ALU.mult).then_inc(cbm_done, 1)
                    dve.wait_ge(cbm_done, g * NT + (c + 2))
                    dve.wait_ge(e_done, g * NT + (c + 1))
                    dve.tensor_tensor(lm[c % 2][:], lm[c % 2][:], bc(cbm[:], 1, [P, GH, P]), ALU.mult
                                      ).then_inc(lm_done, 1)
                    state(c)
                    if c >= 1:
                        finish(c - 1)
                finish(NT - 1)
                dve.wait_ge(ss_full, g * NT + NT)
                link(dve.tensor_tensor(s.norm_sum[:, 0, :], s.norm_sum[:, 0, :], ps[7][:, 0:NT], ALU.add))
                dve.nop().then_inc(ss_read, 1)
                assert link.n == STEPS


def attend(nc, a, s):
    with ExitStack() as ctx:
        sb = lambda n, sh, dt=F32: ctx.enter_context(nc.sbuf_tensor("t_" + n, sh, dt))
        sem = lambda n: ctx.enter_context(nc.semaphore("t_" + n))
        scores = [ctx.enter_context(nc.psum_tensor(f"t_scores{i}", [P, 1024], F32)) for i in range(2)]
        turned_ps = ctx.enter_context(nc.psum_tensor("t_turned", [P, 1024], F32))
        out_ps = [ctx.enter_context(nc.psum_tensor(f"t_out{i}", [P, 512], F32)) for i in range(2)]
        NK = BAND // P
        UNITS = 2 * NT
        ACCS = 3 * QT
        w = [sb(f"w{i}", [P, KD, P]) for i in range(3)]
        bias = sb("bias", [P, 2 * PAIRS, BAND])
        norm_g = sb("norm_g", [P, PAIRS])
        q_T = sb("q_T", [P, T])
        k_T = sb("k_T", [P, T])
        v_r = sb("v_r", [P, NT, P])
        pb = [sb(f"pb{i}", [P, BAND]) for i in range(3)]
        pt = [sb(f"pt{i}", [P, BAND]) for i in range(2)]
        nmax = [sb(f"nmax{i}", [P, 1]) for i in range(3)]
        rsum = [sb(f"rsum{i}", [P, 1]) for i in range(3)]
        rinv = [sb(f"rinv{i}", [P, 1]) for i in range(3)]
        o_T = sb("o_T", [P, T])
        sq = sb("sq", [P, T])
        yo = sb("yo", [P, T])

        w_loaded = sem("w_loaded")
        w_turn = sem("w_turn")
        bias_loaded = sem("bias_loaded")
        bias_ready = sem("bias_ready")
        acc_full = sem("acc_full")
        acc_free = sem("acc_free")
        s_full = sem("s_full")
        biased = sem("biased")
        max_done = sem("max_done")
        exp_done = sem("exp_done")
        probs_done = sem("probs_done")
        turned = sem("turned")
        pt_done = sem("pt_done")
        out_full = sem("out_full")
        out_read = sem("out_read")
        sq_done = sem("sq_done")
        ss_full = sem("ss_full")
        ss_read = sem("ss_read")
        yo_done = sem("yo_done")
        v_step = sem("v_step")
        stored = sem("stored")
        block = ctx.enter_context(nc.Block())
        w_view = a["w_in"].rearrange("(k p) n -> p k n", p=P)
        width = lambda t: (min(t, NK - 1) + 1) * P

        @block.sync
        def _(sp):
            ext = a["ext_dram"]
            sp.dma_start(bias[:], bass.AP(ext.tensor, P - 1, [[2 * PAIRS * EXT - 1, P], [EXT, 2 * PAIRS], [1, BAND]])
                         ).then_inc(bias_loaded, 16)
            sp.dma_start(norm_g[:], a["attn_norm_g"]).then_inc(bias_loaded, 16)
            sp.sem_inc(acc_full, ACCS)
            sp.sem_inc(stored, 16)
            with sp.Fori(0, PAIRS) as p:
                sp.wait_ge(acc_full, p * ACCS + ACCS)
                sp.sem_inc(w_turn, 1)
                for i, col in enumerate((COL_Q, COL_K, COL_V)):
                    sp.dma_start(w[i][:], w_view[:, :, bass.ds(p * P + col, P)]).then_inc(w_loaded, 16)
                sp.wait_ge(yo_done, p + 1)
                sp.sem_inc(w_turn, 1)
                sp.dma_start(a["yT_dram"][bass.ds(p + KS, 1), :, :].rearrange("a p t -> p (a t)"), yo[:]
                             ).then_inc(stored, 16)
            sp.wait_ge(stored, 16 + 16 * PAIRS)

        @block.gpsimd
        def _(pool):
            pool.wait_ge(bias_loaded, 32)
            pool.memset(bias[0:CHUNK, :, BAND - CHUNK:BAND], NEG).then_inc(bias_ready, 1)
            pool.memset(bias[CHUNK:P, :, 0:CHUNK], NEG).then_inc(bias_ready, 1)

        @block.tensor
        def _(pe):
            with pe.Fori(0, PAIRS) as p:
                pe.wait_ge(w_loaded, p * 48 + 48)
                pe.wait_ge(biased, p * UNITS + 2)
                for n in range(ACCS):
                    pe.wait_ge(acc_free, p * ACCS + (n + 1))
                    bank = scores[n % 2]
                    i, q = n // QT, n % QT
                    if i < 2:
                        for k in range(KD):
                            mm = pe.matmul(bank[:, 0:512], w[i][:, k, :], s.hT[:, k, q * 512:(q + 1) * 512],
                                           start=(k == 0), stop=(k == KD - 1))
                    else:
                        for t in range(4 * q, 4 * q + 4):
                            for k in range(KD):
                                mm = pe.matmul(bank[:, (t % 4) * P:(t % 4 + 1) * P], s.hT[:, k, t * P:(t + 1) * P],
                                               w[i][:, k, :], start=(k == 0), stop=(k == KD - 1))
                    mm.then_inc(acc_full, 1)
                pe.wait_ge(acc_free, p * ACCS + (ACCS + 2))

                def attend_scores(n):
                    t, hh = n // 2, n % 2
                    d = slice(hh * HD, hh * HD + HD)
                    k0 = max(0, t - NK + 1) * P
                    pe.wait_ge(biased, p * UNITS + (n + 1))
                    for c0 in range(0, width(t), 512):
                        c1 = min(c0 + 512, width(t))
                        mm = pe.matmul(scores[n % 2][:, c0:c1], q_T[d, t * P:(t + 1) * P], k_T[d, k0 + c0:k0 + c1],
                                       start=True, stop=True)
                    mm.then_inc(s_full, 1)

                def turn(n):
                    pe.wait_ge(probs_done, p * UNITS + (n + 1))
                    pe.wait_ge(pt_done, p * UNITS + (n + 1))
                    if n == 0:
                        pe.wait_ge(ss_read, p + 1)
                    for j in range(width(n // 2) // P):
                        mm = pe.transpose(turned_ps[:, j * P:(j + 1) * P], pb[n % 3][:, j * P:(j + 1) * P], s.ident[:])
                    mm.then_inc(turned, 1)

                def weigh(n):
                    t, hh = n // 2, n % 2
                    nk = width(t) // P
                    pe.wait_ge(pt_done, p * UNITS + (n + 2))
                    if hh == 0:
                        pe.wait_ge(out_read, p * NT + (t + 1))
                    for j in range(nk):
                        mm = pe.matmul(out_ps[t % 2][hh * HD:hh * HD + HD, 0:P],
                                       v_r[:, t - nk + 1 + j, hh * HD:hh * HD + HD], pt[n % 2][:, j * P:(j + 1) * P],
                                       start=(j == 0), stop=(j == nk - 1))
                    mm.then_inc(out_full, 1)

                for n in range(UNITS + 3):
                    if n < UNITS:
                        attend_scores(n)
                    if 2 <= n < UNITS + 2:
                        turn(n - 2)
                    if n >= 3:
                        weigh(n - 3)
                pe.wait_ge(sq_done, p + 1)
                pe.wait_ge(pt_done, p * UNITS + (UNITS + 1))
                for t in range(NT):
                    mm = pe.matmul(turned_ps[:, t:t + 1], sq[:, t * P:(t + 1) * P], s.ones[:, 0:1],
                                   start=True, stop=True)
                mm.then_inc(ss_full, 1)

        @block.scalar
        def _(act):
            act.sem_inc(acc_free, 2)
            act.sem_inc(pt_done, 1)
            with act.Fori(0, PAIRS) as p:
                for n in range(ACCS):
                    i, q = n // QT, n % QT
                    cols = slice(q * 512, (q + 1) * 512)
                    act.wait_ge(acc_full, p * ACCS + (ACCS + n + 1))
                    if i == 0:
                        act.activation(q_T[:, cols], scores[n % 2][:, 0:512], ACT.Copy, scale=HD ** -0.5
                                       ).then_inc(acc_free, 1)
                    elif i == 1:
                        act.activation(k_T[:, cols], scores[n % 2][:, 0:512], ACT.Copy).then_inc(acc_free, 1)
                    else:
                        act.activation(v_r[:, 4 * q:4 * q + 4, :], scores[n % 2][:, 0:512].rearrange("p (t d) -> p t d", d=P),
                                       ACT.Copy).then_inc(acc_free, 1)
                for n in range(UNITS + 2):
                    if n >= 2:
                        u = n - 2
                        act.wait_ge(turned, p * UNITS + (u + 1))
                        if u >= 2:
                            act.wait_ge(out_full, p * UNITS + (u - 1))
                        act.activation(pt[u % 2][:, 0:width(u // 2)], turned_ps[:, 0:width(u // 2)], ACT.Copy
                                       ).then_inc(pt_done, 1)
                    if n < UNITS:
                        act.wait_ge(max_done, p * UNITS + (n + 1))
                        v = pb[n % 3][:, 0:width(n // 2)]
                        act.activation(v, v, ACT.Exp, bias=nmax[n % 3][:], accum_out=rsum[n % 3][:]).then_inc(exp_done, 1)
                act.wait_ge(out_read, p * NT + (NT + 2))
                act.activation(sq[:], o_T[:], ACT.Square).then_inc(sq_done, 1)

        @block.vector
        def _(dve):
            dve.sem_inc(biased, 2)
            dve.sem_inc(out_read, 2)
            dve.sem_inc(ss_read, 1)
            dve.wait_ge(bias_ready, 2)
            STEPS = UNITS + 1
            with dve.Fori(0, PAIRS) as p:
                link = Chain(dve, v_step)
                link.base = p * STEPS
                for n in range(UNITS + 4):
                    if n < UNITS:
                        t, hh = n // 2, n % 2
                        wd = width(t)
                        dve.wait_ge(s_full, p * UNITS + (n + 1))
                        if n >= 3:
                            dve.wait_ge(turned, p * UNITS + (n - 2))
                        b = bias[:, bass.ds(p * 2 + hh, 1), BAND - wd:BAND].rearrange("p a k -> p (a k)")
                        dve.tensor_tensor(pb[n % 3][:, 0:wd], scores[n % 2][:, 0:wd], b, ALU.add).then_inc(biased, 1)
                        dve.wait_ge(biased, p * UNITS + (n + 3))
                        dve.tensor_reduce(nmax[n % 3][:], pb[n % 3][:, 0:wd], AX.X, ALU.max, negate=True
                                          ).then_inc(max_done, 1)
                    if 1 <= n <= UNITS:
                        u = n - 1
                        dve.wait_ge(exp_done, p * UNITS + (u + 1))
                        link(dve.reciprocal(rinv[u % 3][:], rsum[u % 3][:]))
                        v = pb[u % 3][:, 0:width(u // 2)]
                        dve.tensor_scalar(v, v, rinv[u % 3][:], None, ALU.mult).then_inc(probs_done, 1)
                    if n >= 5 and n % 2 == 1:
                        t = (n - 5) // 2
                        dve.wait_ge(out_full, p * UNITS + (2 * t + 2))
                        if t == 0:
                            dve.wait_ge(ss_read, p + 1)
                        dve.tensor_copy(o_T[:, t * P:(t + 1) * P], out_ps[t % 2][:, 0:P]).then_inc(out_read, 1)
                dve.wait_ge(out_read, p * NT + (NT + 2))
                dve.wait_ge(stored, p * 16 + 16)
                dve.tensor_scalar(yo[:], o_T[:], norm_g[:, bass.ds(p, 1)], None, ALU.mult).then_inc(yo_done, 1)
                dve.wait_ge(ss_full, p + 1)
                link(dve.tensor_tensor(s.norm_sum[:, 1, :], s.norm_sum[:, 1, :], turned_ps[:, 0:NT], ALU.add))
                dve.nop().then_inc(ss_read, 1)
                assert link.n == STEPS


def mix(nc, a, s):
    with ExitStack() as ctx:
        sb = lambda n, sh, dt=F32: ctx.enter_context(nc.sbuf_tensor("m_" + n, sh, dt))
        sem = lambda n: ctx.enter_context(nc.semaphore("m_" + n))
        ps = [ctx.enter_context(nc.psum_tensor(f"m_ps{i}", [P, 512], F32)) for i in range(7)]
        NR = NG + NE
        w_out = sb("w_out", [P, KM, D])
        w_r = sb("w_r", [P, KD, NR])
        b_r = sb("b_r", [P, NR])
        gate = sb("gate", [P, D])
        nstd = sb("nstd", [P, 2, NT])
        nrstd = sb("nrstd", [P, 2, NT])
        y_T = [sb(f"y_T{i}", [P, KM, P]) for i in range(2)]
        xt = [sb(f"xt{i}", [P, D]) for i in range(2)]
        x1 = [sb(f"x1{i}", [P, D]) for i in range(2)]
        xn = [sb(f"xn{i}", [P, D]) for i in range(2)]
        junk = sb("junk", [P, D])
        mean_sq = [sb(f"mean_sq{i}", [P, 1]) for i in range(2)]
        std = [sb(f"std{i}", [P, 1]) for i in range(2)]
        rstd = [sb(f"rstd{i}", [P, 1]) for i in range(2)]
        h_T = [sb(f"h_T{i}", [P, KD, P]) for i in range(2)]

        w_loaded = [sem("w_loaded0"), sem("w_loaded1")]
        small_loaded = sem("small_loaded")
        tile_loaded = [sem("tile_loaded0"), sem("tile_loaded1")]
        norm_std = sem("norm_std")
        v_step = sem("v_step")
        out_full = sem("out_full")
        y_free = sem("y_free")
        out_read = sem("out_read")
        x1_done = sem("x1_done")
        a_step = sem("a_step")
        std_done = sem("std_done")
        rstd_done = sem("rstd_done")
        xn_done = sem("xn_done")
        stored = [sem("stored0"), sem("stored1")]
        turned = sem("turned")
        h_done = sem("h_done")
        r_full = sem("r_full")
        r_read = sem("r_read")
        block = ctx.enter_context(nc.Block())

        @block.sync
        def _(sp):
            sp.sem_inc(out_full, 4)
            wv = a["w_out"].rearrange("(k p) n -> p k n", p=P)
            sp.dma_start(w_out[:, 0:KS, :], wv[:, 0:KS, :]).then_inc(w_loaded[0], 16)
            sp.dma_start(w_out[:, KS:KM, :], wv[:, KS:KM, :]).then_inc(w_loaded[1], 16)
            sp.dma_start(w_r[:], a["w_router"]).then_inc(small_loaded, 16)
            sp.dma_start(b_r[:], rows(a["b_router"])).then_inc(small_loaded, 16)
            sp.dma_start(gate[:], rows(a["gates_dram"][:, 0:D])).then_inc(small_loaded, 16)
            with sp.Fori(0, NT // 2) as i:
                for u in range(2):
                    row = sp.snap(i * (2 * P) + u * P, min_val=0, max_val=T - P)
                    sp.wait_ge(out_full, i * 4 + (2 * u + 2))
                    sp.sem_inc(y_free, 1)
                    sp.wait_ge(x1_done, i * 2 + (u + 1))
                    sp.dma_start(y_T[u][:], a["yT_dram"].rearrange("k p t -> p k t")[:, :, bass.ds(row, P)]
                                 ).then_inc(tile_loaded[u], 16)
                    sp.dma_start(xt[u][:], a["x"][bass.ds(row, P), :]).then_inc(tile_loaded[u], 16)

        @block.tensor
        def _(pe):
            pe.wait_ge(small_loaded, 48)

            def project(b, o, u):
                pe.wait_ge(tile_loaded[u], b * 16 + (32 * ((o - u) // 2) + 32))
                for half in range(2):
                    cols = slice(half * 512, (half + 1) * 512)
                    pe.wait_ge(out_read, b * 2 + (2 * o + half + 1))
                    if half == 0:
                        pe.wait_ge(w_loaded[0], 16)
                    for k in range(KS):
                        pe.matmul(ps[half][:], y_T[u][:, k, :], w_out[:, k, cols], start=(k == 0), stop=(k == KS - 1))
                    if half == 0:
                        pe.wait_ge(w_loaded[1], 16)
                    for k in range(KS, KM):
                        mm = pe.matmul(ps[2 + half][:], y_T[u][:, k, :], w_out[:, k, cols],
                                       start=(k == KS), stop=(k == KM - 1))
                    mm.then_inc(out_full, 1)

            def turn(b, o, u):
                pe.wait_ge(xn_done, b + (o + 1))
                pe.wait_ge(h_done, b + (o + 1))
                for k in range(KD):
                    mm = pe.transpose(ps[4 + k // 4][:, (k % 4) * P:(k % 4 + 1) * P], xn[u][:, k * P:(k + 1) * P], s.ident[:])
                mm.then_inc(turned, 1)

            def router(b, o, u):
                pe.wait_ge(h_done, b + (o + 2))
                pe.wait_ge(r_read, b + (o + 1))
                for k in range(KD):
                    mm = pe.matmul(ps[6][:, 0:NR], h_T[u][:, k, :], w_r[:, k, :], start=(k == 0), stop=(k == KD - 1))
                mm.then_inc(r_full, 1)

            pipeline(pe, project, turn, router)

        @block.scalar
        def _(act):
            act.sem_inc(stored[0], 32)
            act.sem_inc(stored[1], 32)
            act.activation(nstd[:, 0, :], s.norm_sum[:, 0, :], ACT.Sqrt, scale=1.0 / D_SSD, bias=s.eps[:]
                           ).then_inc(norm_std, 1)
            act.activation(nstd[:, 1, :], s.norm_sum[:, 1, :], ACT.Sqrt, scale=1.0 / D_ATT, bias=s.eps[:]
                           ).then_inc(norm_std, 1)
            with act.Fori(0, NT // 2) as i:
                for u in range(2):
                    j = i * 2
                    row = act.snap(i * (2 * P) + u * P, min_val=0, max_val=T - P)
                    act.wait_ge(x1_done, j + (u + 3))
                    act.dma_start(a["x1_dram"][bass.ds(row, P), :], x1[u][:]).then_inc(stored[u], 16)
                    act.wait_ge(a_step, j + (u + 1))
                    act.activation(junk[:], x1[u][:], ACT.Square, scale=D ** -0.5, accum_out=mean_sq[u][:]
                                   ).then_inc(a_step, 1)
                    act.wait_ge(a_step, j + (u + 2))
                    act.activation(std[u][:], mean_sq[u][:], ACT.Sqrt, bias=s.eps[:]).then_inc(std_done, 1)
                    act.wait_ge(rstd_done, j + (u + 1))
                    act.wait_ge(turned, j + (u + 1))
                    act.wait_ge(stored[u], i * 32 + 16)
                    act.activation(xn[u][:], x1[u][:], ACT.Copy, scale=rstd[u][:]).then_inc(xn_done, 1)
                    act.wait_ge(xn_done, j + (u + 1))
                    act.dma_start(a["xn_dram"][bass.ds(row, P), :], xn[u][:]).then_inc(stored[u], 16)
            act.wait_ge(stored[0], 32 + 16 * NT)
            act.wait_ge(stored[1], 32 + 16 * NT)

        @block.vector
        def _(dve):
            dve.sem_inc(out_read, 2)
            dve.sem_inc(x1_done, 2)
            dve.sem_inc(h_done, 1)
            dve.sem_inc(r_read, 1)
            dve.sem_inc(turned, 2)
            dve.sem_inc(a_step, 1)
            dve.wait_ge(norm_std, 2)
            dve.reciprocal(nrstd[:], nstd[:]).then_inc(norm_std, 1)
            dve.wait_ge(norm_std, 3)
            dve.wait_ge(small_loaded, 48)

            def combine(b, o, u):
                dve.wait_ge(stored[u], b * 16 + (32 + 32 * ((o - u) // 2)))
                dve.wait_ge(tile_loaded[u], b * 16 + (32 * ((o - u) // 2) + 32))
                col = bass.ds(b + o, 1) if not isinstance(b, int) else slice(b + o, b + o + 1)
                for half in range(2):
                    cols = slice(half * 512, (half + 1) * 512)
                    out = x1[u][:, cols]
                    dve.wait_ge(out_full, b * 2 + (2 * o + half + 5))
                    base = (b + o) * 6 + (3 * half + 1)
                    dve.tensor_scalar(out, ps[half][:], nrstd[:, 0, col], None, ALU.mult).then_inc(v_step, 1)
                    dve.wait_ge(v_step, base)
                    dve.scalar_tensor_tensor(out, ps[2 + half][:], nrstd[:, 1, col], out, ALU.mult, ALU.add
                                             ).then_inc(out_read, 1)
                    dve.wait_ge(out_read, b * 2 + (2 * o + half + 3))
                    dve.tensor_tensor(out, out, gate[:, cols], ALU.mult).then_inc(v_step, 1)
                    dve.wait_ge(v_step, base + 1)
                    ins = dve.tensor_tensor(out, out, xt[u][:, cols], ALU.add)
                    if half == 0:
                        ins.then_inc(v_step, 1)
                    else:
                        ins.then_inc(x1_done, 1)
                dve.sem_inc(v_step, 1)
                dve.wait_ge(std_done, b + (o + 1))
                dve.reciprocal(rstd[u][:], std[u][:]).then_inc(rstd_done, 1)

            def shift(b, o, u):
                dve.wait_ge(turned, b + (o + 3))
                dve.wait_ge(r_full, b + (o + 1))
                for k in range(KD):
                    ins = dve.tensor_scalar(h_T[u][:, k, :], ps[4 + k // 4][:, (k % 4) * P:(k % 4 + 1) * P],
                                            s.scale_col[:, 1, k:k + 1], s.shift_col[:, 1, k:k + 1], ALU.mult, ALU.add)
                ins.then_inc(h_done, 1)

            def logits(b, o, u):
                dve.wait_ge(r_full, b + (o + 3))
                col = bass.ds(b + o, 1) if not isinstance(b, int) else slice(b + o, b + o + 1)
                dve.tensor_tensor(s.logits[:, col, :].rearrange("p a n -> p (a n)"), ps[6][:, 0:NR], b_r[:], ALU.add
                                  ).then_inc(r_read, 1)

            dve.sem_inc(r_full, 2)
            pipeline(dve, combine, shift, logits)


def pipeline(eng, first, second, third):
    first(0, 0, 0)
    first(0, 1, 1)
    second(0, 0, 0)
    with eng.Fori(0, NT // 2 - 1) as i:
        b = i * 2
        for u in range(2):
            first(b, 2 + u, u)
            second(b, 1 + u, 1 - u)
            third(b, u, u)
    second(0, NT - 1, 1)
    third(0, NT - 2, 0)
    third(0, NT - 1, 1)


def route(nc, a, s):
    with ExitStack() as ctx:
        sb = lambda n, sh, dt=F32: ctx.enter_context(nc.sbuf_tensor("r_" + n, sh, dt))
        sem = lambda n: ctx.enter_context(nc.semaphore("r_" + n))
        rank_ps = ctx.enter_context(nc.psum_tensor("r_rank", [P, NT, NE], F32))
        count_ps = ctx.enter_context(nc.psum_tensor("r_count", [P, 512], F32))
        gmax = sb("gmax", [P, NT])
        gd = sb("gd", [P, NT, NG])
        gsum = sb("gsum", [P, NT])
        w4 = sb("w4", [P, NT, NG])
        rev4 = sb("rev4", [P, NG])
        rev32 = sb("rev32", [P, NE])
        em = sb("em", [P, NT, NE])
        w32 = sb("w32", [P, NT, NE])
        pick = [sb(f"pick{i}", [P, NT, NE]) for i in range(2)]
        top = [sb(f"top{i}", [P, NT]) for i in range(2)]
        best = sb("best", [P, NT])
        ex = sb("ex", [P, NT])
        den = sb("den", [P, NT])
        both = sb("both", [P, NT, NE])
        before = sb("before", [P, NT + 1, NE])
        counts_i = sb("counts_i", [P, NE], I32)
        blocks = sb("blocks", [P, NE])
        ends = sb("ends", [P, NE])
        offs = sb("offs", [P, NE])
        slot = sb("slot", [P, NT, NE])
        iota_b = sb("iota_b", [P, BLOCKS])
        cmp = sb("cmp", [P, BLOCKS, NE])
        blk = sb("blk", [P, BLOCKS])
        third = sb("third", [P, BLOCKS], I32)
        third_f = sb("third_f", [P, BLOCKS])
        pairs_i = sb("pairs_i", [P, 1], I32)
        dest_f = sb("dest_f", [P, 2, NT])
        low = sb("low", [P, 2, NT], I32)
        high = sb("high", [P, 2, NT], I32)
        where = sb("where", [P, 2, NT], I32)
        row_id = sb("row_id", [P, NT], I32)
        zeros = sb("zeros", [P, BLOCKS], I32)

        made = sem("made")
        v_step = sem("v_step")
        gd_ready = sem("gd_ready")
        ge_ready = sem("ge_ready")
        diff_ready = sem("diff_ready")
        ex_ready = sem("ex_ready")
        both_ready = sem("both_ready")
        ranked = sem("ranked")
        where_ready = sem("where_ready")
        cleared = sem("cleared")
        scattered = sem("scattered")
        slots_loaded = sem("slots_loaded")
        block = ctx.enter_context(nc.Block())

        @block.gpsimd
        def _(pool):
            pool.memset(zeros[:], 0).then_inc(made, 1)
            pool.iota(rev4[:], [[-1, NG]], base=NG, channel_multiplier=0, allow_small_or_imprecise_dtypes=True
                      ).then_inc(made, 1)
            pool.iota(rev32[:], [[-1, NE]], base=NE, channel_multiplier=0, allow_small_or_imprecise_dtypes=True
                      ).then_inc(made, 1)
            pool.iota(iota_b[:], [[1, BLOCKS]], base=0, channel_multiplier=0, allow_small_or_imprecise_dtypes=True
                      ).then_inc(made, 1)
            pool.iota(row_id[:], [[P, NT]], base=0, channel_multiplier=1).then_inc(made, 1)
            pool.wait_ge(made, 5)
            pool.dma_start(a["slot_dram"].rearrange("(p b) o -> p (b o)", p=P), zeros[:]).then_inc(cleared, 16)
            pool.wait_ge(cleared, 16)
            pool.wait_ge(where_ready, 1)
            for t in range(NT):
                for k in range(2):
                    pool.indirect_dma_start(
                        out=a["slot_dram"], out_offset=bass.IndirectOffsetOnAxis(ap=where[:, k, t:t + 1].bitcast(U32), axis=0),
                        in_=row_id[:, t:t + 1], in_offset=None).then_inc(scattered, 16)
            pool.wait_ge(scattered, 16 * 2 * NT)
            pool.dma_start(s.slots[:], a["slot_dram"].rearrange("(p b) o -> p (b o)", p=P)).then_inc(slots_loaded, 16)
            pool.wait_ge(slots_loaded, 16)

        @block.tensor
        def _(pe):
            pe.wait_ge(both_ready, 1)
            pe.matmul(rank_ps[:], s.tri[:], both[:], start=True, stop=False)
            pe.matmul(rank_ps[:], s.ones[:], before[:, 0:NT, :], start=False, stop=True)
            mm = pe.matmul(count_ps[:, 0:NE], s.ones[:], before[:, NT, :], start=True, stop=True)
            mm.then_inc(ranked, 1)

        @block.scalar
        def _(act):
            act.wait_ge(gd_ready, 1)
            act.activation(gd[:], gd[:], ACT.Exp).then_inc(ge_ready, 1)
            act.wait_ge(diff_ready, 1)
            act.activation(ex[:], ex[:], ACT.Exp).then_inc(ex_ready, 1)

        @block.vector
        def _(dve):
            link = Chain(dve, v_step)
            dve.wait_ge(made, 5)
            lg = s.logits[:, :, 0:NG]
            le = s.logits[:, :, NG:NG + NE]
            wide = [P, NT, NE]
            link(dve.memset(before[:, 0, :], 0.0))
            link(dve.tensor_reduce(gmax[:], lg, AX.X, ALU.max))
            link(dve.tensor_tensor(w4[:], lg, bc(gmax[:], 2, [P, NT, NG]), ALU.is_equal))
            link(dve.tensor_tensor(w4[:], w4[:], bc(rev4[:], 1, [P, NT, NG]), ALU.mult))
            link(dve.tensor_reduce(best[:], w4[:], AX.X, ALU.max))
            dve.tensor_tensor(gd[:], lg, bc(gmax[:], 2, [P, NT, NG]), ALU.subtract).then_inc(gd_ready, 1)
            link(dve.tensor_tensor(w4[:], bc(rev4[:], 1, [P, NT, NG]), bc(best[:], 2, [P, NT, NG]), ALU.is_equal))
            link(dve.tensor_scalar(w4[:], w4[:], -1.0, -NEG, ALU.add, ALU.mult))
            g4 = lambda v: v.rearrange("p t (g e) -> p t g e", e=PER_G)
            link(dve.tensor_tensor(g4(em[:]), g4(le), bc(w4[:], 3, [P, NT, NG, PER_G]), ALU.add))
            for i in range(2):
                link(dve.tensor_reduce(top[i][:], em[:], AX.X, ALU.max))
                link(dve.tensor_tensor(w32[:], em[:], bc(top[i][:], 2, wide), ALU.is_equal))
                link(dve.tensor_tensor(w32[:], w32[:], bc(rev32[:], 1, wide), ALU.mult))
                link(dve.tensor_reduce(best[:], w32[:], AX.X, ALU.max))
                link(dve.tensor_tensor(pick[i][:], bc(rev32[:], 1, wide), bc(best[:], 2, wide), ALU.is_equal))
                if i == 0:
                    link(dve.scalar_tensor_tensor(em[:], pick[0][:], 2 * NEG, em[:], ALU.mult, ALU.add))
            dve.tensor_tensor(ex[:], top[1][:], top[0][:], ALU.subtract).then_inc(diff_ready, 1)
            link(dve.tensor_tensor(both[:], pick[0][:], pick[1][:], ALU.add))
            for t in range(NT):
                ins = dve.tensor_tensor(before[:, t + 1, :], before[:, t, :], both[:, t, :], ALU.add)
                if t < NT - 1:
                    link(ins)
                else:
                    ins.then_inc(both_ready, 1)
            dve.wait_ge(ge_ready, 1)
            link(dve.tensor_reduce(gsum[:], gd[:], AX.X, ALU.add))
            dve.wait_ge(ex_ready, 1)
            link(dve.tensor_scalar(den[:], ex[:], 1.0, None, ALU.add))
            link(dve.tensor_tensor(den[:], den[:], gsum[:], ALU.mult))
            link(dve.reciprocal(s.gates[:, 0, :], den[:]))
            link(dve.tensor_tensor(s.gates[:, 1, :], s.gates[:, 0, :], ex[:], ALU.mult))
            dve.wait_ge(ranked, 1)
            link(dve.tensor_scalar(counts_i[:], count_ps[:, 0:NE], float(P - 1), None, ALU.add))
            link(dve.tensor_scalar(counts_i[:], counts_i[:], P.bit_length() - 1, None, ALU.arith_shift_right))
            link(dve.tensor_copy(blocks[:], counts_i[:]))
            link(dve.tensor_tensor_scan(ends[:], s.ones[:, 0:NE], blocks[:], 0.0, ALU.mult, ALU.add))
            link(dve.tensor_tensor(offs[:], ends[:], blocks[:], ALU.subtract))
            link(dve.tensor_scalar(offs[:], offs[:], float(P), -1.0, ALU.mult, ALU.add))
            link(dve.tensor_tensor(slot[:], rank_ps[:], bc(offs[:], 1, wide), ALU.add))
            for i in range(2):
                link(dve.tensor_tensor(w32[:], slot[:], pick[i][:], ALU.mult))
                link(dve.tensor_reduce(dest_f[:, i, :], w32[:], AX.X, ALU.add))
            link(dve.tensor_copy(s.dest[:], dest_f[:]))
            link(dve.tensor_scalar(low[:], s.dest[:], P - 1, BLOCKS.bit_length() - 1, ALU.bitwise_and,
                                   ALU.logical_shift_left))
            link(dve.tensor_scalar(high[:], s.dest[:], P.bit_length() - 1, None, ALU.logical_shift_right))
            dve.tensor_tensor(where[:], low[:], high[:], ALU.bitwise_or).then_inc(where_ready, 1)
            link(dve.tensor_tensor(cmp[:], bc(ends[:], 1, [P, BLOCKS, NE]), bc(iota_b[:], 2, [P, BLOCKS, NE]), ALU.is_le))
            link(dve.tensor_reduce(blk[:], cmp[:], AX.X, ALU.add))
            link(dve.tensor_scalar(s.block_e[:], blk[:], float(NE - 1), None, ALU.min))
            link(dve.tensor_scalar(s.w_need[:], s.block_e[:], 48.0, 96.0, ALU.mult, ALU.add))
            link(dve.tensor_scalar(third[:], blk[:], float(NE - 1), 43.0, ALU.min, ALU.mult))
            link(dve.tensor_scalar(third[:], third[:], 7, None, ALU.logical_shift_right))
            link(dve.tensor_scalar(third_f[:], third[:], float(-W_BUFS), None, ALU.mult))
            link(dve.tensor_scalar(blk[:], blk[:], float(NE - 1), None, ALU.min))
            link(dve.tensor_tensor(s.w_sel[:], blk[:], third_f[:], ALU.add))
            link(dve.memset(s.free_at[:, 0:W_BUFS], 0))
            link(dve.tensor_copy(s.free_at[:, W_BUFS:NE], ends[:, 0:NE - W_BUFS]))
            link(dve.tensor_scalar(pairs_i[:], ends[:, NE - 1:NE], 1.0, None, ALU.add))
            link(dve.tensor_scalar(pairs_i[:], pairs_i[:], 1, None, ALU.logical_shift_right))
            link(dve.tensor_copy(s.pairs[:, 0:1], pairs_i[:]))
            link(dve.tensor_scalar(s.pairs[:, 1:2], pairs_i[:], -1.0, None, ALU.add))
            link(dve.tensor_scalar(s.pairs[:, 2:3], pairs_i[:], -32.0, float(16 * BLOCKS + 16), ALU.mult, ALU.add))


def experts(nc, a, s):
    with ExitStack() as ctx:
        sb = lambda n, sh, dt=F32: ctx.enter_context(nc.sbuf_tensor("e_" + n, sh, dt))
        sem = lambda n: ctx.enter_context(nc.semaphore("e_" + n))
        ps = [ctx.enter_context(nc.psum_tensor(f"e_ps{i}", [P, 512], F32)) for i in range(8)]
        w1 = sb("w1", [P, W_BUFS, KD, DE])
        w3 = sb("w3", [P, W_BUFS, KD, DE])
        w2 = sb("w2", [P, W_BUFS, KE, D])
        zeros = sb("zeros", [P, D])
        idx = [sb(f"idx{i}", [P, 1], I32) for i in range(2)]
        xg = [sb(f"xg{i}", [P, D]) for i in range(2)]
        x_T = [sb(f"x_T{i}", [P, KD, P]) for i in range(2)]
        up = [sb(f"up{i}", [P, DE]) for i in range(2)]
        up_T = [sb(f"up_T{i}", [P, KE, P]) for i in range(2)]
        yb = [sb(f"yb{i}", [P, D]) for i in range(2)]

        w_loaded = sem("w_loaded")
        idx_ready = sem("idx_ready")
        gathered = [sem("gathered0"), sem("gathered1")]
        x_turned = sem("x_turned")
        x_shifted = sem("x_shifted")
        h1_full = sem("h1_full")
        h3_full = sem("h3_full")
        silu_done = sem("silu_done")
        up_done = sem("up_done")
        up_turned = sem("up_turned")
        up_copied = sem("up_copied")
        y_full = sem("y_full")
        y_copied = sem("y_copied")
        y_copied2 = sem("y_copied2")
        stored = [sem("stored0"), sem("stored1")]
        turn = sem("turn")
        w_turn = sem("w_turn")
        zeroed = sem("zeroed")
        cleared = sem("cleared")
        all_stored = sem("all_stored")
        block = ctx.enter_context(nc.Block())
        HALF = BLOCKS // 2

        def used_pairs(eng):
            return eng.value_load(s.pairs[0:1, 0:1], min_val=T // P, max_val=HALF)

        def last_pair(eng):
            return eng.value_load(s.pairs[0:1, 1:2], min_val=T // P - 1, max_val=HALF - 1)

        @block.sync
        def _(sp):
            def load(i, u):
                e = bass.ds(i * W_BUFS + u, 1) if not isinstance(i, int) else slice(i * W_BUFS + u, i * W_BUFS + u + 1)
                blocks_before = sp.value_load(s.free_at[0:1, e], min_val=0, max_val=BLOCKS)
                sp.wait_ge(w_loaded, i * (48 * W_BUFS) + (48 * u + 48))
                sp.sem_inc(w_turn, 1)
                sp.wait_ge(y_full, blocks_before + 2)
                sp.sem_inc(w_turn, 1)
                for w, name in ((w1, "w1"), (w3, "w3"), (w2, "w2")):
                    sp.dma_start(w[:, u, :, :], a[name][e, :, :].rearrange("a (k p) n -> p (a k) n", p=P)
                                 ).then_inc(w_loaded, 16)

            sp.sem_inc(w_loaded, 48)
            sp.sem_inc(y_full, 2)
            with sp.Fori(0, NE // W_BUFS) as i:
                for u in range(W_BUFS):
                    load(i, u)
            for u in range(NE % W_BUFS):
                load(NE // W_BUFS, u)
            sp.sem_inc(cleared, 16)
            sp.wait_ge(zeroed, 1)
            pairs = used_pairs(sp)
            unused = sp.value_load(s.pairs[0:1, 2:3], min_val=16, max_val=32 * HALF)
            with sp.Fori(0, HALF) as i, sp.If(i >= pairs):
                for u in range(2):
                    row = sp.snap(i * (2 * P) + u * P, min_val=0, max_val=SLOTS - P)
                    sp.dma_start(a["y_dram"][bass.ds(row, P), :], zeros[:]).then_inc(cleared, 16)
            sp.wait_ge(cleared, unused)
            sp.sem_inc(w_turn, 1)
            sp.wait_ge(w_loaded, 48 * NE + 48)

        @block.gpsimd
        def _(pool):
            pool.memset(zeros[:], 0.0).then_inc(zeroed, 1)
            pairs = used_pairs(pool)
            with pool.Fori(0, HALF) as i, pool.If(i < pairs):
                for u in range(2):
                    pool.wait_ge(x_turned, i * 2 + (u + 1))
                    pool.tensor_copy(idx[u][:], s.slots[:, bass.ds(i * 2 + u, 1)]).then_inc(idx_ready, 1)
                    pool.wait_ge(idx_ready, i * 2 + (u + 1))
                    pool.sem_inc(turn, 1)
                    pool.indirect_dma_start(out=xg[u][:], out_offset=None, in_=a["xn_dram"],
                                            in_offset=bass.IndirectOffsetOnAxis(ap=idx[u][:].bitcast(U32), axis=0)
                                            ).then_inc(gathered[u], 16)

        @block.tensor
        def _(pe):
            pe.sem_inc(x_turned, 2)

            def turn_rows(b, o, u):
                pe.wait_ge(gathered[u], b * 8 + (16 * ((o - u) // 2) + 16))
                pe.wait_ge(x_shifted, b + (o + 1))
                for k in range(KD):
                    mm = pe.transpose(ps[k // 4][:, (k % 4) * P:(k % 4 + 1) * P], xg[u][:, k * P:(k + 1) * P], s.ident[:])
                mm.then_inc(x_turned, 1)

            def at(b, o):
                return slice(b + o, b + o + 1) if isinstance(b, int) else bass.ds(b + o, 1)

            def buffer(w, sel, k, cols):
                return w[:, bass.ds(sel, 1), k, cols].rearrange("p a n -> p (a n)")

            def up_products(b, o, u):
                need = pe.value_load(s.w_need[0:1, at(b, o)], min_val=96, max_val=48 * NE + 48)
                sel = pe.value_load(s.w_sel[0:1, at(b, o)], min_val=0, max_val=W_BUFS - 1)
                pe.wait_ge(x_shifted, b + (o + 2))
                pe.wait_ge(w_loaded, need)
                pe.wait_ge(silu_done, b + (o + 1))
                for k in range(KD):
                    mm = pe.matmul(ps[2][:], x_T[u][:, k, :], buffer(w1, sel, k, slice(0, DE)), start=(k == 0), stop=(k == KD - 1))
                mm.then_inc(h1_full, 1)
                pe.wait_ge(up_done, b + (o + 1))
                for k in range(KD):
                    mm = pe.matmul(ps[3][:], x_T[u][:, k, :], buffer(w3, sel, k, slice(0, DE)), start=(k == 0), stop=(k == KD - 1))
                mm.then_inc(h3_full, 1)

            def turn_up(b, o, u):
                pe.wait_ge(up_done, b + (o + 2))
                pe.wait_ge(up_copied, b + (o + 1))
                for k in range(KE):
                    mm = pe.transpose(ps[4][:, k * P:(k + 1) * P], up[u][:, k * P:(k + 1) * P], s.ident[:])
                mm.then_inc(up_turned, 1)

            def down_product(b, o, u):
                sel = pe.value_load(s.w_sel[0:1, at(b, o)], min_val=0, max_val=W_BUFS - 1)
                pe.wait_ge(up_copied, b + (o + 2))
                pe.wait_ge(y_copied, b + (o + 1))
                pe.wait_ge(y_copied2, b + (o + 1))
                for half in range(2):
                    for k in range(KE):
                        mm = pe.matmul(ps[5 + half][:], up_T[u][:, k, :], buffer(w2, sel, k, slice(half * 512, (half + 1) * 512)),
                                       start=(k == 0), stop=(k == KE - 1))
                mm.then_inc(y_full, 1)

            turn_rows(0, 0, 0)
            up_products(0, 0, 0)
            turn_rows(0, 1, 1)
            turn_up(0, 0, 0)
            last = last_pair(pe)
            with pe.Fori(0, HALF - 1) as i, pe.If(i < last):
                b = i * 2
                for v in range(2):
                    u = (1 + v) % 2
                    up_products(b, 1 + v, u)
                    turn_rows(b, 2 + v, 1 - u)
                    down_product(b, v, 1 - u)
                    turn_up(b, 1 + v, u)
            b = last * 2
            up_products(b, 1, 1)
            down_product(b, 0, 0)
            turn_up(b, 1, 1)
            down_product(b, 1, 1)

        @block.scalar
        def _(act):
            act.sem_inc(silu_done, 1)
            act.sem_inc(up_copied, 1)
            act.sem_inc(y_copied, 1)
            act.sem_inc(stored[0], 16)
            act.sem_inc(stored[1], 16)

            def silu(b, o, u):
                act.wait_ge(h1_full, b + (o + 1))
                act.wait_ge(up_turned, b + (o + 1))
                act.activation(up[u][:], ps[2][:], ACT.Silu).then_inc(silu_done, 1)

            def copy_up(b, o, u):
                act.wait_ge(up_turned, b + (o + 3))
                act.wait_ge(y_full, b + (o + 1))
                act.activation(up_T[u][:].rearrange("p k t -> p (k t)"), ps[4][:], ACT.Copy).then_inc(up_copied, 1)

            def copy_y(b, o, u):
                act.wait_ge(y_full, b + (o + 3))
                act.wait_ge(stored[u], b * 8 + (16 * ((o - u) // 2) + 16))
                act.activation(yb[u][:, 0:512], ps[5][:], ACT.Copy).then_inc(y_copied, 1)
                row = act.snap(b * P + o * P, min_val=0, max_val=SLOTS - P) if not isinstance(b, int) else o * P
                act.wait_ge(y_copied, b + (o + 2))
                act.wait_ge(y_copied2, b + (o + 2))
                act.dma_start(a["y_dram"][bass.ds(row, P), :], yb[u][:]).then_inc(stored[u], 16)

            act.sem_inc(up_turned, 2)
            silu(0, 0, 0)
            copy_up(0, 0, 0)
            last = last_pair(act)
            with act.Fori(0, HALF - 1) as i, act.If(i < last):
                b = i * 2
                for v in range(2):
                    u = (1 + v) % 2
                    silu(b, 1 + v, u)
                    copy_y(b, v, 1 - u)
                    copy_up(b, 1 + v, u)
            b = last * 2
            silu(b, 1, 1)
            copy_y(b, 0, 0)
            copy_up(b, 1, 1)
            copy_y(b, 1, 1)
            act.wait_ge(stored[0], last * 16 + 32)
            act.wait_ge(stored[1], last * 16 + 32)
            act.sem_inc(all_stored, 1)

        @block.vector
        def _(dve):
            dve.sem_inc(x_shifted, 1)
            dve.sem_inc(up_done, 1)
            dve.sem_inc(h3_full, 2)
            dve.sem_inc(y_copied2, 1)

            def shift(b, o, u):
                dve.wait_ge(x_turned, b + (o + 3))
                dve.wait_ge(h3_full, b + (o + 1))
                for k in range(KD):
                    ins = dve.tensor_scalar(x_T[u][:, k, :], ps[k // 4][:, (k % 4) * P:(k % 4 + 1) * P],
                                            s.scale_col[:, 1, k:k + 1], s.shift_col[:, 1, k:k + 1], ALU.mult, ALU.add)
                ins.then_inc(x_shifted, 1)

            def gate(b, o, u):
                dve.wait_ge(silu_done, b + (o + 2))
                dve.wait_ge(h3_full, b + (o + 3))
                dve.tensor_tensor(up[u][:], up[u][:], ps[3][:], ALU.mult).then_inc(up_done, 1)

            def copy_y(b, o, u):
                dve.wait_ge(y_full, b + (o + 3))
                dve.wait_ge(stored[u], b * 8 + (16 * ((o - u) // 2) + 16))
                dve.tensor_copy(yb[u][:, 512:1024], ps[6][:]).then_inc(y_copied2, 1)

            shift(0, 0, 0)
            shift(0, 1, 1)
            gate(0, 0, 0)
            last = last_pair(dve)
            with dve.Fori(0, HALF - 1) as i, dve.If(i < last):
                b = i * 2
                for v in range(2):
                    u = (1 + v) % 2
                    shift(b, 2 + v, 1 - u)
                    gate(b, 1 + v, u)
                    copy_y(b, v, 1 - u)
            b = last * 2
            gate(b, 1, 1)
            copy_y(b, 0, 0)
            copy_y(b, 1, 1)


def combine(nc, a, s):
    with ExitStack() as ctx:
        sb = lambda n, sh, dt=F32: ctx.enter_context(nc.sbuf_tensor("c_" + n, sh, dt))
        sem = lambda n: ctx.enter_context(nc.semaphore("c_" + n))
        gate = sb("gate", [P, D])
        norm_g = sb("norm_g", [P, D])
        idx = [sb(f"idx{i}", [P, 2], I32) for i in range(2)]
        x1 = [sb(f"x1{i}", [P, D]) for i in range(2)]
        y0 = [sb(f"y0{i}", [P, D]) for i in range(2)]
        y1 = [sb(f"y1{i}", [P, D]) for i in range(2)]
        junk = sb("junk", [P, D])
        o = [sb(f"o{i}", [P, D]) for i in range(2)]
        mean_sq = [sb(f"mean_sq{i}", [P, 1]) for i in range(2)]
        std = [sb(f"std{i}", [P, 1]) for i in range(2)]
        rstd = [sb(f"rstd{i}", [P, 1]) for i in range(2)]

        rows_loaded = sem("rows_loaded")
        x_loaded = [sem("x_loaded0"), sem("x_loaded1")]
        idx_ready = sem("idx_ready")
        turn = sem("turn")
        gathered = [sem("gathered0"), sem("gathered1")]
        v_step = sem("v_step")
        sum_done = sem("sum_done")
        sq_done = sem("sq_done")
        std_done = sem("std_done")
        out_done = sem("out_done")
        stored = [sem("stored0"), sem("stored1")]
        block = ctx.enter_context(nc.Block())

        @block.sync
        def _(sp):
            sp.dma_start(gate[:], rows(a["gates_dram"][:, D:2 * D])).then_inc(rows_loaded, 16)
            sp.dma_start(norm_g[:], rows(a["final_norm_g"])).then_inc(rows_loaded, 16)
            with sp.Fori(0, NT // 2) as i:
                for u in range(2):
                    row = sp.snap(i * (2 * P) + u * P, min_val=0, max_val=T - P)
                    sp.wait_ge(out_done, i * 2 + (u + 1))
                    sp.dma_start(x1[u][:], a["x1_dram"][bass.ds(row, P), :]).then_inc(x_loaded[u], 16)

        @block.gpsimd
        def _(pool):
            with pool.Fori(0, NT // 2) as i:
                for u in range(2):
                    pool.wait_ge(sum_done, i * 2 + (u + 1))
                    pool.tensor_copy(idx[u][:], s.dest[:, :, bass.ds(i * 2 + u, 1)].rearrange("p k a -> p (k a)")
                                     ).then_inc(idx_ready, 1)
                    pool.wait_ge(idx_ready, i * 2 + (u + 1))
                    pool.sem_inc(turn, 1)
                    for k, y in enumerate((y0, y1)):
                        pool.indirect_dma_start(out=y[u][:], out_offset=None, in_=a["y_dram"],
                                                in_offset=bass.IndirectOffsetOnAxis(ap=idx[u][:, k:k + 1].bitcast(U32), axis=0)
                                                ).then_inc(gathered[u], 16)

        @block.scalar
        def _(act):
            act.sem_inc(stored[0], 16)
            act.sem_inc(stored[1], 16)
            with act.Fori(0, NT // 2) as i:
                for u in range(2):
                    j = i * 2
                    act.wait_ge(sum_done, j + (u + 3))
                    act.wait_ge(sq_done, j + (u + 1))
                    act.activation(junk[:], x1[u][:], ACT.Square, scale=D ** -0.5, accum_out=mean_sq[u][:]
                                   ).then_inc(sq_done, 1)
                    act.wait_ge(sq_done, j + (u + 2))
                    act.activation(std[u][:], mean_sq[u][:], ACT.Sqrt, bias=s.eps[:]).then_inc(std_done, 1)
                    row = act.snap(i * (2 * P) + u * P, min_val=0, max_val=T - P)
                    act.wait_ge(out_done, j + (u + 3))
                    act.dma_start(a["out"][bass.ds(row, P), :], o[u][:]).then_inc(stored[u], 16)
            act.wait_ge(stored[0], 16 + 8 * NT)
            act.wait_ge(stored[1], 16 + 8 * NT)

        @block.vector
        def _(dve):
            dve.sem_inc(sum_done, 2)
            dve.sem_inc(out_done, 2)
            dve.sem_inc(sq_done, 1)
            dve.wait_ge(rows_loaded, 32)
            with dve.Fori(0, NT // 2) as i:
                link = Chain(dve, v_step)
                link.base = i * 8
                for u in range(2):
                    j = i * 2
                    dve.wait_ge(gathered[u], i * 32 + 32)
                    dve.wait_ge(x_loaded[u], i * 16 + 16)
                    t = bass.ds(j + u, 1)
                    link(dve.tensor_scalar(y0[u][:], y0[u][:], s.gates[:, 0, t], None, ALU.mult))
                    link(dve.scalar_tensor_tensor(y0[u][:], y1[u][:], s.gates[:, 1, t], y0[u][:], ALU.mult, ALU.add))
                    link(dve.tensor_tensor(y0[u][:], y0[u][:], gate[:], ALU.mult))
                    dve.tensor_tensor(x1[u][:], x1[u][:], y0[u][:], ALU.add).then_inc(sum_done, 1)
                    dve.wait_ge(std_done, j + (u + 1))
                    link(dve.reciprocal(rstd[u][:], std[u][:]))
                    dve.wait_ge(stored[u], i * 16 + 16)
                    dve.wait_ge(sum_done, j + (u + 3))
                    dve.scalar_tensor_tensor(o[u][:], x1[u][:], rstd[u][:], norm_g[:], ALU.mult, ALU.mult
                                             ).then_inc(out_done, 1)


def program(nc, a):
    with ExitStack() as ctx:
        sb = lambda n, sh, dt=F32: ctx.enter_context(nc.sbuf_tensor("s_" + n, sh, dt))

        class s:
            ident = sb("ident", [P, P])
            tri = sb("tri", [P, P])
            ones = sb("ones", [P, P])
            eps = sb("eps", [P, 1])
            scale_col = sb("scale_col", [P, 2, KD])
            shift_col = sb("shift_col", [P, 2, KD])
            norm_sum = sb("norm_sum", [P, 2, NT])

        with ExitStack() as ctx2:
            sb2 = lambda n, sh, dt=F32: ctx2.enter_context(nc.sbuf_tensor("s_" + n, sh, dt))
            s.hT = sb2("hT", [P, KD, T])
            with ExitStack() as ctx3:
                sb3 = lambda n, sh, dt=F32: ctx3.enter_context(nc.sbuf_tensor("s_" + n, sh, dt))
                s.dt = sb3("dt", [P, NT * NH])
                s.dtdec = sb3("dtdec", [P, NT * NH])
                s.acc = sb3("acc", [P, NT * NH])
                prepare(nc, a, s)
                ssd(nc, a, s)
            attend(nc, a, s)
        s.logits = sb("logits", [P, NT, NG + NE])
        mix(nc, a, s)
        s.slots = sb("slots", [P, BLOCKS], I32)
        s.dest = sb("dest", [P, 2, NT], I32)
        s.gates = sb("gates", [P, 2, NT])
        s.block_e = sb("block_e", [P, BLOCKS], I32)
        s.w_need = sb("w_need", [P, BLOCKS], I32)
        s.w_sel = sb("w_sel", [P, BLOCKS], I32)
        s.free_at = sb("free_at", [P, NE], I32)
        s.pairs = sb("pairs", [P, 3], I32)
        route(nc, a, s)
        experts(nc, a, s)
        combine(nc, a, s)


def layouts(inputs):
    g = {k: np.asarray(v) for k, v in inputs.items()}
    col = lambda v, n: np.ascontiguousarray(v.reshape(n, P).T)
    conv_w, conv_b = g["conv_w"][0], g["conv_b"][0]
    w_in = g["w_in"][0]
    params = []
    for i in range(GROUPS):
        feats = [COL_X - D_SSD + i * GD + f * P for f in range(GF)]
        feats += [D_SSD + i * NSTATE, D_SSD + GROUPS * NSTATE + i * NSTATE]
        cw = [conv_w[j, f:f + P] for f in feats for j in range(CONV)]
        cb = [conv_b[f:f + P] for f in feats]
        ds = np.repeat(g["d_skip"][0][i * GH:(i + 1) * GH], HD).reshape(GF, P)
        ng = g["ssd_norm_g"][0][i * GD:(i + 1) * GD].reshape(GF, P)
        params.append(np.stack(cw + cb + list(ds) + list(ng), axis=1))
    return {
        "x": np.ascontiguousarray(g["x"].reshape(T, D)),
        "c": col(g["c"][0], KD),
        "w_ada": g["w_ada"][0],
        "b_ada": g["b_ada"].reshape(1, -1),
        "norm_mix_g": col(g["norm_mix_g"][0], KD),
        "norm_ffn_g": col(g["norm_ffn_g"][0], KD),
        "w_in": w_in,
        "w_dt": np.ascontiguousarray(w_in[:, COL_DT:COL_DT + NH].reshape(KD, P, NH).transpose(1, 0, 2)),
        "dt_bias": g["dt_bias"].reshape(1, -1),
        "a_log": g["a_log"].reshape(1, -1),
        "group_params": np.ascontiguousarray(np.stack(params)),
        "attn_norm_g": col(g["attn_norm_g"][0], PAIRS),
        "rel_rev": np.ascontiguousarray(g["rel_bias"][0][:, ::-1]),
        "w_out": g["w_out"][0],
        "w_router": np.ascontiguousarray(np.concatenate([g["w_router_group"][0], g["w_router_expert"][0]], axis=1)
                                         .reshape(KD, P, NG + NE).transpose(1, 0, 2)),
        "b_router": np.concatenate([g["b_router_group"][0], g["b_router_expert"][0]]).reshape(1, -1),
        "w1": g["w1"][0],
        "w3": g["w3"][0],
        "w2": g["w2"][0],
        "final_norm_g": g["final_norm_g"].reshape(1, -1),
    }


SCRATCH = {
    "acc_dram": ([NH, T], F32),
    "gates_dram": ([1, 2 * D], F32),
    "ext_dram": ([P, 2 * PAIRS, EXT], F32),
    "yT_dram": ([KM, P, T], F32),
    "x1_dram": ([T, D], F32),
    "xn_dram": ([T, D], F32),
    "slot_dram": ([SLOTS, 1], I32),
    "y_dram": ([SLOTS, D], F32),
}


def kernel(**inputs):
    import concourse.bacc as bacc
    from concourse.bass_utils import run_bass_kernel_spmd

    nc = bacc.Bacc("TRN2", target_bir_lowering=False, num_devices=1)
    arrays, a = {}, {}
    for name, v in layouts(inputs).items():
        arrays[f"in_{name}"] = v
        a[name] = nc.dram_tensor(f"in_{name}", v.shape, mybir.dt.from_np(v.dtype), kind="ExternalInput").ap()
    for name, (shape, dt) in SCRATCH.items():
        a[name] = nc.dram_tensor(name, shape, dt).ap()
    a["out"] = nc.dram_tensor("out", (T, D), F32, kind="ExternalOutput").ap()
    program(nc, a)
    r = run_bass_kernel_spmd(nc, [arrays], core_ids=[0])
    return r.results[0]["out"].reshape(1, T, D)
```

```python
from contextlib import ExitStack

import numpy as np
import concourse.bass as bass
from concourse import mybir

F32 = mybir.dt.float32
F32R = mybir.dt.float32r
I32 = mybir.dt.int32
U32 = mybir.dt.uint32
ALU = mybir.AluOpType
ACT = mybir.ActivationFunctionType
AX = mybir.AxisListType

P = 128
T = 2048
NT = T // P
D = 1024
KD = D // P
CHUNK = 64
HD = 64
D_SSD = 1536
GROUPS = 4
GH = 6
NH = GROUPS * GH
GD = GH * HD
GF = GD // P
NSTATE = 128
D_ATT = 512
PAIRS = 4
CONV = 4
COL_Z = 0
COL_X = D_SSD
COL_B = 2 * D_SSD
COL_C = COL_B + GROUPS * NSTATE
COL_DT = COL_C + GROUPS * NSTATE
COL_Q = COL_DT + NH
COL_K = COL_Q + D_ATT
COL_V = COL_K + D_ATT
IN_COLS = COL_V + D_ATT
BACK = 8 * CHUNK
BAND = BACK + P
CLIP = 256
EXT = 768
MIX = 2 * D
KM = MIX // P
KS = D_SSD // P
NG = 4
NE = 32
PER_G = NE // NG
DE = 512
KE = DE // P
BLOCKS = 2 * T // P + NE
SLOTS = BLOCKS * P
W_BUFS = 3
EPS = 1e-6
PAR = 28
TILES = 11
N_CONV = 5
NEG = -1e30
QT = T // 512


class Chain:

    def __init__(self, eng, sem):
        self.eng, self.sem, self.base, self.n = eng, sem, 0, 0

    def __call__(self, ins):
        ins.then_inc(self.sem, 1)
        self.n += 1
        self.eng.wait_ge(self.sem, self.base + self.n)


def bc(ap, axis, shape):
    return ap.unsqueeze(axis).broadcast_to(shape)


def rows(ap2d):
    return bass.AP(ap2d.tensor, ap2d.offset, [[0, P]] + list(ap2d.ap)[1:])


def prepare(nc, a, s):
    with ExitStack() as ctx:
        sb = lambda n, sh, dt=F32: ctx.enter_context(nc.sbuf_tensor("p_" + n, sh, dt))
        sem = lambda n: nc.alloc_semaphore("p_" + n)
        ps = [ctx.enter_context(nc.psum_tensor(f"p_ps{i}", [P, 512], F32)) for i in range(8)]
        wa = [sb(f"wa{i}", [P, KD, 512]) for i in range(2)]
        brow = [sb(f"brow{i}", [1, 512]) for i in range(2)]
        modrow = [sb(f"modrow{i}", [P, 512]) for i in range(2)]
        modcol = sb("modcol", [P, 6, KD])
        silc = sb("silc", [P, KD])
        wsum = [sb(f"wsum{i}", [P, 512]) for i in range(2)]
        X_BUFS = 4
        xt = [sb(f"xt{i}", [P, D]) for i in range(X_BUFS)]
        junk = sb("junk", [P, D])
        h32 = [sb(f"h32{i}", [P, 4, P]) for i in range(2)]
        std = sb("std", [P, NT])
        ssq = sb("ssq", [P, NT])
        rstd = sb("rstd", [P, NT])
        gcol = sb("gcol", [P, 2, KD])
        wdt = sb("wdt", [P, KD, NH])
        wdt_hi = sb("wdt_hi", [P, KD, NH], F32R)
        wdt_lo = sb("wdt_lo", [P, KD, NH], F32R)

        ada_loaded = [sem("ada_loaded0"), sem("ada_loaded1")]
        x_loaded = [sem(f"x_loaded{i}") for i in range(X_BUFS)]
        small_loaded = sem("small_loaded")
        w_split = sem("w_split")
        dt_raw = sem("dt_raw")
        consts_made = sem("consts_made")
        pool_step = sem("pool_step")
        silc_ready = sem("silc_ready")
        ada_part = sem("ada_part")
        ada_summed = sem("ada_summed")
        ada_row = sem("ada_row")
        ada_turned = sem("ada_turned")
        ada_col = sem("ada_col")
        ssq_ready = sem("ssq_ready")
        rstd_ready = sem("rstd_ready")
        std_ready = sem("std_ready")
        xn_ready = sem("xn_ready")
        x_turned = sem("x_turned")
        h_made = sem("h_made")
        hi_done = sem("hi_done")
        lo_done = sem("lo_done")
        v_step = sem("v_step")
        gate_stored = sem("gate_stored")
        block = ctx.enter_context(nc.Block())
        wada = a["w_ada"].rearrange("(k p) n -> p k n", p=P)
        GATES = {2: 0, 5: 1}
        FIRST = 4

        def row_tiles(part, ada, first, tile):
            part(0)
            for j in range(FIRST):
                if j + 1 < FIRST:
                    part(j + 1)
                ada(j)
            first()
            for t in range(NT):
                if t % 2 == 0:
                    part(FIRST + t // 2)
                tile(t)
                if t % 2 == 1:
                    ada(FIRST + t // 2)

        @block.sync
        def _(sp):
            for j in range(14):
                if j < 12:
                    if j >= 2:
                        sp.wait_ge(ada_part, j - 1)
                    sp.dma_start(wa[j % 2][:], wada[:, :, j * 512:(j + 1) * 512]).then_inc(ada_loaded[j % 2], 16)
                    if j >= 2:
                        sp.wait_ge(ada_summed, j - 1)
                    sp.dma_start(brow[j % 2][:], a["b_ada"][:, j * 512:(j + 1) * 512]).then_inc(ada_loaded[j % 2], 16)
                if (j - 2) // 2 in GATES:
                    col = GATES[(j - 2) // 2] * D + (j % 2) * 512
                    sp.wait_ge(ada_row, j - 1)
                    sp.dma_start(a["gates_dram"][:, col:col + 512], modrow[j % 2][0:1, :]).then_inc(gate_stored, 16)
            sp.wait_ge(gate_stored, 64)

        @block.gpsimd
        def _(pool):
            pool.dma_start(gcol[:, 0, :], a["norm_mix_g"]).then_inc(small_loaded, 16)
            pool.dma_start(gcol[:, 1, :], a["norm_ffn_g"]).then_inc(small_loaded, 16)
            pool.dma_start(wdt[:], a["w_dt"]).then_inc(small_loaded, 16)
            pool.memset(s.ident[:], 0.0).then_inc(pool_step, 1)
            pool.memset(s.tri[:], 1.0).then_inc(pool_step, 1)
            pool.memset(s.ones[:], 1.0).then_inc(consts_made, 1)
            pool.memset(s.eps[:], EPS).then_inc(consts_made, 1)
            pool.wait_ge(pool_step, 2)
            pool.affine_select(out=s.ident[:], in_=s.ident[:], compare_op=ALU.not_equal, fill=1.0, base=0,
                               pattern=[[-1, P]], channel_multiplier=1).then_inc(consts_made, 1)
            pool.affine_select(out=s.tri[:], in_=s.tri[:], compare_op=ALU.is_ge, fill=0.0, base=0,
                               pattern=[[1, P]], channel_multiplier=-1).then_inc(consts_made, 1)
            pool.wait_ge(small_loaded, 48)
            pool.tensor_copy(wdt_hi[:], wdt[:]).then_inc(w_split, 1)
            pool.wait_ge(w_split, 1)
            pool.tensor_tensor(wdt_lo[:], wdt[:], wdt_hi[:].bitcast(F32), ALU.subtract).then_inc(w_split, 1)
            for t in range(NT):
                if t >= X_BUFS:
                    pool.wait_ge(x_turned, 2 * (t - X_BUFS + 1))
                pool.dma_start(xt[t % X_BUFS][:], a["x"][t * P:(t + 1) * P, :]).then_inc(x_loaded[t % X_BUFS], 16)

        @block.tensor
        def _(pe):
            pe.wait_ge(consts_made, 4)

            def turn_rows(j):
                pe.wait_ge(ada_row, j + 1)
                if j >= 1:
                    pe.wait_ge(ada_col, j)
                for q in range(4):
                    mm = pe.transpose(ps[2][:, q * P:(q + 1) * P],
                                      modrow[j % 2][:, q * P:(q + 1) * P], s.ident[:])
                mm.then_inc(ada_turned, 1)

            def ada(j):
                pe.wait_ge(ada_loaded[j % 2], 32 * (j // 2 + 1))
                pe.wait_ge(ada_part, j + 1)
                if j >= 2:
                    pe.wait_ge(ada_row, j - 1)
                pe.matmul(ps[j % 2][:], s.ones[:], wsum[j % 2][:], start=True, stop=False)
                pe.matmul(ps[j % 2][:], s.ones[0:1, :], brow[j % 2][:], start=False, stop=True).then_inc(ada_summed, 1)
                if j not in (0, FIRST):
                    turn_rows(j - 1)

            def tile(t):
                for half in range(2):
                    n = 2 * t + half
                    pe.wait_ge(xn_ready, t + 1)
                    if n >= 4:
                        pe.wait_ge(h_made, n - 3)
                    for q in range(4):
                        k = half * 4 + q
                        mm = pe.transpose(ps[4 + n % 4][:, q * P:(q + 1) * P], xt[t % X_BUFS][:, k * P:(k + 1) * P], s.ident[:])
                    mm.then_inc(x_turned, 1)
                if t >= 2:
                    steps(t - 2)

            def steps(t):
                pe.wait_ge(hi_done, 2 * t + 2)
                pe.wait_ge(lo_done, 2 * t + 2)
                if t == 0:
                    pe.wait_ge(w_split, 2)
                rows_of = slice(t * P, (t + 1) * P)
                out = ps[3][:, t * NH:(t + 1) * NH]
                for k in range(KD):
                    pe.matmul(out, s.h_hi[:, k, rows_of], wdt_hi[:, k, :], start=(k == 0), stop=False)
                    pe.matmul(out, s.h_hi[:, k, rows_of], wdt_lo[:, k, :], start=False, stop=False)
                    mm = pe.matmul(out, s.h_lo[:, k, rows_of], wdt_hi[:, k, :], start=False, stop=(k == KD - 1))
                mm.then_inc(dt_raw, 1)

            row_tiles(lambda j: None, ada, lambda: turn_rows(FIRST - 1), tile)
            steps(NT - 2)
            steps(NT - 1)
            turn_rows(11)

        @block.scalar
        def _(act):
            act.dma_start(silc[:], a["c"]).then_inc(silc_ready, 16)
            act.wait_ge(silc_ready, 16)
            act.activation(silc[:], silc[:], ACT.Silu).then_inc(silc_ready, 1)
            act.wait_ge(consts_made, 4)
            for t in range(NT + 2):
                if t < NT:
                    act.wait_ge(x_loaded[t % X_BUFS], 16 * (t // X_BUFS + 1))
                    if t >= 1:
                        act.wait_ge(ssq_ready, t)
                    act.activation(junk[:], xt[t % X_BUFS][:], ACT.Square, scale=D ** -0.5,
                                   accum_out=ssq[:, t:t + 1]).then_inc(ssq_ready, 1)
                    act.wait_ge(ssq_ready, t + 1)
                    act.activation(std[:, t:t + 1], ssq[:, t:t + 1], ACT.Sqrt, bias=s.eps[:]).then_inc(std_ready, 1)
                if 1 <= t <= NT:
                    u = t - 1
                    act.wait_ge(rstd_ready, t)
                    act.activation(xt[u % X_BUFS][:], xt[u % X_BUFS][:], ACT.Copy, scale=rstd[:, u:u + 1]).then_inc(xn_ready, 1)
                if t >= 2:
                    for n in range(2 * (t - 2), 2 * (t - 2) + 2):
                        act.wait_ge(h_made, n + 1)
                        act.activation(high_part(s, n), h32[n % 2][:], ACT.Copy).then_inc(hi_done, 1)

        @block.vector
        def _(dve):
            link = Chain(dve, v_step)
            dve.wait_ge(silc_ready, 17)

            def part(j):
                dve.wait_ge(ada_loaded[j % 2], 32 * (j // 2 + 1))
                if j >= 2:
                    dve.wait_ge(ada_summed, j - 1)
                for k in range(KD):
                    w = wa[j % 2][:, k, :]
                    if k == 0:
                        link(dve.tensor_scalar(wsum[j % 2][:], w, silc[:, k:k + 1], None, ALU.mult))
                        continue
                    ins = dve.scalar_tensor_tensor(wsum[j % 2][:], w, silc[:, k:k + 1], wsum[j % 2][:], ALU.mult, ALU.add)
                    if k < KD - 1:
                        link(ins)
                    else:
                        ins.then_inc(ada_part, 1)

            def column_of(j):
                dve.wait_ge(ada_turned, j + 1)
                dve.tensor_copy(modcol[:, j // 2, (j % 2) * 4:(j % 2) * 4 + 4],
                                ps[2][:, 0:512:P]).then_inc(ada_col, 1)

            def modulation(m, sh, sc):
                link(dve.tensor_scalar(modcol[:, sc, :], modcol[:, sc, :], 1.0, None, ALU.add))
                link(dve.tensor_tensor(s.scale_col[:, m, :], modcol[:, sc, :], gcol[:, m, :], ALU.mult))
                link(dve.tensor_copy(s.shift_col[:, m, :], modcol[:, sh, :]))

            def ada(j):
                dve.wait_ge(ada_summed, j + 1)
                if j >= 2:
                    dve.wait_ge(ada_turned, j - 1)
                if (j - 2) // 2 in GATES:
                    dve.wait_ge(gate_stored, 32 * (GATES[(j - 2) // 2] + 1))
                dve.tensor_copy(modrow[j % 2][:], ps[j % 2][:]).then_inc(ada_row, 1)
                if j not in (0, FIRST):
                    column_of(j - 1)

            def rstd_of(t):
                dve.wait_ge(std_ready, t + 1)
                dve.reciprocal(rstd[:, t:t + 1], std[:, t:t + 1]).then_inc(rstd_ready, 1)

            def low_part(n):
                dve.wait_ge(hi_done, n + 1)
                dve.tensor_tensor(low_part_of(s, n), h32[n % 2][:], high_part(s, n).bitcast(F32), ALU.subtract
                                  ).then_inc(lo_done, 1)

            def tile(t):
                if t + 2 < NT:
                    rstd_of(t + 2)
                for half in range(2):
                    n = 2 * t + half
                    dve.wait_ge(x_turned, n + 1)
                    if n >= 2:
                        dve.wait_ge(lo_done, n - 1)
                    for q in range(4):
                        k = half * 4 + q
                        mm = dve.tensor_scalar(h32[n % 2][:, q, :], ps[4 + n % 4][:, q * P:(q + 1) * P],
                                               s.scale_col[:, 0, k:k + 1], s.shift_col[:, 0, k:k + 1],
                                               ALU.mult, ALU.add)
                    mm.then_inc(h_made, 1)
                    if n >= 1:
                        low_part(n - 1)

            def mixer_vectors():
                column_of(FIRST - 1)
                dve.wait_ge(ada_col, FIRST)
                dve.wait_ge(small_loaded, 48)
                modulation(0, 0, 1)
                rstd_of(0)
                rstd_of(1)

            row_tiles(part, ada, mixer_vectors, tile)
            low_part(2 * NT - 1)
            column_of(11)
            dve.wait_ge(ada_col, 12)
            modulation(1, 3, 4)
            dve.wait_ge(dt_raw, NT)
            dve.tensor_copy(s.dt[:], ps[3][:, 0:NT * NH])


def high_part(s, n):
    return s.h_hi[:, (n % 2) * 4:(n % 2) * 4 + 4, (n // 2) * P:(n // 2 + 1) * P]


def low_part_of(s, n):
    return s.h_lo[:, (n % 2) * 4:(n % 2) * 4 + 4, (n // 2) * P:(n // 2 + 1) * P]


def decays(nc, a, s):
    with ExitStack() as ctx:
        sb = lambda n, sh, dt=F32: ctx.enter_context(nc.sbuf_tensor("d_" + n, sh, dt))
        sem = lambda n: nc.alloc_semaphore("d_" + n)
        ps = [ctx.enter_context(nc.psum_tensor(f"d_ps{i}", [P, 512], F32)) for i in range(8)]
        hrow = sb("hrow", [P, 2, NH])
        tmp = [sb(f"tmp{i}", [P, NT * NH]) for i in range(6)]
        accT = sb("accT", [NH, T])
        extb = sb("extb", [8, EXT])

        small_loaded = sem("small_loaded")
        v_step = sem("v_step")
        to_scalar = sem("to_scalar")
        from_scalar = sem("from_scalar")
        a_ready = sem("a_ready")
        cum_ready = sem("cum_ready")
        accT_ready = sem("accT_ready")
        stored = sem("stored")
        ext_loaded = sem("ext_loaded")
        ext_ready = sem("ext_ready")
        block = ctx.enter_context(nc.Block())

        @block.sync
        def _(sp):
            sp.dma_start(extb[:, EXT - 385:EXT - 1], a["rel_rev"][:, 0:384]).then_inc(ext_loaded, 16)
            sp.dma_start(hrow[:, 0, :], rows(a["dt_bias"])).then_inc(small_loaded, 16)
            sp.dma_start(hrow[:, 1, :], rows(a["a_log"])).then_inc(small_loaded, 16)
            sp.wait_ge(ext_ready, 1)
            sp.dma_start(a["ext_dram"].rearrange("p h j -> h p j"), bc(extb[:], 1, [2 * PAIRS, P, EXT])).then_inc(stored, 16)
            sp.wait_ge(accT_ready, QT)
            sp.dma_start(a["acc_dram"], accT[:]).then_inc(stored, 16)
            sp.wait_ge(stored, 32)

        @block.tensor
        def _(pe):
            pe.wait_ge(a_ready, 1)
            pe.matmul(ps[1][:, 0:NT * NH], s.tri[:], tmp[5][:], start=True, stop=True)
            pe.matmul(ps[2][:, 0:NT * NH], s.ones[:], tmp[5][:], start=True, stop=True).then_inc(cum_ready, 1)
            for t in range(NT):
                mm = pe.matmul(ps[4 + t // 4][0:NH, (t % 4) * P:(t % 4 + 1) * P], tmp[5][:, t * NH:(t + 1) * NH],
                               s.tri[:], start=True, stop=True)
            mm.then_inc(cum_ready, 1)

        @block.scalar
        def _(act):
            act.wait_ge(to_scalar, 1)
            act.activation(tmp[1][:], tmp[1][:], ACT.Exp, scale=-1.0).then_inc(from_scalar, 1)
            act.activation(hrow[:, 1, :], hrow[:, 1, :], ACT.Exp).then_inc(from_scalar, 1)
            act.wait_ge(to_scalar, 2)
            act.activation(tmp[3][:], tmp[2][:], ACT.Ln).then_inc(from_scalar, 1)
            act.wait_ge(to_scalar, 3)
            act.activation(tmp[1][:], tmp[0][:], ACT.Exp).then_inc(from_scalar, 1)
            act.wait_ge(cum_ready, 2)
            for q in range(QT):
                act.activation(accT[:, q * 512:(q + 1) * 512], ps[4 + q][0:NH, :], ACT.Copy).then_inc(accT_ready, 1)

        @block.vector
        def _(dve):
            link = Chain(dve, v_step)
            dve.wait_ge(ext_loaded, 16)
            link(dve.memset(extb[:, EXT - 1:EXT], 0.0))
            link(dve.memset(extb[:, 0:EXT - 385], 0.0))
            dve.tensor_scalar(extb[:, 0:EXT - 385], extb[:, 0:EXT - 385], extb[:, EXT - 385:EXT - 384], None,
                              ALU.add).then_inc(ext_ready, 1)
            v3 = lambda t: t[:].rearrange("p (c h) -> p c h", h=NH)
            dve.wait_ge(small_loaded, 32)
            link(dve.tensor_tensor(v3(tmp[0]), v3(s.dt),
                                   bc(hrow[:, 0, :], 1, [P, NT, NH]), ALU.add))
            link(dve.tensor_scalar(tmp[1][:], tmp[0][:], -1.0, None, ALU.mult))
            dve.tensor_tensor(tmp[1][:], tmp[1][:], tmp[0][:], ALU.max).then_inc(to_scalar, 1)
            dve.wait_ge(from_scalar, 2)
            link(dve.tensor_scalar(tmp[2][:], tmp[1][:], 1.0, None, ALU.add))
            link(dve.tensor_scalar(tmp[4][:], tmp[2][:], -1.0, None, ALU.add))
            dve.tensor_scalar(tmp[5][:], tmp[4][:], 0.0, None, ALU.is_equal).then_inc(to_scalar, 1)
            dve.wait_ge(to_scalar, 2)
            link(dve.tensor_tensor(tmp[4][:], tmp[4][:], tmp[5][:], ALU.add))
            link(dve.reciprocal(tmp[4][:], tmp[4][:]))
            link(dve.tensor_tensor(tmp[4][:], tmp[4][:], tmp[1][:], ALU.mult))
            link(dve.tensor_tensor(tmp[5][:], tmp[5][:], tmp[1][:], ALU.mult))
            dve.wait_ge(from_scalar, 3)
            link(dve.tensor_tensor(tmp[4][:], tmp[4][:], tmp[3][:], ALU.mult))
            link(dve.tensor_tensor(tmp[4][:], tmp[4][:], tmp[5][:], ALU.add))
            link(dve.tensor_scalar(tmp[0][:], tmp[0][:], 0.0, None, ALU.max))
            link(dve.tensor_tensor(s.dt[:], tmp[4][:], tmp[0][:], ALU.add))
            link(dve.tensor_tensor(v3(tmp[5]), v3(s.dt), bc(hrow[:, 1, :], 1, [P, NT, NH]), ALU.mult))
            dve.tensor_scalar(tmp[5][:], tmp[5][:], -1.0, None, ALU.mult).then_inc(a_ready, 1)
            dve.wait_ge(cum_ready, 1)
            link(dve.tensor_copy(s.acc[:], ps[1][:, 0:NT * NH]))
            link(dve.tensor_tensor(tmp[0][:], ps[2][:, 0:NT * NH], s.acc[:], ALU.subtract))
            link(dve.tensor_scalar(tmp[0][:], tmp[0][:], 0.0, None, ALU.min))
            dve.nop().then_inc(to_scalar, 1)
            dve.wait_ge(from_scalar, 4)
            link(dve.tensor_tensor(s.dtdec[:], s.dt[:], tmp[1][:], ALU.mult))


def project(nc, a, s):
    with ExitStack() as ctx:
        sb = lambda n, sh, dt=F32: ctx.enter_context(nc.sbuf_tensor("j_" + n, sh, dt))
        sem = lambda n: nc.alloc_semaphore("j_" + n)
        BUFS, BANKS = 3, 4
        ps = [ctx.enter_context(nc.psum_tensor(f"j_ps{i}", [P, 512], F32)) for i in range(BANKS)]
        wr = [sb(f"wr{i}", [P, KD, P]) for i in range(BUFS)]
        w_hi = [sb(f"w_hi{i}", [P, KD, P], F32R) for i in range(BUFS)]
        w_lo = [sb(f"w_lo{i}", [P, KD, P], F32R) for i in range(BUFS)]
        raw = sb("raw", [P, CONV - 1 + T])
        done = [sb(f"done{i}", [P, T]) for i in range(BUFS)]
        turned_ps = ctx.enter_context(nc.psum_tensor("j_turned", [P, 512], F32))
        v_T = [sb(f"v_T{i}", [P, 512]) for i in range(2)]
        par_all = sb("par_all", [P, GROUPS, PAR])
        par = sb("par", [P, PAR])

        w_loaded = [sem(f"w_loaded{i}") for i in range(BUFS)]
        w_split = sem("w_split")
        w_turn = sem("w_turn")
        w_turn_pool = sem("w_turn_pool")
        par_loaded = sem("par_loaded")
        par_ready = sem("par_ready")
        acc_full = sem("acc_full")
        acc_free = sem("acc_free")
        conv_done = sem("conv_done")
        made = sem("made")
        v_copied = sem("v_copied")
        v_turned = sem("v_turned")
        v_done = sem("v_done")
        raw_zero = sem("raw_zero")
        v_step = sem("v_step")
        stored = [sem(f"stored{i}") for i in range(BUFS)]
        block = ctx.enter_context(nc.Block())
        w_view = a["w_in"].rearrange("(k p) n -> p k n", p=P)
        BACK_TILES = 3
        USES = [len(range(i, TILES, BUFS)) for i in range(BUFS)]

        def tile_col(g, m):
            if m < GF:
                return g * GD + (COL_X + m * P)
            if m < N_CONV:
                return g * NSTATE + (COL_B if m == GF else COL_C)
            if m < 8:
                return g * GD + (COL_Z + (m - N_CONV) * P)
            return g * P + (COL_Q, COL_K, COL_V)[m - 8]

        def through(m):
            last = m - BUFS if m >= BUFS else max(range(m, TILES, BUFS)) - TILES
            return last + 1

        def uses(m):
            return m // BUFS

        @block.sync
        def _(sp):
            sp.sem_inc(w_split, 2 * BACK_TILES)
            sp.dma_start(par_all[:], a["group_params"].rearrange("g p n -> p g n")).then_inc(par_loaded, 16)
            with sp.Fori(0, GROUPS) as g:
                for m in range(TILES):
                    col = sp.snap(tile_col(g, m), min_val=0, max_val=IN_COLS - P)
                    sp.wait_ge(w_split, g * (2 * TILES) + 2 * (through(m) + BACK_TILES))
                    sp.sem_inc(w_turn, 1)
                    sp.dma_start(wr[m % BUFS][:], w_view[:, :, bass.ds(col, P)]).then_inc(w_loaded[m % BUFS], 16)

        @block.gpsimd
        def _(pool):
            pool.sem_inc(acc_full, BACK_TILES * QT)
            with pool.Fori(0, GROUPS) as g:
                for m in range(TILES):
                    i = m % BUFS
                    pool.wait_ge(w_loaded[i], g * (16 * USES[i]) + 16 * (uses(m) + 1))
                    pool.wait_ge(acc_full, g * (QT * TILES) + QT * (through(m) + BACK_TILES))
                    pool.sem_inc(w_turn_pool, 1)
                    pool.tensor_copy(w_hi[i][:], wr[i][:]).then_inc(w_split, 1)
                    pool.wait_ge(w_split, g * (2 * TILES) + (2 * (m + BACK_TILES) + 1))
                    pool.tensor_tensor(w_lo[i][:], wr[i][:], w_hi[i][:].bitcast(F32), ALU.subtract).then_inc(w_split, 1)

        @block.tensor
        def _(pe):
            def turn(g, q):
                pe.wait_ge(v_copied, g * QT + (q + 1))
                pe.wait_ge(v_done, g * QT + (q + 1))
                for j in range(4):
                    mm = pe.transpose(turned_ps[:, j * P:(j + 1) * P], v_T[q % 2][:, j * P:(j + 1) * P], s.ident[:])
                mm.then_inc(v_turned, 1)

            with pe.Fori(0, GROUPS) as g:
                for n in range(TILES * QT):
                    m, q = n // QT, n % QT
                    i = m % BUFS
                    out = ps[n % BANKS]
                    if q == 0:
                        pe.wait_ge(w_split, g * (2 * TILES) + 2 * (m + 1 + BACK_TILES))
                    pe.wait_ge(acc_free, g * (TILES * QT) + (n + 1))
                    for k in range(KD):
                        cols = slice(q * 512, (q + 1) * 512)
                        pe.matmul(out[:], w_hi[i][:, k, :], s.h_hi[:, k, cols], start=(k == 0), stop=False)
                        pe.matmul(out[:], w_hi[i][:, k, :], s.h_lo[:, k, cols], start=False, stop=False)
                        mm = pe.matmul(out[:], w_lo[i][:, k, :], s.h_hi[:, k, cols], start=False, stop=(k == KD - 1))
                    mm.then_inc(acc_full, 1)
                    if m == TILES - 1 and q > 0:
                        turn(g, q - 1)
                turn(g, QT - 1)

        @block.scalar
        def _(act):
            act.sem_inc(acc_free, BANKS)
            for i in range(BUFS):
                act.sem_inc(stored[i], 16)

            def store(g, m):
                i = m % BUFS
                act.wait_ge(made, g * TILES + (m + 2))
                act.dma_start(a["proj_dram"][bass.ds(g, 1), m, :, :].rearrange("a p t -> p (a t)"), done[i][:]
                              ).then_inc(stored[i], 16)

            def silu(g, m):
                act.wait_ge(conv_done, g * N_CONV + (m + 2))
                act.activation(done[m % BUFS][:], done[m % BUFS][:], ACT.Silu, bias=par[:, 20 + m:21 + m]
                               ).then_inc(made, 1)
                store(g, m)

            def copy_v(g, i, q):
                act.wait_ge(v_turned, g * QT + (q + 3))
                act.activation(done[i][:, q * 512:(q + 1) * 512], turned_ps[:], ACT.Copy).then_inc(v_done, 1)

            act.sem_inc(v_turned, 2)
            act.sem_inc(v_done, 1)
            with act.Fori(0, GROUPS) as g:
                for n in range(TILES * QT):
                    m, q = n // QT, n % QT
                    i = m % BUFS
                    cols = slice(q * 512, (q + 1) * 512)
                    act.wait_ge(acc_full, g * (TILES * QT) + (BACK_TILES * QT + n + 1))
                    if m < N_CONV:
                        if q == 0:
                            act.wait_ge(conv_done, g * N_CONV + (m + 1))
                        act.activation(raw[:, CONV - 1 + q * 512:CONV - 1 + (q + 1) * 512], ps[n % BANKS][:],
                                       ACT.Copy).then_inc(acc_free, 1)
                    else:
                        if q == 0:
                            act.wait_ge(stored[i], g * (16 * USES[i]) + 16 * (uses(m) + 1))
                        if m < TILES - 1:
                            func, scale = (ACT.Silu, 1.0) if m < 8 else (ACT.Copy, HD ** -0.5 if m == 8 else 1.0)
                            act.activation(done[i][:, cols], ps[n % BANKS][:], func, scale=scale).then_inc(acc_free, 1)
                        else:
                            act.wait_ge(v_turned, g * QT + (q + 1))
                            act.activation(v_T[q % 2][:], ps[n % BANKS][:], ACT.Copy).then_inc(v_copied, 1)
                            act.wait_ge(v_copied, g * QT + (q + 1))
                            act.sem_inc(acc_free, 1)
                            if q > 0:
                                copy_v(g, i, q - 1)
                    if q == 1 and 1 <= m <= N_CONV:
                        silu(g, m - 1)
                    if q == QT - 1 and m >= N_CONV:
                        if m == TILES - 1:
                            copy_v(g, i, QT - 1)
                            act.wait_ge(v_done, g * QT + (QT + 1))
                        else:
                            act.wait_ge(acc_free, g * (TILES * QT) + (n + 1 + BANKS))
                        act.sem_inc(made, 1)
                        store(g, m)
            for i in range(BUFS):
                act.wait_ge(stored[i], 16 + 16 * GROUPS * USES[i])

        @block.vector
        def _(dve):
            dve.sem_inc(conv_done, 1)
            dve.memset(raw[:, 0:CONV - 1], 0.0).then_inc(raw_zero, 1)
            dve.wait_ge(raw_zero, 1)
            dve.wait_ge(par_loaded, 16)
            dve.sem_inc(made, 1)
            STEPS = N_CONV * (CONV - 1)
            with dve.Fori(0, GROUPS) as g:
                link = Chain(dve, v_step)
                link.base = g * STEPS
                dve.wait_ge(made, g * TILES + 1)
                dve.tensor_copy(par[:], par_all[:, bass.ds(g, 1), :].rearrange("p a n -> p (a n)")).then_inc(par_ready, 1)
                dve.wait_ge(par_ready, g + 1)
                for m in range(N_CONV):
                    i = m % BUFS
                    dve.wait_ge(acc_free, g * (TILES * QT) + ((m + 1) * QT + BANKS))
                    dve.wait_ge(stored[i], g * (16 * USES[i]) + 16 * (uses(m) + 1))
                    for j in range(CONV):
                        w = par[:, m * CONV + j:m * CONV + j + 1]
                        if j == 0:
                            link(dve.tensor_scalar(done[i][:], raw[:, 0:T], w, None, ALU.mult))
                        else:
                            ins = dve.scalar_tensor_tensor(done[i][:], raw[:, j:j + T], w, done[i][:], ALU.mult, ALU.add)
                            if j < CONV - 1:
                                link(ins)
                            else:
                                ins.then_inc(conv_done, 1)
                assert link.n == STEPS


def ssd(nc, a, s):
    with ExitStack() as ctx:
        sb = lambda n, sh, dt=F32: ctx.enter_context(nc.sbuf_tensor("g_" + n, sh, dt))
        sem = lambda n: nc.alloc_semaphore("g_" + n)
        ps = [ctx.enter_context(nc.psum_tensor(f"g_ps{i}", [P, 512], F32)) for i in range(8)]
        CB, CT, CZ = 3, 4, 5
        LOADED = 8
        tiles = [sb(f"tiles{i}", [P, LOADED, 512]) for i in range(2)]
        par_all = sb("par_all", [P, GROUPS, PAR])
        par = sb("par", [P, PAR])
        dt_g = sb("dt_g", [P, 3, NT, GH])
        abc = [sb(f"abc{i}", [P, GH, P]) for i in range(2)]
        ea = [sb(f"ea{i}", [P, GH, P]) for i in range(2)]
        lm = [sb(f"lm{i}", [P, GH, P]) for i in range(2)]
        cs = [sb(f"cs{i}", [P, GH, P]) for i in range(2)]
        cbm = sb("cbm", [P, P])
        xdt = [sb(f"xdt{i}", [P, GD]) for i in range(2)]
        xde = [sb(f"xde{i}", [P, GD]) for i in range(2)]
        btok = [sb(f"btok{i}", [P, NSTATE]) for i in range(2)]
        st = [sb(f"st{i}", [P, GD]) for i in range(2)]
        stmp = sb("stmp", [P, GD])
        yb = [sb(f"yb{i}", [P, GF, P]) for i in range(2)]
        sq = [sb(f"sq{i}", [P, GF, P]) for i in range(2)]

        tiles_loaded = [sem("tiles_loaded0"), sem("tiles_loaded1")]
        par_loaded = sem("par_loaded")
        sum_zero = sem("sum_zero")
        turn_sem = sem("turn_sem")
        v_step = sem("v_step")
        abc_loaded = [sem("abc_loaded0"), sem("abc_loaded1")]
        seg_done = sem("seg_done")
        ea_done = sem("ea_done")
        e_done = sem("e_done")
        lm_done = sem("lm_done")
        cs_done = sem("cs_done")
        x_turned = sem("x_turned")
        xdt_done = sem("xdt_done")
        btok_done = sem("btok_done")
        cb_full = sem("cb_full")
        cbm_done = sem("cbm_done")
        st_full = sem("st_full")
        st_done = sem("st_done")
        st_decayed = sem("st_decayed")
        y_full = sem("y_full")
        y_read = sem("y_read")
        gated = sem("gated")
        sq_done = sem("sq_done")
        ss_full = sem("ss_full")
        ss_read = sem("ss_read")
        y_stored = [sem("y_stored0"), sem("y_stored1")]
        block = ctx.enter_context(nc.Block())

        BACK_CHUNKS = 5

        def part(i, c):
            return tiles[(c // 4) % 2][:, i, (c % 4) * P:(c % 4 + 1) * P]

        def wait_tiles(eng, g, c):
            eng.wait_ge(tiles_loaded[(c // 4) % 2], g * 32 + 16 * (c // 8 + 1))

        @block.sync
        def _(sp):
            sp.sem_inc(y_stored[0], 16)
            sp.sem_inc(y_stored[1], 16)
            sp.dma_start(par_all[:], a["group_params"].rearrange("g p n -> p g n")).then_inc(par_loaded, 16)

            def load(g, r):
                group = bass.ds(g, 1) if not isinstance(g, int) else slice(g, g + 1)
                sp.dma_start(tiles[r % 2][:], a["proj_dram"][group, 0:LOADED, :, r * 512:(r + 1) * 512]
                             .rearrange("a m p t -> p (a m) t")).then_inc(tiles_loaded[r % 2], 16)

            load(0, 0)
            with sp.Fori(0, GROUPS) as g:
                head0 = sp.snap(g * GH, min_val=0, max_val=NH - GH)
                for c in range(NT):
                    if c % 4 == 2 and c < NT - 4:
                        sp.wait_ge(gated, g * NT + (c - 2 + BACK_CHUNKS))
                        sp.sem_inc(turn_sem, 1)
                        load(g, c // 4 + 1)
                    if c == NT - 2:
                        sp.wait_ge(gated, g * NT + (c - 2 + BACK_CHUNKS))
                        sp.sem_inc(turn_sem, 1)
                        with sp.If(g < GROUPS - 1):
                            load((g + 1) & (GROUPS - 1), 0)
                    if c < NT:
                        sp.wait_ge(seg_done, g * NT + (c + 1))
                        sp.wait_ge(ea_done, g * NT + (c + 1))
                        src = a["acc_dram"][bass.ds(head0, GH), c * P:(c + 1) * P]
                        sp.dma_start(abc[c % 2][:], src.partition_broadcast(P)).then_inc(abc_loaded[c % 2], 16)

        @block.gpsimd
        def _(pool):
            def gate(g, c):
                pool.wait_ge(y_read, g * NT + (c + 3))
                pool.tensor_tensor(yb[c % 2][:], yb[c % 2][:], tiles[(c // 4) % 2][:, CZ:CZ + GF, (c % 4) * P:(c % 4 + 1) * P],
                                   ALU.mult).then_inc(gated, 1)

            with pool.Fori(0, GROUPS) as g:
                for c in range(1, NT):
                    pool.wait_ge(ea_done, g * NT + (c + 3))
                    wait_tiles(pool, g, c)
                    if c >= 3:
                        pool.wait_ge(y_full, g * NT + (c - 1))
                    pool.tensor_tensor(cs[c % 2][:], bc(part(CT, c), 1, [P, GH, P]), ea[c % 2][:],
                                       ALU.mult).then_inc(cs_done, 1)
                    pool.wait_ge(st_done, g * NT + (c + 1))
                    v = lambda t: t[:].rearrange("p (h d) -> p h d", d=HD)
                    pool.tensor_tensor(v(stmp), v(st[c % 2]), ea[c % 2][:, :, P - 1:P].broadcast_to([P, GH, HD]),
                                       ALU.mult).then_inc(st_decayed, 1)
                    gate(g, c - 1)
                gate(g, NT - 1)

        @block.tensor
        def _(pe):
            with pe.Fori(0, GROUPS) as g:
                def turn(c):
                    wait_tiles(pe, g, c)
                    pe.wait_ge(xdt_done, g * NT + (c + 1))
                    pe.wait_ge(btok_done, g * NT + (c + 1))
                    for j in range(GF):
                        pe.transpose(ps[2][:, j * P:(j + 1) * P], part(j, c), s.ident[:])
                    pe.transpose(ps[0][:, 0:P], part(CB, c), s.ident[:]).then_inc(x_turned, 1)
                    pe.wait_ge(cbm_done, g * NT + (c + 1))
                    pe.matmul(ps[3][:, 0:P], part(CB, c), part(CT, c), start=True, stop=True
                              ).then_inc(cb_full, 1)

                def sums(c):
                    pe.wait_ge(sq_done, g * NT + (c + 1))
                    if c == 0:
                        pe.wait_ge(ss_read, g + 1)
                    for j in range(GF):
                        mm = pe.matmul(ps[7][:, c:c + 1], sq[c % 2][:, j, :], s.ones[:, 0:1],
                                       start=(j == 0), stop=(j == GF - 1))
                    mm.then_inc(ss_full, 1)

                turn(0)
                for c in range(NT):
                    pe.wait_ge(xdt_done, g * NT + (c + 2))
                    pe.wait_ge(btok_done, g * NT + (c + 2))
                    pe.wait_ge(st_done, g * NT + (c + 1))
                    pe.matmul(ps[4][:, 0:GD], btok[c % 2][:], xde[c % 2][:], start=True, stop=True
                              ).then_inc(st_full, 1)
                    if c + 1 < NT:
                        turn(c + 1)
                    pe.wait_ge(lm_done, g * NT + (c + 1))
                    if c > 0:
                        pe.wait_ge(cs_done, g * (NT - 1) + c)
                    pe.wait_ge(y_read, g * NT + (c + 1))
                    for h in range(GH):
                        out = ps[5 + c % 2][64 * (h % 2):64 * (h % 2) + 64, (h // 2) * P:(h // 2 + 1) * P]
                        hc = slice(h * HD, (h + 1) * HD)
                        if c > 0:
                            pe.matmul(out, st[c % 2][:, hc], cs[c % 2][:, h, :], start=True, stop=False)
                        mm = pe.matmul(out, xdt[c % 2][:, hc], lm[c % 2][:, h, :], start=(c == 0), stop=True)
                    mm.then_inc(y_full, 1)
                    if c >= 2:
                        sums(c - 2)
                sums(NT - 2)
                sums(NT - 1)

        @block.scalar
        def _(act):
            act.sem_inc(ea_done, 2)
            act.sem_inc(btok_done, 1)
            with act.Fori(0, GROUPS) as g:
                feat0 = act.snap(g * GF, min_val=0, max_val=KS - GF)
                for c in range(NT + 2):
                    if c < NT:
                        act.wait_ge(abc_loaded[c % 2], g * (8 * NT) + 16 * (c // 2 + 1))
                        if c >= 3:
                            act.wait_ge(cs_done, g * (NT - 1) + (c - 2))
                        act.wait_ge(st_done, g * NT + max(c, 1))
                        act.activation(ea[c % 2][:], abc[c % 2][:], ACT.Exp).then_inc(ea_done, 1)
                        act.wait_ge(x_turned, g * NT + (c + 1))
                        if c >= 2:
                            act.wait_ge(st_full, g * NT + (c - 1))
                        act.activation(btok[c % 2][:], ps[0][:, 0:P], ACT.Copy).then_inc(btok_done, 1)
                        act.wait_ge(seg_done, g * NT + (c + 3))
                        act.activation(lm[c % 2][:], lm[c % 2][:], ACT.Exp).then_inc(e_done, 1)
                    if c >= 2:
                        u = c - 2
                        act.wait_ge(gated, g * NT + (u + 1 + BACK_CHUNKS))
                        dst = a["yT_dram"][bass.ds(feat0, GF), :, u * P:(u + 1) * P].rearrange("j p t -> p j t")
                        act.dma_start(dst, yb[u % 2][:]).then_inc(y_stored[u % 2], 16)
                        if u >= 2:
                            act.wait_ge(ss_full, g * NT + (u - 1))
                        act.activation(sq[u % 2][:], yb[u % 2][:], ACT.Square).then_inc(sq_done, 1)
            for i in range(2):
                act.wait_ge(y_stored[i], 16 + 16 * GROUPS * NT // 2)

        @block.vector
        def _(dve):
            dve.sem_inc(seg_done, 2)
            dve.sem_inc(gated, BACK_CHUNKS)
            dve.sem_inc(xdt_done, 1)
            dve.sem_inc(cbm_done, 1)
            dve.sem_inc(st_done, 1)
            dve.sem_inc(y_read, 2)
            dve.sem_inc(ss_read, 1)
            dve.memset(s.norm_sum[:], 0.0).then_inc(sum_zero, 1)
            dve.wait_ge(sum_zero, 1)
            dve.wait_ge(par_loaded, 16)
            STEPS = 4 + NT + 1
            with dve.Fori(0, GROUPS) as g:
                link = Chain(dve, v_step)
                link.base = g * STEPS
                link(dve.tensor_copy(par[:], par_all[:, bass.ds(g, 1), :].rearrange("p a n -> p (a n)")))
                for i, t in enumerate((s.dt, s.dtdec, s.acc)):
                    link(dve.tensor_copy(dt_g[:, i, :, :],
                                         t[:].rearrange("p (c h) -> p c h", h=NH)[:, :, bass.ds(g * GH, GH)]))
                def state(c):
                    dve.wait_ge(st_full, g * NT + (c + 1))
                    if c >= 1:
                        dve.wait_ge(y_full, g * NT + c)
                    if c == 0:
                        dve.tensor_copy(st[1][:], ps[4][:, 0:GD]).then_inc(st_done, 1)
                    else:
                        dve.wait_ge(st_decayed, g * (NT - 1) + c)
                        dve.tensor_tensor(st[(c + 1) % 2][:], stmp[:], ps[4][:, 0:GD], ALU.add).then_inc(st_done, 1)

                def finish(c):
                    dve.wait_ge(y_full, g * NT + (c + 1))
                    if c >= 2:
                        dve.wait_ge(sq_done, g * NT + (c - 1))
                    dve.wait_ge(y_stored[c % 2], g * (8 * NT) + 16 * (c // 2 + 1))
                    for j in range(GF):
                        ins = dve.scalar_tensor_tensor(yb[c % 2][:, j, :], part(j, c), par[:, 25 + j:26 + j],
                                                       ps[5 + c % 2][:, j * P:(j + 1) * P], ALU.mult, ALU.add)
                    ins.then_inc(y_read, 1)

                for c in range(NT):
                    dve.wait_ge(abc_loaded[c % 2], g * (8 * NT) + 16 * (c // 2 + 1))
                    if c >= 2:
                        dve.wait_ge(y_full, g * NT + (c - 1))
                    for h in range(GH):
                        ins = dve.tensor_scalar(lm[c % 2][:, h, :], abc[c % 2][:, h, :], dt_g[:, 2, c, h:h + 1], 0.0,
                                                ALU.subtract, ALU.min)
                    ins.then_inc(seg_done, 1)
                    dve.wait_ge(x_turned, g * NT + (c + 1))
                    x3 = ps[2][:, 0:GD].rearrange("p (h d) -> p h d", d=HD)
                    v = lambda t: t[:].rearrange("p (h d) -> p h d", d=HD)
                    link(dve.tensor_tensor(v(xdt[c % 2]), x3, bc(dt_g[:, 0, c, :], 2, [P, GH, HD]), ALU.mult))
                    dve.tensor_tensor(v(xde[c % 2]), x3, bc(dt_g[:, 1, c, :], 2, [P, GH, HD]), ALU.mult
                                      ).then_inc(xdt_done, 1)
                    dve.wait_ge(cb_full, g * NT + (c + 1))
                    if c >= 1:
                        dve.wait_ge(lm_done, g * NT + c)
                    dve.tensor_tensor(cbm[:], ps[3][:, 0:P], s.tri[:], ALU.mult).then_inc(cbm_done, 1)
                    dve.wait_ge(cbm_done, g * NT + (c + 2))
                    dve.wait_ge(e_done, g * NT + (c + 1))
                    dve.tensor_tensor(lm[c % 2][:], lm[c % 2][:], bc(cbm[:], 1, [P, GH, P]), ALU.mult
                                      ).then_inc(lm_done, 1)
                    if c >= 1:
                        finish(c - 1)
                    state(c)
                finish(NT - 1)
                dve.wait_ge(ss_full, g * NT + NT)
                link(dve.tensor_tensor(s.norm_sum[:, 0, :], s.norm_sum[:, 0, :], ps[7][:, 0:NT], ALU.add))
                dve.nop().then_inc(ss_read, 1)
                assert link.n == STEPS


def attend(nc, a, s):
    with ExitStack() as ctx:
        sb = lambda n, sh, dt=F32: ctx.enter_context(nc.sbuf_tensor("t_" + n, sh, dt))
        sem = lambda n: nc.alloc_semaphore("t_" + n)
        scores = [ctx.enter_context(nc.psum_tensor(f"t_scores{i}", [P, 1024], F32)) for i in range(2)]
        turned_ps = ctx.enter_context(nc.psum_tensor("t_turned", [P, 1024], F32))
        out_ps = [ctx.enter_context(nc.psum_tensor(f"t_out{i}", [P, 512], F32)) for i in range(2)]
        NK = BAND // P
        UNITS = 2 * NT
        BACK_UNITS = UNITS
        bias = sb("bias", [P, 2 * PAIRS, BAND])
        q_T = sb("q_T", [P, T])
        k_T = sb("k_T", [P, T])
        v_r = sb("v_r", [P, NT, P])
        pb = [sb(f"pb{i}", [P, BAND]) for i in range(3)]
        pt = [sb(f"pt{i}", [P, BAND]) for i in range(2)]
        nmax = [sb(f"nmax{i}", [P, 1]) for i in range(3)]
        rsum = [sb(f"rsum{i}", [P, 1]) for i in range(3)]
        rinv = [sb(f"rinv{i}", [P, 1]) for i in range(3)]
        o_T = sb("o_T", [P, T])
        sq = sb("sq", [P, T])

        loaded = [sem(f"loaded{i}") for i in range(QT)]
        turn_sem = sem("turn_sem")
        bias_loaded = sem("bias_loaded")
        bias_ready = sem("bias_ready")
        s_full = sem("s_full")
        biased = sem("biased")
        max_done = sem("max_done")
        exp_done = sem("exp_done")
        probs_done = sem("probs_done")
        turned = sem("turned")
        pt_done = sem("pt_done")
        out_full = sem("out_full")
        out_read = sem("out_read")
        sq_done = sem("sq_done")
        ss_full = sem("ss_full")
        ss_read = sem("ss_read")
        v_step = sem("v_step")
        stored = sem("stored")
        block = ctx.enter_context(nc.Block())
        width = lambda t: (min(t, NK - 1) + 1) * P

        @block.sync
        def _(sp):
            ext = a["ext_dram"]
            sp.dma_start(bias[:], bass.AP(ext.tensor, P - 1, [[2 * PAIRS * EXT - 1, P], [EXT, 2 * PAIRS], [1, BAND]])
                         ).then_inc(bias_loaded, 16)
            sp.sem_inc(out_full, BACK_UNITS)
            sp.sem_inc(stored, 16)
            with sp.Fori(0, PAIRS) as p:
                for r in range(QT):
                    sp.wait_ge(out_full, p * UNITS + min(8 * (r + 2), UNITS))
                    sp.sem_inc(turn_sem, 1)
                    cols = slice(r * 512, (r + 1) * 512)
                    for i, t in enumerate((q_T[:, cols], k_T[:, cols],
                                           v_r[:, 4 * r:4 * r + 4, :].rearrange("p t d -> p (t d)"))):
                        sp.dma_start(t, a["proj_dram"][bass.ds(p, 1), 8 + i, :, cols].rearrange("a p t -> p (a t)")
                                     ).then_inc(loaded[r], 16)
                sp.wait_ge(out_read, p * NT + (NT + 2))
                sp.sem_inc(turn_sem, 1)
                sp.dma_start(a["yT_dram"][bass.ds(p + KS, 1), :, :].rearrange("a p t -> p (a t)"), o_T[:]
                             ).then_inc(stored, 16)
            sp.wait_ge(stored, 16 + 16 * PAIRS)

        @block.gpsimd
        def _(pool):
            pool.wait_ge(bias_loaded, 16)
            pool.memset(bias[0:CHUNK, :, BAND - CHUNK:BAND], NEG).then_inc(bias_ready, 1)
            pool.memset(bias[CHUNK:P, :, 0:CHUNK], NEG).then_inc(bias_ready, 1)

        @block.tensor
        def _(pe):
            with pe.Fori(0, PAIRS) as p:
                def attend_scores(n):
                    t, hh = n // 2, n % 2
                    d = slice(hh * HD, hh * HD + HD)
                    k0 = max(0, t - NK + 1) * P
                    if n % 8 == 0:
                        pe.wait_ge(loaded[t // 4], p * 48 + 48)
                    pe.wait_ge(biased, p * UNITS + (n + 1))
                    for c0 in range(0, width(t), 512):
                        c1 = min(c0 + 512, width(t))
                        mm = pe.matmul(scores[n % 2][:, c0:c1], q_T[d, t * P:(t + 1) * P], k_T[d, k0 + c0:k0 + c1],
                                       start=True, stop=True)
                    mm.then_inc(s_full, 1)

                def turn(n):
                    pe.wait_ge(probs_done, p * UNITS + (n + 1))
                    pe.wait_ge(pt_done, p * UNITS + (n + 1))
                    if n == 0:
                        pe.wait_ge(ss_read, p + 1)
                    for j in range(width(n // 2) // P):
                        mm = pe.transpose(turned_ps[:, j * P:(j + 1) * P], pb[n % 3][:, j * P:(j + 1) * P], s.ident[:])
                    mm.then_inc(turned, 1)

                def weigh(n):
                    t, hh = n // 2, n % 2
                    nk = width(t) // P
                    pe.wait_ge(pt_done, p * UNITS + (n + 2))
                    if hh == 0:
                        pe.wait_ge(out_read, p * NT + (t + 1))
                    for j in range(nk):
                        mm = pe.matmul(out_ps[t % 2][hh * HD:hh * HD + HD, 0:P],
                                       v_r[:, t - nk + 1 + j, hh * HD:hh * HD + HD], pt[n % 2][:, j * P:(j + 1) * P],
                                       start=(j == 0), stop=(j == nk - 1))
                    mm.then_inc(out_full, 1)

                for n in range(UNITS + 3):
                    if n < UNITS:
                        attend_scores(n)
                    if 2 <= n < UNITS + 2:
                        turn(n - 2)
                    if n >= 3:
                        weigh(n - 3)
                pe.wait_ge(sq_done, p + 1)
                pe.wait_ge(pt_done, p * UNITS + (UNITS + 1))
                for t in range(NT):
                    mm = pe.matmul(turned_ps[:, t:t + 1], sq[:, t * P:(t + 1) * P], s.ones[:, 0:1],
                                   start=True, stop=True)
                mm.then_inc(ss_full, 1)

        @block.scalar
        def _(act):
            act.sem_inc(pt_done, 1)
            with act.Fori(0, PAIRS) as p:
                for n in range(UNITS + 2):
                    if n >= 2:
                        u = n - 2
                        act.wait_ge(turned, p * UNITS + (u + 1))
                        if u >= 2:
                            act.wait_ge(out_full, p * UNITS + (u - 1 + BACK_UNITS))
                        act.activation(pt[u % 2][:, 0:width(u // 2)], turned_ps[:, 0:width(u // 2)], ACT.Copy
                                       ).then_inc(pt_done, 1)
                    if n < UNITS:
                        act.wait_ge(max_done, p * UNITS + (n + 1))
                        v = pb[n % 3][:, 0:width(n // 2)]
                        act.activation(v, v, ACT.Exp, bias=nmax[n % 3][:], accum_out=rsum[n % 3][:]).then_inc(exp_done, 1)
                act.wait_ge(out_read, p * NT + (NT + 2))
                act.activation(sq[:], o_T[:], ACT.Square).then_inc(sq_done, 1)

        @block.vector
        def _(dve):
            dve.sem_inc(biased, 2)
            dve.sem_inc(out_read, 2)
            dve.sem_inc(ss_read, 1)
            dve.wait_ge(bias_ready, 2)
            STEPS = UNITS + 1
            with dve.Fori(0, PAIRS) as p:
                link = Chain(dve, v_step)
                link.base = p * STEPS
                for n in range(UNITS + 4):
                    if n < UNITS:
                        t, hh = n // 2, n % 2
                        wd = width(t)
                        dve.wait_ge(s_full, p * UNITS + (n + 1))
                        if n >= 3:
                            dve.wait_ge(turned, p * UNITS + (n - 2))
                        b = bias[:, bass.ds(p * 2 + hh, 1), BAND - wd:BAND].rearrange("p a k -> p (a k)")
                        dve.tensor_tensor(pb[n % 3][:, 0:wd], scores[n % 2][:, 0:wd], b, ALU.add).then_inc(biased, 1)
                        dve.wait_ge(biased, p * UNITS + (n + 3))
                        dve.tensor_reduce(nmax[n % 3][:], pb[n % 3][:, 0:wd], AX.X, ALU.max, negate=True
                                          ).then_inc(max_done, 1)
                    if 1 <= n <= UNITS:
                        u = n - 1
                        dve.wait_ge(exp_done, p * UNITS + (u + 1))
                        link(dve.reciprocal(rinv[u % 3][:], rsum[u % 3][:]))
                        v = pb[u % 3][:, 0:width(u // 2)]
                        dve.tensor_scalar(v, v, rinv[u % 3][:], None, ALU.mult).then_inc(probs_done, 1)
                    if n >= 5 and n % 2 == 1:
                        t = (n - 5) // 2
                        dve.wait_ge(out_full, p * UNITS + (2 * t + 2 + BACK_UNITS))
                        if t == 0:
                            dve.wait_ge(ss_read, p + 1)
                            dve.wait_ge(stored, p * 16 + 16)
                        dve.tensor_copy(o_T[:, t * P:(t + 1) * P], out_ps[t % 2][:, 0:P]).then_inc(out_read, 1)
                dve.wait_ge(ss_full, p + 1)
                link(dve.tensor_tensor(s.norm_sum[:, 1, :], s.norm_sum[:, 1, :], turned_ps[:, 0:NT], ALU.add))
                dve.nop().then_inc(ss_read, 1)
                assert link.n == STEPS


def mix(nc, a, s):
    with ExitStack() as ctx:
        sb = lambda n, sh, dt=F32: ctx.enter_context(nc.sbuf_tensor("m_" + n, sh, dt))
        sem = lambda n: nc.alloc_semaphore("m_" + n)
        ps = [ctx.enter_context(nc.psum_tensor(f"m_ps{i}", [P, 512], F32)) for i in range(7)]
        NR = NG + NE
        w_raw = [sb(f"w_raw{i}", [P, D]) for i in range(2)]
        w_hi = sb("w_hi", [P, KM, D], F32R)
        w_lo = sb("w_lo", [P, KM, D], F32R)
        norm_g = sb("norm_g", [P, KM])
        w_r = sb("w_r", [P, KD, NR])
        b_r = sb("b_r", [P, NR])
        gate = sb("gate", [P, D])
        nstd = sb("nstd", [P, 2, NT])
        nrstd = sb("nrstd", [P, 2, NT])
        y_hi = [sb(f"y_hi{i}", [P, KM, P], F32R) for i in range(2)]
        y_lo = [sb(f"y_lo{i}", [P, KM, P], F32R) for i in range(2)]
        tmp = [sb(f"tmp{i}", [P, 512]) for i in range(2)]
        x1 = [sb(f"x1{i}", [P, D]) for i in range(2)]
        xn = [sb(f"xn{i}", [P, D]) for i in range(2)]
        mean_sq = [sb(f"mean_sq{i}", [P, 1]) for i in range(2)]
        std = [sb(f"std{i}", [P, 1]) for i in range(2)]
        rstd = [sb(f"rstd{i}", [P, 1]) for i in range(2)]
        h_T = [sb(f"h_T{i}", [P, KD, P]) for i in range(2)]

        w_loaded = [sem("w_loaded0"), sem("w_loaded1")]
        w_hi_done = sem("w_hi_done")
        w_lo_done = sem("w_lo_done")
        y_loaded = [sem("y_loaded0"), sem("y_loaded1")]
        y_hi_done = sem("y_hi_done")
        y_lo_done = sem("y_lo_done")
        pool_turn = sem("pool_turn")
        small_loaded = sem("small_loaded")
        tile_loaded = [sem("tile_loaded0"), sem("tile_loaded1")]
        norm_std = sem("norm_std")
        v_step = sem("v_step")
        out_full = sem("out_full")
        y_free = sem("y_free")
        out_read = sem("out_read")
        x1_done = sem("x1_done")
        a_step = sem("a_step")
        std_done = sem("std_done")
        rstd_done = sem("rstd_done")
        xn_done = sem("xn_done")
        stored = [sem("stored0"), sem("stored1")]
        turned = sem("turned")
        h_done = sem("h_done")
        r_full = sem("r_full")
        r_read = sem("r_read")
        block = ctx.enter_context(nc.Block())

        @block.sync
        def _(sp):
            sp.sem_inc(out_full, 4)
            sp.dma_start(norm_g[:], a["y_norm_g"]).then_inc(small_loaded, 16)
            wv = a["w_out"].rearrange("(k p) n -> k p n", p=P)

            def load_w(k):
                if k >= 2:
                    sp.wait_ge(w_lo_done, k - 1)
                sp.dma_start(w_raw[k % 2][:], wv[k, :, :]).then_inc(w_loaded[k % 2], 16)

            def load_y(row, u):
                sp.dma_start(y_lo[u][:].bitcast(F32), a["yT_dram"].rearrange("k p t -> p k t")[:, :, bass.ds(row, P)]
                             ).then_inc(y_loaded[u], 16)

            def load_x(row, u):
                sp.dma_start(x1[u][:], a["x"][bass.ds(row, P), :]).then_inc(tile_loaded[u], 16)

            load_w(0)
            load_y(0, 0)
            load_w(1)
            sp.dma_start(w_r[:], a["w_router"]).then_inc(small_loaded, 16)
            sp.dma_start(b_r[:], rows(a["b_router"])).then_inc(small_loaded, 16)
            sp.dma_start(gate[:], rows(a["gates_dram"][:, 0:D])).then_inc(small_loaded, 16)
            for k in range(2, KM):
                load_w(k)
                if k == 4:
                    load_x(0, 0)
                if k == 6:
                    load_y(P, 1)
                if k == 8:
                    load_x(P, 1)
            with sp.Fori(1, NT // 2) as i:
                for u in range(2):
                    row = sp.snap(i * (2 * P) + u * P, min_val=0, max_val=T - P)
                    sp.wait_ge(out_full, i * 4 + (2 * u + 2))
                    sp.sem_inc(y_free, 1)
                    load_y(row, u)
                    sp.wait_ge(stored[u], i * 32 + 32)
                    sp.sem_inc(y_free, 1)
                    load_x(row, u)

        @block.gpsimd
        def _(pool):
            with pool.Fori(0, NT // 2) as i:
                for u in range(2):
                    whole = y_lo[u][:].bitcast(F32)
                    pool.wait_ge(y_loaded[u], i * 16 + 16)
                    pool.sem_inc(pool_turn, 1)
                    pool.tensor_copy(y_hi[u][:], whole).then_inc(y_hi_done, 1)
                    pool.wait_ge(y_hi_done, i * 2 + (u + 1))
                    pool.tensor_tensor(y_lo[u][:], whole, y_hi[u][:].bitcast(F32), ALU.subtract).then_inc(y_lo_done, 1)

        @block.tensor
        def _(pe):
            pe.wait_ge(small_loaded, 64)

            def project(b, o, u):
                pe.wait_ge(y_lo_done, b + (o + 1))
                first = isinstance(b, int) and o == 0
                order = [(k, half) for k in range(KM) for half in range(2)] if first else \
                        [(k, half) for half in range(2) for k in range(KM)]
                for k, half in order:
                    cols = slice(half * 512, (half + 1) * 512)
                    if k == 0:
                        pe.wait_ge(out_read, b * 2 + (2 * o + half + 1))
                    if first:
                        pe.wait_ge(w_lo_done, k + 1)
                    out = ps[half if k < KS else 2 + half][:]
                    pe.matmul(out, y_hi[u][:, k, :], w_hi[:, k, cols], start=(k in (0, KS)), stop=False)
                    pe.matmul(out, y_hi[u][:, k, :], w_lo[:, k, cols], start=False, stop=False)
                    mm = pe.matmul(out, y_lo[u][:, k, :], w_hi[:, k, cols], start=False, stop=(k in (KS - 1, KM - 1)))
                    if k == KM - 1:
                        mm.then_inc(out_full, 1)

            def turn(b, o, u):
                pe.wait_ge(xn_done, b + (o + 1))
                pe.wait_ge(h_done, b + (o + 1))
                for k in range(KD):
                    mm = pe.transpose(ps[4 + k // 4][:, (k % 4) * P:(k % 4 + 1) * P], xn[u][:, k * P:(k + 1) * P], s.ident[:])
                mm.then_inc(turned, 1)

            def router(b, o, u):
                pe.wait_ge(h_done, b + (o + 2))
                pe.wait_ge(r_read, b + (o + 1))
                for k in range(KD):
                    mm = pe.matmul(ps[6][:, 0:NR], h_T[u][:, k, :], w_r[:, k, :], start=(k == 0), stop=(k == KD - 1))
                mm.then_inc(r_full, 1)

            pipeline(pe, project, turn, router)

        @block.scalar
        def _(act):
            act.sem_inc(stored[0], 32)
            act.sem_inc(stored[1], 32)
            act.activation(nstd[:, 0, :], s.norm_sum[:, 0, :], ACT.Sqrt, scale=1.0 / D_SSD, bias=s.eps[:]
                           ).then_inc(norm_std, 1)
            act.activation(nstd[:, 1, :], s.norm_sum[:, 1, :], ACT.Sqrt, scale=1.0 / D_ATT, bias=s.eps[:]
                           ).then_inc(norm_std, 1)
            act.wait_ge(small_loaded, 64)
            for k in range(KM):
                act.wait_ge(w_loaded[k % 2], 16 * (k // 2 + 1))
                act.activation(w_hi[:, k, :], w_raw[k % 2][:], ACT.Copy, scale=norm_g[:, k:k + 1]).then_inc(w_hi_done, 1)
            with act.Fori(0, NT // 2) as i:
                for u in range(2):
                    j = i * 2
                    row = act.snap(i * (2 * P) + u * P, min_val=0, max_val=T - P)
                    act.wait_ge(x1_done, j + (u + 3))
                    act.dma_start(a["x1_dram"][bass.ds(row, P), :], x1[u][:]).then_inc(stored[u], 16)
                    act.wait_ge(turned, j + (u + 1))
                    act.wait_ge(stored[u], i * 32 + 32)
                    act.activation(xn[u][:], x1[u][:], ACT.Square, scale=D ** -0.5, accum_out=mean_sq[u][:]
                                   ).then_inc(a_step, 1)
                    act.wait_ge(a_step, j + (u + 1))
                    act.activation(std[u][:], mean_sq[u][:], ACT.Sqrt, bias=s.eps[:]).then_inc(std_done, 1)
                    act.wait_ge(rstd_done, j + (u + 1))
                    act.activation(xn[u][:], x1[u][:], ACT.Copy, scale=rstd[u][:]).then_inc(xn_done, 1)
                    act.wait_ge(xn_done, j + (u + 1))
                    act.dma_start(a["xn_dram"][bass.ds(row, P), :], xn[u][:]).then_inc(stored[u], 16)
            act.wait_ge(stored[0], 32 + 16 * NT)
            act.wait_ge(stored[1], 32 + 16 * NT)

        @block.vector
        def _(dve):
            dve.sem_inc(out_read, 2)
            dve.sem_inc(x1_done, 2)
            dve.sem_inc(h_done, 1)
            dve.sem_inc(r_read, 1)
            dve.sem_inc(turned, 2)
            dve.wait_ge(norm_std, 2)
            dve.reciprocal(nrstd[:], nstd[:]).then_inc(norm_std, 1)
            dve.wait_ge(norm_std, 3)
            dve.wait_ge(small_loaded, 64)
            for k in range(KM):
                dve.wait_ge(w_hi_done, k + 1)
                dve.scalar_tensor_tensor(w_lo[:, k, :], w_raw[k % 2][:], norm_g[:, k:k + 1], w_hi[:, k, :].bitcast(F32),
                                         ALU.mult, ALU.subtract).then_inc(w_lo_done, 1)

            def combine(b, o, u):
                dve.wait_ge(tile_loaded[u], b * 8 + (16 * ((o - u) // 2) + 16))
                col = bass.ds(b + o, 1) if not isinstance(b, int) else slice(b + o, b + o + 1)
                for half in range(2):
                    cols = slice(half * 512, (half + 1) * 512)
                    out = tmp[half][:]
                    dve.wait_ge(out_full, b * 2 + (2 * o + half + 5))
                    base = (b + o) * 6 + (3 * half + 1)
                    dve.tensor_scalar(out, ps[half][:], nrstd[:, 0, col], None, ALU.mult).then_inc(v_step, 1)
                    dve.wait_ge(v_step, base)
                    dve.scalar_tensor_tensor(out, ps[2 + half][:], nrstd[:, 1, col], out, ALU.mult, ALU.add
                                             ).then_inc(out_read, 1)
                    dve.wait_ge(out_read, b * 2 + (2 * o + half + 3))
                    dve.tensor_tensor(out, out, gate[:, cols], ALU.mult).then_inc(v_step, 1)
                    dve.wait_ge(v_step, base + 1)
                    ins = dve.tensor_tensor(x1[u][:, cols], x1[u][:, cols], out, ALU.add)
                    if half == 0:
                        ins.then_inc(v_step, 1)
                    else:
                        ins.then_inc(x1_done, 1)
                dve.sem_inc(v_step, 1)
                dve.wait_ge(std_done, b + (o + 1))
                dve.reciprocal(rstd[u][:], std[u][:]).then_inc(rstd_done, 1)

            def shift(b, o, u):
                dve.wait_ge(turned, b + (o + 3))
                dve.wait_ge(r_full, b + (o + 1))
                for k in range(KD):
                    ins = dve.tensor_scalar(h_T[u][:, k, :], ps[4 + k // 4][:, (k % 4) * P:(k % 4 + 1) * P],
                                            s.scale_col[:, 1, k:k + 1], s.shift_col[:, 1, k:k + 1], ALU.mult, ALU.add)
                ins.then_inc(h_done, 1)

            def logits(b, o, u):
                dve.wait_ge(r_full, b + (o + 3))
                col = bass.ds(b + o, 1) if not isinstance(b, int) else slice(b + o, b + o + 1)
                dve.tensor_tensor(s.logits[:, col, :].rearrange("p a n -> p (a n)"), ps[6][:, 0:NR], b_r[:], ALU.add
                                  ).then_inc(r_read, 1)

            dve.sem_inc(r_full, 2)
            pipeline(dve, combine, shift, logits)


def pipeline(eng, first, second, third):
    first(0, 0, 0)
    first(0, 1, 1)
    second(0, 0, 0)
    with eng.Fori(0, NT // 2 - 1) as i:
        b = i * 2
        for u in range(2):
            first(b, 2 + u, u)
            second(b, 1 + u, 1 - u)
            third(b, u, u)
    second(0, NT - 1, 1)
    third(0, NT - 2, 0)
    third(0, NT - 1, 1)


def load_expert(eng, a, s, e, u, loaded):
    for w, name in ((s.w1, "w1"), (s.w3, "w3"), (s.w2, "w2")):
        eng.dma_start(w[:, u, :, :], a[name][e, :, :].rearrange("a (k p) n -> p (a k) n", p=P)).then_inc(loaded, 16)


def route(nc, a, s):
    with ExitStack() as ctx:
        sb = lambda n, sh, dt=F32: ctx.enter_context(nc.sbuf_tensor("r_" + n, sh, dt))
        sem = lambda n: nc.alloc_semaphore("r_" + n)
        rank_ps = ctx.enter_context(nc.psum_tensor("r_rank", [P, NT, NE], F32))
        count_ps = ctx.enter_context(nc.psum_tensor("r_count", [P, 512], F32))
        gmax = sb("gmax", [P, NT])
        gd = sb("gd", [P, NT, NG])
        gsum = sb("gsum", [P, NT])
        w4 = sb("w4", [P, NT, NG])
        rev4 = sb("rev4", [P, NG])
        rev32 = sb("rev32", [P, NE])
        em = sb("em", [P, NT, NE])
        w32 = sb("w32", [P, NT, NE])
        pick = [sb(f"pick{i}", [P, NT, NE]) for i in range(2)]
        top = [sb(f"top{i}", [P, NT]) for i in range(2)]
        best = sb("best", [P, NT])
        ex = sb("ex", [P, NT])
        den = sb("den", [P, NT])
        both = sb("both", [P, NT, NE])
        before = sb("before", [P, NT + 1, NE])
        counts_i = sb("counts_i", [P, NE], I32)
        blocks = sb("blocks", [P, NE])
        ends = sb("ends", [P, NE])
        offs = sb("offs", [P, NE])
        slot = sb("slot", [P, NT, NE])
        iota_b = sb("iota_b", [P, BLOCKS])
        cmp = sb("cmp", [P, BLOCKS, NE])
        blk = sb("blk", [P, BLOCKS])
        third = sb("third", [P, BLOCKS], I32)
        third_f = sb("third_f", [P, BLOCKS])
        pairs_i = sb("pairs_i", [P, 1], I32)
        dest_f = sb("dest_f", [P, 2, NT])
        low = sb("low", [P, 2, NT], I32)
        high = sb("high", [P, 2, NT], I32)
        where = sb("where", [P, 2, NT], I32)
        row_id = sb("row_id", [P, NT], I32)
        zeros = sb("zeros", [P, BLOCKS], I32)

        made = sem("made")
        v_step = sem("v_step")
        gd_ready = sem("gd_ready")
        ge_ready = sem("ge_ready")
        diff_ready = sem("diff_ready")
        ex_ready = sem("ex_ready")
        both_ready = sem("both_ready")
        ranked = sem("ranked")
        where_ready = sem("where_ready")
        cleared = sem("cleared")
        scattered = sem("scattered")
        slots_loaded = sem("slots_loaded")
        w_loaded = sem("w_loaded")
        block = ctx.enter_context(nc.Block())

        @block.sync
        def _(sp):
            for e in range(W_BUFS):
                load_expert(sp, a, s, slice(e, e + 1), e, w_loaded)
            sp.wait_ge(w_loaded, 48 * W_BUFS)

        @block.gpsimd
        def _(pool):
            pool.memset(zeros[:], 0).then_inc(made, 1)
            pool.iota(rev4[:], [[-1, NG]], base=NG, channel_multiplier=0, allow_small_or_imprecise_dtypes=True
                      ).then_inc(made, 1)
            pool.iota(rev32[:], [[-1, NE]], base=NE, channel_multiplier=0, allow_small_or_imprecise_dtypes=True
                      ).then_inc(made, 1)
            pool.iota(iota_b[:], [[1, BLOCKS]], base=0, channel_multiplier=0, allow_small_or_imprecise_dtypes=True
                      ).then_inc(made, 1)
            pool.iota(row_id[:], [[P, NT]], base=0, channel_multiplier=1).then_inc(made, 1)
            pool.wait_ge(made, 5)
            pool.dma_start(a["slot_dram"].rearrange("(p b) o -> p (b o)", p=P), zeros[:]).then_inc(cleared, 16)
            pool.wait_ge(cleared, 16)
            pool.wait_ge(where_ready, 1)
            for t in range(NT):
                for k in range(2):
                    pool.indirect_dma_start(
                        out=a["slot_dram"], out_offset=bass.IndirectOffsetOnAxis(ap=where[:, k, t:t + 1].bitcast(U32), axis=0),
                        in_=row_id[:, t:t + 1], in_offset=None).then_inc(scattered, 16)
            pool.wait_ge(scattered, 16 * 2 * NT)
            pool.dma_start(s.slots[:], a["slot_dram"].rearrange("(p b) o -> p (b o)", p=P)).then_inc(slots_loaded, 16)
            pool.wait_ge(slots_loaded, 16)

        @block.tensor
        def _(pe):
            pe.wait_ge(both_ready, 1)
            pe.matmul(rank_ps[:], s.tri[:], both[:], start=True, stop=False)
            pe.matmul(rank_ps[:], s.ones[:], before[:, 0:NT, :], start=False, stop=True)
            mm = pe.matmul(count_ps[:, 0:NE], s.ones[:], before[:, NT, :], start=True, stop=True)
            mm.then_inc(ranked, 1)

        @block.scalar
        def _(act):
            act.wait_ge(gd_ready, 1)
            act.activation(gd[:], gd[:], ACT.Exp).then_inc(ge_ready, 1)
            act.wait_ge(diff_ready, 1)
            act.activation(ex[:], ex[:], ACT.Exp).then_inc(ex_ready, 1)

        @block.vector
        def _(dve):
            link = Chain(dve, v_step)
            dve.wait_ge(made, 5)
            lg = s.logits[:, :, 0:NG]
            le = s.logits[:, :, NG:NG + NE]
            wide = [P, NT, NE]
            link(dve.memset(before[:, 0, :], 0.0))
            link(dve.tensor_reduce(gmax[:], lg, AX.X, ALU.max))
            link(dve.tensor_tensor(w4[:], lg, bc(gmax[:], 2, [P, NT, NG]), ALU.is_equal))
            link(dve.tensor_tensor(w4[:], w4[:], bc(rev4[:], 1, [P, NT, NG]), ALU.mult))
            link(dve.tensor_reduce(best[:], w4[:], AX.X, ALU.max))
            dve.tensor_tensor(gd[:], lg, bc(gmax[:], 2, [P, NT, NG]), ALU.subtract).then_inc(gd_ready, 1)
            link(dve.tensor_tensor(w4[:], bc(rev4[:], 1, [P, NT, NG]), bc(best[:], 2, [P, NT, NG]), ALU.is_equal))
            link(dve.tensor_scalar(w4[:], w4[:], -1.0, -NEG, ALU.add, ALU.mult))
            g4 = lambda v: v.rearrange("p t (g e) -> p t g e", e=PER_G)
            link(dve.tensor_tensor(g4(em[:]), g4(le), bc(w4[:], 3, [P, NT, NG, PER_G]), ALU.add))
            for i in range(2):
                link(dve.tensor_reduce(top[i][:], em[:], AX.X, ALU.max))
                link(dve.tensor_tensor(w32[:], em[:], bc(top[i][:], 2, wide), ALU.is_equal))
                link(dve.tensor_tensor(w32[:], w32[:], bc(rev32[:], 1, wide), ALU.mult))
                link(dve.tensor_reduce(best[:], w32[:], AX.X, ALU.max))
                link(dve.tensor_tensor(pick[i][:], bc(rev32[:], 1, wide), bc(best[:], 2, wide), ALU.is_equal))
                if i == 0:
                    link(dve.scalar_tensor_tensor(em[:], pick[0][:], 2 * NEG, em[:], ALU.mult, ALU.add))
            dve.tensor_tensor(ex[:], top[1][:], top[0][:], ALU.subtract).then_inc(diff_ready, 1)
            link(dve.tensor_tensor(both[:], pick[0][:], pick[1][:], ALU.add))
            for t in range(NT):
                ins = dve.tensor_tensor(before[:, t + 1, :], before[:, t, :], both[:, t, :], ALU.add)
                if t < NT - 1:
                    link(ins)
                else:
                    ins.then_inc(both_ready, 1)
            dve.wait_ge(ge_ready, 1)
            link(dve.tensor_reduce(gsum[:], gd[:], AX.X, ALU.add))
            dve.wait_ge(ex_ready, 1)
            link(dve.tensor_scalar(den[:], ex[:], 1.0, None, ALU.add))
            link(dve.tensor_tensor(den[:], den[:], gsum[:], ALU.mult))
            link(dve.reciprocal(s.gates[:, 0, :], den[:]))
            link(dve.tensor_tensor(s.gates[:, 1, :], s.gates[:, 0, :], ex[:], ALU.mult))
            dve.wait_ge(ranked, 1)
            link(dve.tensor_scalar(counts_i[:], count_ps[:, 0:NE], float(P - 1), None, ALU.add))
            link(dve.tensor_scalar(counts_i[:], counts_i[:], P.bit_length() - 1, None, ALU.arith_shift_right))
            link(dve.tensor_copy(blocks[:], counts_i[:]))
            link(dve.tensor_tensor_scan(ends[:], s.ones[:, 0:NE], blocks[:], 0.0, ALU.mult, ALU.add))
            link(dve.tensor_tensor(offs[:], ends[:], blocks[:], ALU.subtract))
            link(dve.tensor_scalar(offs[:], offs[:], float(P), -1.0, ALU.mult, ALU.add))
            link(dve.tensor_tensor(slot[:], rank_ps[:], bc(offs[:], 1, wide), ALU.add))
            for i in range(2):
                link(dve.tensor_tensor(w32[:], slot[:], pick[i][:], ALU.mult))
                link(dve.tensor_reduce(dest_f[:, i, :], w32[:], AX.X, ALU.add))
            link(dve.tensor_copy(s.dest[:], dest_f[:]))
            link(dve.tensor_scalar(low[:], s.dest[:], P - 1, BLOCKS.bit_length() - 1, ALU.bitwise_and,
                                   ALU.logical_shift_left))
            link(dve.tensor_scalar(high[:], s.dest[:], P.bit_length() - 1, None, ALU.logical_shift_right))
            dve.tensor_tensor(where[:], low[:], high[:], ALU.bitwise_or).then_inc(where_ready, 1)
            link(dve.tensor_tensor(cmp[:], bc(ends[:], 1, [P, BLOCKS, NE]), bc(iota_b[:], 2, [P, BLOCKS, NE]), ALU.is_le))
            link(dve.tensor_reduce(blk[:], cmp[:], AX.X, ALU.add))
            link(dve.tensor_scalar(s.block_e[:], blk[:], float(NE - 1), None, ALU.min))
            link(dve.tensor_scalar(s.w_need[:], s.block_e[:], 48.0, 96.0, ALU.mult, ALU.add))
            link(dve.tensor_scalar(third[:], blk[:], float(NE - 1), 43.0, ALU.min, ALU.mult))
            link(dve.tensor_scalar(third[:], third[:], 7, None, ALU.logical_shift_right))
            link(dve.tensor_scalar(third_f[:], third[:], float(-W_BUFS), None, ALU.mult))
            link(dve.tensor_scalar(blk[:], blk[:], float(NE - 1), None, ALU.min))
            link(dve.tensor_tensor(s.w_sel[:], blk[:], third_f[:], ALU.add))
            link(dve.memset(s.free_at[:, 0:W_BUFS], 0))
            link(dve.tensor_copy(s.free_at[:, W_BUFS:NE], ends[:, 0:NE - W_BUFS]))
            link(dve.tensor_scalar(pairs_i[:], ends[:, NE - 1:NE], 1.0, None, ALU.add))
            link(dve.tensor_scalar(pairs_i[:], pairs_i[:], 1, None, ALU.logical_shift_right))
            link(dve.tensor_copy(s.pairs[:, 0:1], pairs_i[:]))
            link(dve.tensor_scalar(s.pairs[:, 1:2], pairs_i[:], -1.0, None, ALU.add))
            link(dve.tensor_scalar(s.pairs[:, 2:3], pairs_i[:], -32.0, float(16 * BLOCKS + 16), ALU.mult, ALU.add))


def experts(nc, a, s):
    with ExitStack() as ctx:
        sb = lambda n, sh, dt=F32: ctx.enter_context(nc.sbuf_tensor("e_" + n, sh, dt))
        sem = lambda n: nc.alloc_semaphore("e_" + n)
        ps = [ctx.enter_context(nc.psum_tensor(f"e_ps{i}", [P, 512], F32)) for i in range(8)]
        w1, w3, w2 = s.w1, s.w3, s.w2
        zeros = sb("zeros", [P, D])
        gate_row = sb("gate_row", [P, D])
        idx = [sb(f"idx{i}", [P, 1], I32) for i in range(2)]
        xg = [sb(f"xg{i}", [P, D]) for i in range(2)]
        x_T = [sb(f"x_T{i}", [P, KD, P]) for i in range(2)]
        up = [sb(f"up{i}", [P, DE]) for i in range(2)]
        up_T = [sb(f"up_T{i}", [P, KE, P]) for i in range(2)]
        yb = [sb(f"yb{i}", [P, D]) for i in range(2)]

        w_loaded = sem("w_loaded")
        idx_ready = sem("idx_ready")
        gathered = [sem("gathered0"), sem("gathered1")]
        x_turned = sem("x_turned")
        x_shifted = sem("x_shifted")
        h1_full = sem("h1_full")
        h3_full = sem("h3_full")
        silu_done = sem("silu_done")
        up_done = sem("up_done")
        up_turned = sem("up_turned")
        up_copied = sem("up_copied")
        y_full = sem("y_full")
        y_copied = sem("y_copied")
        gate_loaded = sem("gate_loaded")
        stored = [sem("stored0"), sem("stored1")]
        turn = sem("turn")
        w_turn = sem("w_turn")
        zeroed = sem("zeroed")
        cleared = sem("cleared")
        all_stored = sem("all_stored")
        block = ctx.enter_context(nc.Block())
        HALF = BLOCKS // 2

        def used_pairs(eng):
            return eng.value_load(s.pairs[0:1, 0:1], min_val=T // P, max_val=HALF)

        def last_pair(eng):
            return eng.value_load(s.pairs[0:1, 1:2], min_val=T // P - 1, max_val=HALF - 1)

        @block.sync
        def _(sp):
            def load(i, u):
                e = bass.ds(i * W_BUFS + u, 1) if not isinstance(i, int) else slice(i * W_BUFS + u, i * W_BUFS + u + 1)
                blocks_before = sp.value_load(s.free_at[0:1, e], min_val=0, max_val=BLOCKS)
                sp.wait_ge(w_loaded, i * (48 * W_BUFS) + (48 * u + 48))
                sp.sem_inc(w_turn, 1)
                sp.wait_ge(y_full, blocks_before + 2)
                sp.sem_inc(w_turn, 1)
                load_expert(sp, a, s, e, u, w_loaded)

            sp.dma_start(gate_row[:], rows(a["gates_dram"][:, D:2 * D])).then_inc(gate_loaded, 16)
            sp.sem_inc(w_loaded, 48 + 48 * W_BUFS)
            sp.sem_inc(y_full, 2)
            with sp.Fori(1, NE // W_BUFS) as i:
                for u in range(W_BUFS):
                    load(i, u)
            for u in range(NE % W_BUFS):
                load(NE // W_BUFS, u)
            sp.sem_inc(cleared, 16)
            sp.wait_ge(zeroed, 1)
            pairs = used_pairs(sp)
            unused = sp.value_load(s.pairs[0:1, 2:3], min_val=16, max_val=32 * HALF)
            with sp.Fori(0, HALF) as i, sp.If(i >= pairs):
                for u in range(2):
                    row = sp.snap(i * (2 * P) + u * P, min_val=0, max_val=SLOTS - P)
                    sp.dma_start(a["y_dram"][bass.ds(row, P), :], zeros[:]).then_inc(cleared, 16)
            sp.wait_ge(cleared, unused)
            sp.sem_inc(w_turn, 1)
            sp.wait_ge(w_loaded, 48 * NE + 48)

        @block.gpsimd
        def _(pool):
            pool.memset(zeros[:], 0.0).then_inc(zeroed, 1)
            pairs = used_pairs(pool)
            with pool.Fori(0, HALF) as i, pool.If(i < pairs):
                for u in range(2):
                    pool.wait_ge(x_turned, i * 2 + (u + 1))
                    pool.tensor_copy(idx[u][:], s.slots[:, bass.ds(i * 2 + u, 1)]).then_inc(idx_ready, 1)
                    pool.wait_ge(idx_ready, i * 2 + (u + 1))
                    pool.sem_inc(turn, 1)
                    pool.indirect_dma_start(out=xg[u][:], out_offset=None, in_=a["xn_dram"],
                                            in_offset=bass.IndirectOffsetOnAxis(ap=idx[u][:].bitcast(U32), axis=0)
                                            ).then_inc(gathered[u], 16)

        @block.tensor
        def _(pe):
            pe.sem_inc(x_turned, 2)

            def turn_rows(b, o, u):
                pe.wait_ge(gathered[u], b * 8 + (16 * ((o - u) // 2) + 16))
                pe.wait_ge(x_shifted, b + (o + 1))
                for k in range(KD):
                    mm = pe.transpose(ps[k // 4][:, (k % 4) * P:(k % 4 + 1) * P], xg[u][:, k * P:(k + 1) * P], s.ident[:])
                mm.then_inc(x_turned, 1)

            def at(b, o):
                return slice(b + o, b + o + 1) if isinstance(b, int) else bass.ds(b + o, 1)

            def buffer(w, sel, k, cols):
                return w[:, bass.ds(sel, 1), k, cols].rearrange("p a n -> p (a n)")

            def up_products(b, o, u):
                need = pe.value_load(s.w_need[0:1, at(b, o)], min_val=96, max_val=48 * NE + 48)
                sel = pe.value_load(s.w_sel[0:1, at(b, o)], min_val=0, max_val=W_BUFS - 1)
                pe.wait_ge(x_shifted, b + (o + 2))
                pe.wait_ge(w_loaded, need)
                pe.wait_ge(silu_done, b + (o + 1))
                for k in range(KD):
                    mm = pe.matmul(ps[2][:], x_T[u][:, k, :], buffer(w1, sel, k, slice(0, DE)), start=(k == 0), stop=(k == KD - 1))
                mm.then_inc(h1_full, 1)
                pe.wait_ge(up_done, b + (o + 1))
                for k in range(KD):
                    mm = pe.matmul(ps[3][:], x_T[u][:, k, :], buffer(w3, sel, k, slice(0, DE)), start=(k == 0), stop=(k == KD - 1))
                mm.then_inc(h3_full, 1)

            def turn_up(b, o, u):
                pe.wait_ge(up_done, b + (o + 2))
                pe.wait_ge(up_copied, b + (o + 1))
                for k in range(KE):
                    mm = pe.transpose(ps[4][:, k * P:(k + 1) * P], up[u][:, k * P:(k + 1) * P], s.ident[:])
                mm.then_inc(up_turned, 1)

            def down_product(b, o, u):
                sel = pe.value_load(s.w_sel[0:1, at(b, o)], min_val=0, max_val=W_BUFS - 1)
                pe.wait_ge(up_copied, b + (o + 2))
                pe.wait_ge(y_copied, b * 2 + (2 * o + 2))
                for half in range(2):
                    for k in range(KE):
                        mm = pe.matmul(ps[5 + half][:], up_T[u][:, k, :], buffer(w2, sel, k, slice(half * 512, (half + 1) * 512)),
                                       start=(k == 0), stop=(k == KE - 1))
                mm.then_inc(y_full, 1)

            turn_rows(0, 0, 0)
            up_products(0, 0, 0)
            turn_rows(0, 1, 1)
            turn_up(0, 0, 0)
            last = last_pair(pe)
            with pe.Fori(0, HALF - 1) as i, pe.If(i < last):
                b = i * 2
                for v in range(2):
                    u = (1 + v) % 2
                    up_products(b, 1 + v, u)
                    turn_rows(b, 2 + v, 1 - u)
                    down_product(b, v, 1 - u)
                    turn_up(b, 1 + v, u)
            b = last * 2
            up_products(b, 1, 1)
            down_product(b, 0, 0)
            turn_up(b, 1, 1)
            down_product(b, 1, 1)

        @block.scalar
        def _(act):
            act.sem_inc(silu_done, 1)
            act.sem_inc(up_copied, 1)
            act.sem_inc(stored[0], 16)
            act.sem_inc(stored[1], 16)

            def silu(b, o, u):
                act.wait_ge(h1_full, b + (o + 1))
                act.wait_ge(up_turned, b + (o + 1))
                act.activation(up[u][:], ps[2][:], ACT.Silu).then_inc(silu_done, 1)

            def copy_up(b, o, u):
                act.wait_ge(up_turned, b + (o + 3))
                act.wait_ge(y_full, b + (o + 1))
                act.activation(up_T[u][:].rearrange("p k t -> p (k t)"), ps[4][:], ACT.Copy).then_inc(up_copied, 1)

            def store_y(b, o, u):
                row = act.snap(b * P + o * P, min_val=0, max_val=SLOTS - P) if not isinstance(b, int) else o * P
                act.wait_ge(y_copied, b * 2 + (2 * o + 4))
                act.dma_start(a["y_dram"][bass.ds(row, P), :], yb[u][:]).then_inc(stored[u], 16)

            act.sem_inc(up_turned, 2)
            silu(0, 0, 0)
            copy_up(0, 0, 0)
            last = last_pair(act)
            with act.Fori(0, HALF - 1) as i, act.If(i < last):
                b = i * 2
                for v in range(2):
                    u = (1 + v) % 2
                    silu(b, 1 + v, u)
                    store_y(b, v, 1 - u)
                    copy_up(b, 1 + v, u)
            b = last * 2
            silu(b, 1, 1)
            store_y(b, 0, 0)
            copy_up(b, 1, 1)
            store_y(b, 1, 1)
            act.wait_ge(stored[0], last * 16 + 32)
            act.wait_ge(stored[1], last * 16 + 32)
            act.sem_inc(all_stored, 1)

        @block.vector
        def _(dve):
            dve.sem_inc(x_shifted, 1)
            dve.sem_inc(up_done, 1)
            dve.sem_inc(h3_full, 2)
            dve.sem_inc(y_copied, 2)
            dve.wait_ge(gate_loaded, 16)

            def shift(b, o, u):
                dve.wait_ge(x_turned, b + (o + 3))
                dve.wait_ge(h3_full, b + (o + 1))
                for k in range(KD):
                    ins = dve.tensor_scalar(x_T[u][:, k, :], ps[k // 4][:, (k % 4) * P:(k % 4 + 1) * P],
                                            s.scale_col[:, 1, k:k + 1], s.shift_col[:, 1, k:k + 1], ALU.mult, ALU.add)
                ins.then_inc(x_shifted, 1)

            def gate(b, o, u):
                dve.wait_ge(silu_done, b + (o + 2))
                dve.wait_ge(h3_full, b + (o + 3))
                dve.tensor_tensor(up[u][:], up[u][:], ps[3][:], ALU.mult).then_inc(up_done, 1)

            def copy_y(b, o, u):
                dve.wait_ge(y_full, b + (o + 3))
                dve.wait_ge(stored[u], b * 8 + (16 * ((o - u) // 2) + 16))
                for half in range(2):
                    cols = slice(half * 512, (half + 1) * 512)
                    dve.tensor_tensor(yb[u][:, cols], ps[5 + half][:], gate_row[:, cols], ALU.mult).then_inc(y_copied, 1)

            shift(0, 0, 0)
            shift(0, 1, 1)
            gate(0, 0, 0)
            last = last_pair(dve)
            with dve.Fori(0, HALF - 1) as i, dve.If(i < last):
                b = i * 2
                for v in range(2):
                    u = (1 + v) % 2
                    shift(b, 2 + v, 1 - u)
                    gate(b, 1 + v, u)
                    copy_y(b, v, 1 - u)
            b = last * 2
            gate(b, 1, 1)
            copy_y(b, 0, 0)
            copy_y(b, 1, 1)


def combine(nc, a, s):
    with ExitStack() as ctx:
        sb = lambda n, sh, dt=F32: ctx.enter_context(nc.sbuf_tensor("c_" + n, sh, dt))
        sem = lambda n: nc.alloc_semaphore("c_" + n)
        norm_g = sb("norm_g", [P, D])
        idx = [sb(f"idx{i}", [P, 2], I32) for i in range(2)]
        x1 = [sb(f"x1{i}", [P, D]) for i in range(2)]
        y0 = [sb(f"y0{i}", [P, D]) for i in range(2)]
        y1 = [sb(f"y1{i}", [P, D]) for i in range(2)]
        junk = sb("junk", [P, D])
        o = [sb(f"o{i}", [P, D]) for i in range(2)]
        mean_sq = [sb(f"mean_sq{i}", [P, 1]) for i in range(2)]
        std = [sb(f"std{i}", [P, 1]) for i in range(2)]
        rstd = [sb(f"rstd{i}", [P, 1]) for i in range(2)]

        rows_loaded = sem("rows_loaded")
        x_loaded = [sem("x_loaded0"), sem("x_loaded1")]
        idx_ready = sem("idx_ready")
        turn = sem("turn")
        gathered = [sem("gathered0"), sem("gathered1")]
        v_step = sem("v_step")
        y0_scaled = sem("y0_scaled")
        sum_done = sem("sum_done")
        sq_done = sem("sq_done")
        std_done = sem("std_done")
        out_done = sem("out_done")
        stored = [sem("stored0"), sem("stored1")]
        block = ctx.enter_context(nc.Block())

        @block.sync
        def _(sp):
            sp.dma_start(norm_g[:], rows(a["final_norm_g"])).then_inc(rows_loaded, 16)
            with sp.Fori(0, NT // 2) as i:
                for u in range(2):
                    row = sp.snap(i * (2 * P) + u * P, min_val=0, max_val=T - P)
                    sp.wait_ge(out_done, i * 2 + (u + 1))
                    sp.dma_start(x1[u][:], a["x1_dram"][bass.ds(row, P), :]).then_inc(x_loaded[u], 16)

        @block.gpsimd
        def _(pool):
            with pool.Fori(0, NT // 2) as i:
                for u in range(2):
                    pool.wait_ge(sum_done, i * 2 + (u + 1))
                    pool.tensor_copy(idx[u][:], s.dest[:, :, bass.ds(i * 2 + u, 1)].rearrange("p k a -> p (k a)")
                                     ).then_inc(idx_ready, 1)
                    pool.wait_ge(idx_ready, i * 2 + (u + 1))
                    pool.sem_inc(turn, 1)
                    for k, y in enumerate((y0, y1)):
                        pool.indirect_dma_start(out=y[u][:], out_offset=None, in_=a["y_dram"],
                                                in_offset=bass.IndirectOffsetOnAxis(ap=idx[u][:, k:k + 1].bitcast(U32), axis=0)
                                                ).then_inc(gathered[u], 16)

        @block.scalar
        def _(act):
            act.sem_inc(stored[0], 16)
            act.sem_inc(stored[1], 16)
            with act.Fori(0, NT // 2) as i:
                for u in range(2):
                    j = i * 2
                    act.wait_ge(gathered[u], i * 32 + 32)
                    act.activation(y0[u][:], y0[u][:], ACT.Copy, scale=s.gates[:, 0, bass.ds(j + u, 1)]
                                   ).then_inc(y0_scaled, 1)
                    act.wait_ge(sum_done, j + (u + 3))
                    act.wait_ge(sq_done, j + (u + 1))
                    act.activation(junk[:], x1[u][:], ACT.Square, scale=D ** -0.5, accum_out=mean_sq[u][:]
                                   ).then_inc(sq_done, 1)
                    act.wait_ge(sq_done, j + (u + 2))
                    act.activation(std[u][:], mean_sq[u][:], ACT.Sqrt, bias=s.eps[:]).then_inc(std_done, 1)
                    row = act.snap(i * (2 * P) + u * P, min_val=0, max_val=T - P)
                    act.wait_ge(out_done, j + (u + 3))
                    act.dma_start(a["out"][bass.ds(row, P), :], o[u][:]).then_inc(stored[u], 16)
            act.wait_ge(stored[0], 16 + 8 * NT)
            act.wait_ge(stored[1], 16 + 8 * NT)

        @block.vector
        def _(dve):
            dve.sem_inc(sum_done, 2)
            dve.sem_inc(out_done, 2)
            dve.sem_inc(sq_done, 1)
            dve.wait_ge(rows_loaded, 16)
            with dve.Fori(0, NT // 2) as i:
                link = Chain(dve, v_step)
                link.base = i * 4
                for u in range(2):
                    j = i * 2
                    dve.wait_ge(x_loaded[u], i * 16 + 16)
                    dve.wait_ge(y0_scaled, j + (u + 1))
                    t = bass.ds(j + u, 1)
                    link(dve.scalar_tensor_tensor(y0[u][:], y1[u][:], s.gates[:, 1, t], y0[u][:], ALU.mult, ALU.add))
                    dve.tensor_tensor(x1[u][:], x1[u][:], y0[u][:], ALU.add).then_inc(sum_done, 1)
                    dve.wait_ge(std_done, j + (u + 1))
                    link(dve.reciprocal(rstd[u][:], std[u][:]))
                    dve.wait_ge(stored[u], i * 16 + 16)
                    dve.wait_ge(sum_done, j + (u + 3))
                    dve.scalar_tensor_tensor(o[u][:], x1[u][:], rstd[u][:], norm_g[:], ALU.mult, ALU.mult
                                             ).then_inc(out_done, 1)


def program(nc, a):
    with ExitStack() as ctx:
        sb = lambda n, sh, dt=F32: ctx.enter_context(nc.sbuf_tensor("s_" + n, sh, dt))

        class s:
            ident = sb("ident", [P, P])
            tri = sb("tri", [P, P])
            ones = sb("ones", [P, P])
            eps = sb("eps", [P, 1])
            scale_col = sb("scale_col", [P, 2, KD])
            shift_col = sb("shift_col", [P, 2, KD])
            norm_sum = sb("norm_sum", [P, 2, NT])

        with ExitStack() as ctx2:
            sb2 = lambda n, sh, dt=F32: ctx2.enter_context(nc.sbuf_tensor("s_" + n, sh, dt))
            s.dt = sb2("dt", [P, NT * NH])
            s.dtdec = sb2("dtdec", [P, NT * NH])
            s.acc = sb2("acc", [P, NT * NH])
            with ExitStack() as ctx3:
                sb3 = lambda n, sh, dt=F32: ctx3.enter_context(nc.sbuf_tensor("s_" + n, sh, dt))
                s.h_hi = sb3("h_hi", [P, KD, T], F32R)
                s.h_lo = sb3("h_lo", [P, KD, T], F32R)
                with nc.cleanup_on_exit():
                    prepare(nc, a, s)
                with nc.cleanup_on_exit():
                    decays(nc, a, s)
                with nc.cleanup_on_exit():
                    project(nc, a, s)
            with nc.cleanup_on_exit():
                ssd(nc, a, s)
        with nc.cleanup_on_exit():
            attend(nc, a, s)
        s.logits = sb("logits", [P, NT, NG + NE])
        with nc.cleanup_on_exit():
            mix(nc, a, s)
        s.slots = sb("slots", [P, BLOCKS], I32)
        s.dest = sb("dest", [P, 2, NT], I32)
        s.gates = sb("gates", [P, 2, NT])
        s.block_e = sb("block_e", [P, BLOCKS], I32)
        s.w_need = sb("w_need", [P, BLOCKS], I32)
        s.w_sel = sb("w_sel", [P, BLOCKS], I32)
        s.free_at = sb("free_at", [P, NE], I32)
        s.pairs = sb("pairs", [P, 3], I32)
        s.w1 = sb("w1", [P, W_BUFS, KD, DE])
        s.w3 = sb("w3", [P, W_BUFS, KD, DE])
        s.w2 = sb("w2", [P, W_BUFS, KE, D])
        with nc.cleanup_on_exit():
            route(nc, a, s)
        with nc.cleanup_on_exit():
            experts(nc, a, s)
        with nc.cleanup_on_exit():
            combine(nc, a, s)


def layouts(inputs):
    g = {k: np.asarray(v) for k, v in inputs.items()}
    col = lambda v, n: np.ascontiguousarray(v.reshape(n, P).T)
    conv_w, conv_b = g["conv_w"][0], g["conv_b"][0]
    w_in = g["w_in"][0]
    params = []
    for i in range(GROUPS):
        feats = [COL_X - D_SSD + i * GD + f * P for f in range(GF)]
        feats += [D_SSD + i * NSTATE, D_SSD + GROUPS * NSTATE + i * NSTATE]
        cw = [conv_w[j, f:f + P] for f in feats for j in range(CONV)]
        cb = [conv_b[f:f + P] for f in feats]
        ds = np.repeat(g["d_skip"][0][i * GH:(i + 1) * GH], HD).reshape(GF, P)
        params.append(np.stack(cw + cb + list(ds), axis=1))
    return {
        "x": np.ascontiguousarray(g["x"].reshape(T, D)),
        "c": col(g["c"][0], KD),
        "w_ada": g["w_ada"][0],
        "b_ada": g["b_ada"].reshape(1, -1),
        "norm_mix_g": col(g["norm_mix_g"][0], KD),
        "norm_ffn_g": col(g["norm_ffn_g"][0], KD),
        "w_in": w_in,
        "w_dt": np.ascontiguousarray(w_in[:, COL_DT:COL_DT + NH].reshape(KD, P, NH).transpose(1, 0, 2)),
        "dt_bias": g["dt_bias"].reshape(1, -1),
        "a_log": g["a_log"].reshape(1, -1),
        "group_params": np.ascontiguousarray(np.stack(params)),
        "y_norm_g": col(np.concatenate([g["ssd_norm_g"][0], g["attn_norm_g"][0]]), KM),
        "rel_rev": np.ascontiguousarray(g["rel_bias"][0][:, ::-1]),
        "w_out": g["w_out"][0],
        "w_router": np.ascontiguousarray(np.concatenate([g["w_router_group"][0], g["w_router_expert"][0]], axis=1)
                                         .reshape(KD, P, NG + NE).transpose(1, 0, 2)),
        "b_router": np.concatenate([g["b_router_group"][0], g["b_router_expert"][0]]).reshape(1, -1),
        "w1": g["w1"][0],
        "w3": g["w3"][0],
        "w2": g["w2"][0],
        "final_norm_g": g["final_norm_g"].reshape(1, -1),
    }


SCRATCH = {
    "acc_dram": ([NH, T], F32),
    "gates_dram": ([1, 2 * D], F32),
    "ext_dram": ([P, 2 * PAIRS, EXT], F32),
    "yT_dram": ([KM, P, T], F32),
    "proj_dram": ([GROUPS, TILES, P, T], F32),
    "x1_dram": ([T, D], F32),
    "xn_dram": ([T, D], F32),
    "slot_dram": ([SLOTS, 1], I32),
    "y_dram": ([SLOTS, D], F32),
}


def kernel(**inputs):
    import concourse.bacc as bacc
    from concourse.bass_utils import run_bass_kernel_spmd

    nc = bacc.Bacc("TRN2", target_bir_lowering=False, num_devices=1)
    arrays, a = {}, {}
    for name, v in layouts(inputs).items():
        arrays[f"in_{name}"] = v
        a[name] = nc.dram_tensor(f"in_{name}", v.shape, mybir.dt.from_np(v.dtype), kind="ExternalInput").ap()
    for name, (shape, dt) in SCRATCH.items():
        a[name] = nc.dram_tensor(name, shape, dt).ap()
    a["out"] = nc.dram_tensor("out", (T, D), F32, kind="ExternalOutput").ap()
    program(nc, a)
    r = run_bass_kernel_spmd(nc, [arrays], core_ids=[0])
    return r.results[0]["out"].reshape(1, T, D)
```
